# Optimizing a Trainium2 kernel written in Bass

```python
import jax, jax.numpy as jnp
from jax import lax
import numpy as np

D_MODEL = 1024
BATCH = 1
SEQ = 1024
DEPTH = 1

GRID_W = 64
ML_HEADS = 4
ML_DH = 128
ML_WIDTH = ML_HEADS * ML_DH
ML_CHUNK = 64
CONV_W = 5
NA_HEADS = 8
NA_DH = 64
NA_WIDTH = NA_HEADS * NA_DH
NA_KH_MAX = 8
NA_KW = 16
D_MIX = ML_WIDTH + NA_WIDTH
N_GATES = 4 * ML_HEADS
D_IN = 3 * ML_WIDTH + N_GATES + 3 * NA_WIDTH
SPLITS = (ML_WIDTH, 2 * ML_WIDTH, 3 * ML_WIDTH, 3 * ML_WIDTH + N_GATES,
          3 * ML_WIDTH + N_GATES + NA_WIDTH, 3 * ML_WIDTH + N_GATES + 2 * NA_WIDTH)
D_FF = 2816
EPS = 1e-6

kernel_name = "hybrid_mlstm_natten_macaron_encoder"

def rmsnorm(x, g):
    xf = x.astype(jnp.float32)
    y = xf * lax.rsqrt(jnp.mean(xf * xf, axis=-1, keepdims=True) + EPS)
    return (y * g.astype(jnp.float32)).astype(x.dtype)

def swiglu(x, w_gate, w_up, w_down):
    return (jax.nn.silu(x @ w_gate) * (x @ w_up)) @ w_down

def dwconv_centred(u, w, b):
    C = u.shape[-1]
    y = lax.conv_general_dilated(
        u, w[:, None, :].astype(u.dtype), window_strides=(1,),
        padding=[(CONV_W // 2, CONV_W // 2)],
        dimension_numbers=("NWC", "WIO", "NWC"), feature_group_count=C)
    return y + b

def mlstm_chunkwise(q, k, v, log_i, log_f):
    B, H, T, d = q.shape
    L = ML_CHUNK
    NC = T // L
    q = q.astype(jnp.float32).reshape(B, H, NC, L, d)
    k = k.astype(jnp.float32).reshape(B, H, NC, L, d)
    v = v.astype(jnp.float32).reshape(B, H, NC, L, d)
    li = log_i.reshape(B, H, NC, L)
    lf = log_f.reshape(B, H, NC, L)
    b = jnp.cumsum(lf, axis=-1)
    g = b[..., -1]
    a = g[..., None] - b + li
    m_loc = jnp.max(a, axis=-1)
    w = jnp.exp(a - m_loc[..., None])
    C_loc = jnp.einsum('bhnl,bhnld,bhnle->bhnde', w, v, k)
    n_loc = jnp.einsum('bhnl,bhnle->bhne', w, k)

    def step(carry, xs):
        C, n, m = carry
        g_k, ml_k, Cl_k, nl_k = xs
        m_new = jnp.maximum(g_k + m, ml_k)
        s_old = jnp.exp(g_k + m - m_new)
        s_loc = jnp.exp(ml_k - m_new)
        C_new = s_old[..., None, None] * C + s_loc[..., None, None] * Cl_k
        n_new = s_old[..., None] * n + s_loc[..., None] * nl_k
        return (C_new, n_new, m_new), (C, n, m)

    init = (jnp.zeros((B, H, d, d), jnp.float32), jnp.zeros((B, H, d), jnp.float32),
            jnp.zeros((B, H), jnp.float32))
    xs = (jnp.moveaxis(g, 2, 0), jnp.moveaxis(m_loc, 2, 0),
          jnp.moveaxis(C_loc, 2, 0), jnp.moveaxis(n_loc, 2, 0))
    _, (C0, n0, m0) = lax.scan(step, init, xs)
    C0 = jnp.moveaxis(C0, 0, 2)
    n0 = jnp.moveaxis(n0, 0, 2)
    m0 = jnp.moveaxis(m0, 0, 2)

    D = b[..., :, None] - b[..., None, :] + li[..., None, :]
    mask = np.tril(np.ones((L, L), dtype=bool))
    D = jnp.where(mask, D, -jnp.inf)
    inter = b + m0[..., None]
    m_t = jnp.maximum(inter, jnp.max(D, axis=-1))
    s = jnp.einsum('bhnld,bhnsd->bhnls', q, k) * jnp.exp(D - m_t[..., None])
    sc_inter = jnp.exp(inter - m_t)
    num = jnp.einsum('bhnls,bhnsd->bhnld', s, v) + \
        sc_inter[..., None] * jnp.einsum('bhnde,bhnle->bhnld', C0, q)
    den = jnp.sum(s, axis=-1) + sc_inter * jnp.einsum('bhne,bhnle->bhnl', n0, q)
    den = jnp.maximum(jnp.abs(den), jnp.exp(-m_t))
    h = num / den[..., None]
    return h.reshape(B, H, T, d)

def mlstm_mixer(c, v, o, gates, conv_w, conv_b, w_q, w_k, gn):
    B, T, _ = c.shape
    u = jax.nn.silu(dwconv_centred(c, conv_w, conv_b)).reshape(B, T, ML_HEADS, ML_DH)
    q = jnp.einsum('bthd,hde->bhte', u, w_q)
    k = jnp.einsum('bthd,hde->bhte', u, w_k) * (ML_DH ** -0.5)
    vh = v.reshape(B, T, ML_HEADS, ML_DH).transpose(0, 2, 1, 3)
    gt = gates.astype(jnp.float32).reshape(B, T, 2, 2, ML_HEADS).transpose(2, 3, 0, 4, 1)
    log_i = gt[:, 0]
    log_f = jax.nn.log_sigmoid(gt[:, 1])
    flip = lambda a: jnp.flip(a, axis=2)
    h_fwd = mlstm_chunkwise(q, k, vh, log_i[0], log_f[0])
    h_bwd = flip(mlstm_chunkwise(flip(q), flip(k), flip(vh), flip(log_i[1]), flip(log_f[1])))
    hs = (h_fwd + h_bwd).transpose(0, 2, 1, 3)
    hn = rmsnorm(hs, gn).reshape(B, T, ML_WIDTH)
    return (jax.nn.sigmoid(o.astype(jnp.float32)) * hn).astype(c.dtype)

def na_mixer(q, k, v, gq, gk, rpb):
    B, T, _ = q.shape
    rows = T // GRID_W
    kh = min(NA_KH_MAX, rows)
    qh = rmsnorm(q.reshape(B, T, NA_HEADS, NA_DH), gq) * (NA_DH ** -0.5)
    khd = rmsnorm(k.reshape(B, T, NA_HEADS, NA_DH), gk)
    to_grid = lambda a: a.reshape(B, rows, GRID_W, NA_HEADS, NA_DH).transpose(0, 3, 1, 2, 4)
    qg, kg = to_grid(qh), to_grid(khd)
    vg = to_grid(v.reshape(B, T, NA_HEADS, NA_DH))
    col_start = np.clip(np.arange(GRID_W) - NA_KW // 2, 0, GRID_W - NA_KW)
    col_idx = col_start[:, None] + np.arange(NA_KW)[None, :]
    dc_idx = col_idx - np.arange(GRID_W)[:, None] + (NA_KW - 1)

    def row_block(r):
        rs = jnp.clip(r - kh // 2, 0, rows - kh)
        k_rows = lax.dynamic_slice_in_dim(kg, rs, kh, axis=2)
        v_rows = lax.dynamic_slice_in_dim(vg, rs, kh, axis=2)
        k_win = k_rows[:, :, :, col_idx, :]
        v_win = v_rows[:, :, :, col_idx, :]
        q_r = lax.dynamic_index_in_dim(qg, r, axis=2, keepdims=False)
        s = jnp.einsum('bhcd,bhrcwd->bhcrw', q_r, k_win).astype(jnp.float32)
        dr = rs + jnp.arange(kh) - r + (NA_KH_MAX - 1)
        bias = rpb[:, dr][:, :, dc_idx].transpose(0, 2, 1, 3)
        s = s + bias[None].astype(jnp.float32)
        p = jax.nn.softmax(s.reshape(B, NA_HEADS, GRID_W, kh * NA_KW), axis=-1)
        p = p.reshape(B, NA_HEADS, GRID_W, kh, NA_KW).astype(v_win.dtype)
        return jnp.einsum('bhcrw,bhrcwd->bhcd', p, v_win)

    out = lax.map(row_block, jnp.arange(rows))
    return out.transpose(1, 0, 3, 2, 4).reshape(B, T, NA_WIDTH).astype(q.dtype)

def setup_inputs(seed: int = 0) -> dict:
    key = jax.random.key(seed)
    ks = jax.random.split(key, 24)
    nrm = lambda k, shape, s: jax.random.normal(k, shape, jnp.float32) * s
    gain = lambda k, shape: 1.0 + 0.02 * jax.random.normal(k, shape, jnp.float32)
    ig = 0.1 * jax.random.normal(ks[7], (DEPTH, 2, 1, ML_HEADS), jnp.float32)
    fg = jnp.linspace(3.0, 6.0, ML_HEADS, dtype=jnp.float32) + \
        0.1 * jax.random.normal(ks[8], (DEPTH, 2, 1, ML_HEADS), jnp.float32)
    b_gates = jnp.concatenate([ig, fg], axis=2).reshape(DEPTH, N_GATES)
    return {
        "x": nrm(ks[0], (BATCH, SEQ, D_MODEL), 1.0),
        "norm_ffn1": gain(ks[1], (DEPTH, D_MODEL)),
        "w1_gate": nrm(ks[2], (DEPTH, D_MODEL, D_FF), D_MODEL ** -0.5),
        "w1_up": nrm(ks[3], (DEPTH, D_MODEL, D_FF), D_MODEL ** -0.5),
        "w1_down": nrm(ks[4], (DEPTH, D_FF, D_MODEL), D_FF ** -0.5),
        "norm_mix": gain(ks[5], (DEPTH, D_MODEL)),
        "w_in": nrm(ks[6], (DEPTH, D_MODEL, D_IN), D_MODEL ** -0.5),
        "b_gates": b_gates,
        "conv_w": nrm(ks[9], (DEPTH, CONV_W, ML_WIDTH), CONV_W ** -0.5),
        "conv_b": nrm(ks[10], (DEPTH, ML_WIDTH), 0.02),
        "w_q_ml": nrm(ks[11], (DEPTH, ML_HEADS, ML_DH, ML_DH), ML_DH ** -0.5),
        "w_k_ml": nrm(ks[12], (DEPTH, ML_HEADS, ML_DH, ML_DH), ML_DH ** -0.5),
        "gn_ml": gain(ks[13], (DEPTH, ML_HEADS, ML_DH)),
        "gq_na": gain(ks[14], (DEPTH, NA_DH)),
        "gk_na": gain(ks[15], (DEPTH, NA_DH)),
        "rpb": nrm(ks[16], (DEPTH, NA_HEADS, 2 * NA_KH_MAX - 1, 2 * NA_KW - 1), 0.1),
        "w_out": nrm(ks[17], (DEPTH, D_MIX, D_MODEL), D_MIX ** -0.5),
        "norm_ffn2": gain(ks[18], (DEPTH, D_MODEL)),
        "w2_gate": nrm(ks[19], (DEPTH, D_MODEL, D_FF), D_MODEL ** -0.5),
        "w2_up": nrm(ks[20], (DEPTH, D_MODEL, D_FF), D_MODEL ** -0.5),
        "w2_down": nrm(ks[21], (DEPTH, D_FF, D_MODEL), D_FF ** -0.5),
        "norm_final": gain(ks[22], (DEPTH, D_MODEL)),
    }

def reference(x, norm_ffn1, w1_gate, w1_up, w1_down, norm_mix, w_in, b_gates, conv_w,
              conv_b, w_q_ml, w_k_ml, gn_ml, gq_na, gk_na, rpb, w_out, norm_ffn2,
              w2_gate, w2_up, w2_down, norm_final):
    for l in range(DEPTH):
        x = x + 0.5 * swiglu(rmsnorm(x, norm_ffn1[l]), w1_gate[l], w1_up[l], w1_down[l])
        h = rmsnorm(x, norm_mix[l])
        proj = h @ w_in[l]
        c_ml, v_ml, o_ml, g_ml, q_na, k_na, v_na = jnp.split(proj, SPLITS, axis=-1)
        y_ml = mlstm_mixer(c_ml, v_ml, o_ml, g_ml + b_gates[l], conv_w[l], conv_b[l],
                           w_q_ml[l], w_k_ml[l], gn_ml[l])
        y_na = na_mixer(q_na, k_na, v_na, gq_na[l], gk_na[l], rpb[l])
        x = x + jnp.concatenate([y_ml, y_na], axis=-1) @ w_out[l]
        x = x + 0.5 * swiglu(rmsnorm(x, norm_ffn2[l]), w2_gate[l], w2_up[l], w2_down[l])
        x = rmsnorm(x, norm_final[l])
    return x


_drawn_inputs = setup_inputs


def setup_inputs(seed=0):
    import zlib

    import numpy as np

    out = dict(_drawn_inputs(seed))
    spreads = {}
    factors = {'norm_ffn1': 4.553,
     'norm_mix': 2.786,
     'gn_ml': 8.0,
     'gq_na': 8.0,
     'gk_na': 8.0,
     'rpb': 6.412,
     'norm_ffn2': 7.81,
     'norm_final': 2.823}
    for name, (base, spread) in spreads.items():
        noise = np.random.default_rng([zlib.crc32(name.encode()), seed]).standard_normal(out[name].shape)
        drawn = base * np.exp(spread * noise) if base else spread * noise
        out[name] = __import__('jax').numpy.asarray(drawn.astype(out[name].dtype))
    for name, factor in factors.items():
        out[name] = (out[name] * factor).astype(out[name].dtype)
    return out
```

```python
from contextlib import ExitStack

import concourse.bass as bass
from concourse import mybir

F32 = mybir.dt.float32
F32R = mybir.dt.float32r
ALU = mybir.AluOpType
ACT = mybir.ActivationFunctionType
AX = mybir.AxisListType

P = 128
KB = 1024
BANK = 512
EPS = 1e-6

T = 1024
D = 1024
DFF = 2816
TT = T // P
KD = D // P
HALVES = T // BANK
NF = DFF // P
NCH = NF // 2

GRID_W = 64
GRID_H = T // GRID_W
MLH, MLD = 4, 128
MLW = MLH * MLD
TAPS = 5
NAH, NAD = 8, 64
NAW = NAH * NAD
PAIRS = NAH // 2
WIN_H, WIN_W = 8, 16
NDR, NDC = 2 * WIN_H - 1, 2 * WIN_W - 1
NGATE = 4 * MLH
DIN = 3 * MLW + NGATE + 3 * NAW
NEG = -1.0e30


class Memory:

    def __init__(self, nc):
        self.nc = nc
        self.semaphores = []
        self.base = -(-nc.sbuf_base // 64) * 64

    def semaphore(self, name):
        self.semaphores.append(self.nc.alloc_semaphore(name))
        return self.semaphores[-1]

    def clear_semaphores(self):
        self.nc.all_engine_barrier()
        self.nc.clear_and_free_semaphores(self.semaphores)
        self.nc.all_engine_barrier()
        self.semaphores = []

    def at(self, name, kib, shape, dtype=F32):
        return self.nc.alloc_sbuf_tensor_at(name, shape, dtype, offset=self.base + int(kib * KB))


AT_SMALL = 0
AT_X = 7
AT_H = 39
AT_W = 103
AT_REST = 135


def make_identity(nc, mem):
    ident = mem.at("ident", AT_SMALL, [P, P])
    identity_zeroed = mem.semaphore("identity_zeroed")
    identity_made = mem.semaphore("identity_made")
    with nc.Block() as block:
        @block.gpsimd
        def _(pool):
            pool.memset(ident[:], 0.0).then_inc(identity_zeroed, 1)
            pool.wait_ge(identity_zeroed, 1)
            pool.affine_select(out=ident[:], in_=ident[:], compare_op=ALU.not_equal, fill=1.0, base=0,
                               pattern=[[-1, P]], channel_multiplier=1).then_inc(identity_made, 1)
            pool.wait_ge(identity_made, 1)
    return ident


class Norm:

    def __init__(self, nc, mem, tag, x, gain, ident, banks, at_scaled):
        sem = lambda s: mem.semaphore(f"{tag}_{s}")
        self.nc, self.x, self.gain, self.ident, self.banks = nc, x, gain, ident, banks
        self.h_hi = mem.at(f"{tag}_h_hi", AT_H, [P, KD, T], F32R)
        self.h_lo = mem.at(f"{tag}_h_lo", AT_H + 32, [P, KD, T], F32R)
        self.scaled = mem.at(f"{tag}_scaled", at_scaled, [P, TT, D])
        self.g = mem.at(f"{tag}_g", AT_SMALL + 0.5, [P, KD])
        self.sumsq = mem.at(f"{tag}_sumsq", AT_SMALL + 0.625, [P, TT])
        self.meansq = mem.at(f"{tag}_meansq", AT_SMALL + 0.6875, [P, TT])
        self.root = mem.at(f"{tag}_root", AT_SMALL + 0.75, [P, TT])
        self.rstd = mem.at(f"{tag}_rstd", AT_SMALL + 0.8125, [P, TT])
        self.gain_loaded = sem("gain_loaded")
        self.squared = sem("squared")
        self.mean_ready = sem("mean_ready")
        self.root_ready = sem("root_ready")
        self.rstd_ready = sem("rstd_ready")
        self.scaled_ready = sem("scaled_ready")
        self.transposed = sem("transposed")
        self.hi_ready = sem("hi_ready")
        self.lo_ready = sem("lo_ready")

    def load(self, sp):
        with self.nc.allow_non_contiguous_dma(reason="a gain per partition"):
            sp.dma_start(self.g[:], self.gain.rearrange("o (k p) -> p (o k)", p=P)).then_inc(self.gain_loaded, 16)

    def on_scalar(self, act, x_here):
        for t in range(TT):
            x_here(act, t)
            act.activation(self.scaled[:, t, :], self.x[:, t, :], ACT.Square,
                           accum_out=self.sumsq[:, t:t + 1]).then_inc(self.squared, 1)
        for half in range(HALVES):
            tiles = slice(4 * half, 4 * half + 4)
            act.wait_ge(self.mean_ready, half + 1)
            act.activation(self.root[:, tiles], self.meansq[:, tiles], ACT.Sqrt).then_inc(self.root_ready, 1)
        act.wait_ge(self.gain_loaded, 16)
        for n in range(HALVES * KD):
            half, kd = divmod(n, KD)
            act.wait_ge(self.transposed, n + 1)
            act.activation(self.h_hi[:, kd, half * BANK:(half + 1) * BANK], self.banks[4 + n % 4][:], ACT.Copy,
                           scale=self.g[:, kd:kd + 1]).then_inc(self.hi_ready, 1)

    def on_vector(self, dve):
        dve.wait_ge(self.gain_loaded, 16)
        for half in range(HALVES):
            tiles = slice(4 * half, 4 * half + 4)
            dve.wait_ge(self.squared, 4 * half + 4)
            dve.tensor_scalar(self.meansq[:, tiles], self.sumsq[:, tiles], 1.0 / D, EPS, ALU.mult,
                              ALU.add).then_inc(self.mean_ready, 1)
            dve.wait_ge(self.root_ready, half + 1)
            dve.reciprocal(self.rstd[:, tiles], self.root[:, tiles]).then_inc(self.rstd_ready, 1)
            dve.wait_ge(self.rstd_ready, half + 1)
            for t in range(4 * half, 4 * half + 4):
                dve.tensor_scalar(self.scaled[:, t, :], self.x[:, t, :], self.rstd[:, t:t + 1], None,
                                  ALU.mult).then_inc(self.scaled_ready, 1)
        for n in range(HALVES * KD):
            half, kd = divmod(n, KD)
            dve.wait_ge(self.hi_ready, n + 1)
            dve.scalar_tensor_tensor(out=self.h_lo[:, kd, half * BANK:(half + 1) * BANK],
                                     in0=self.banks[4 + n % 4][:], scalar=self.g[:, kd:kd + 1],
                                     in1=self.h_hi[:, kd, half * BANK:(half + 1) * BANK].bitcast(F32),
                                     op0=ALU.mult, op1=ALU.subtract).then_inc(self.lo_ready, 1)

    def on_tensor(self, pe):
        for n in range(HALVES * KD):
            half, kd = divmod(n, KD)
            if kd == 0:
                pe.wait_ge(self.scaled_ready, 4 * half + 4)
            if n >= 4:
                pe.wait_ge(self.lo_ready, n - 3)
            for j in range(4):
                last = pe.transpose(self.banks[4 + n % 4][:, j * P:(j + 1) * P],
                                    self.scaled[:, 4 * half + j, kd * P:(kd + 1) * P], self.ident[:])
            last.then_inc(self.transposed, 1)
        pe.wait_ge(self.lo_ready, HALVES * KD)


def split_product(pe, out, w_hi, w_lo, r_hi, r_lo, first, last):
    pe.matmul(out, w_hi, r_hi, start=first, stop=False)
    pe.matmul(out, w_hi, r_lo, start=False, stop=False)
    return pe.matmul(out, w_lo, r_hi, start=False, stop=last)


def feed_forward(nc, mem, tag, x, x_dram, x_scratch, gain, w_gate, w_up, w_down, ident, banks):
    sem = lambda s: mem.semaphore(f"{tag}_{s}")
    norm = Norm(nc, mem, tag, x, gain, ident, banks, AT_REST)

    w_hi = mem.at(f"{tag}_w_hi", AT_W, [P, 2, 2, KD, P], F32R)
    w_lo = mem.at(f"{tag}_w_lo", AT_W + 16, [P, 2, 2, KD, P], F32R)
    act_hi = mem.at(f"{tag}_act_hi", AT_REST, [P, 4, T], F32R)
    act_lo = mem.at(f"{tag}_act_lo", AT_REST + 16, [P, 4, T], F32R)
    raw_gate = mem.at(f"{tag}_raw_gate", AT_REST + 32, [P, KD, 2 * P])
    raw_up = mem.at(f"{tag}_raw_up", AT_REST + 40, [P, KD, 2 * P])
    raw_down = mem.at(f"{tag}_raw_down", AT_REST + 48, [P, 2, D])
    down_hi = mem.at(f"{tag}_down_hi", AT_REST + 56, [P, 2, D], F32R)
    down_lo = mem.at(f"{tag}_down_lo", AT_REST + 64, [P, 2, D], F32R)
    silu = mem.at(f"{tag}_silu", AT_SMALL + 1, [P, BANK])
    act = mem.at(f"{tag}_act", AT_SMALL + 3, [P, BANK])

    x_loaded = [sem(f"x_loaded{t}") for t in range(TT)]
    gate_loaded = sem("gate_loaded")
    up_loaded = sem("up_loaded")
    down_loaded = sem("down_loaded")
    gate_up_hi = sem("gate_up_hi")
    gate_up_split = sem("gate_up_split")
    down_hi_ready = sem("down_hi_ready")
    down_split = sem("down_split")
    gate_up_done = sem("gate_up_done")
    silu_ready = sem("silu_ready")
    act_ready = sem("act_ready")
    act_hi_ready = sem("act_hi_ready")
    act_split = sem("act_split")
    down_done = sem("down_done")
    added = sem("added")
    stored = sem("stored")

    gate_v = w_gate.rearrange("o (k p) f -> p (o k) f", p=P)
    up_v = w_up.rearrange("o (k p) f -> p (o k) f", p=P)
    down_v = w_down.rearrange("o (f p) d -> p (o f) d", p=P)
    OUT = TT * HALVES

    def chunks(eng, step):
        step(1, 1, True)
        with eng.Fori(0, (NCH - 3) // 2) as i:
            for parity in range(2):
                step(2 * i + (2 + parity), parity, False)
        step(NCH - 1, (NCH - 1) % 2, False)

    with nc.Block() as block:
        @block.sync
        def _(sp):
            if x_dram is not None:
                for t in range(TT):
                    sp.dma_start(x[:, t, :], x_dram[t * P:(t + 1) * P, :]).then_inc(x_loaded[t], 16)
            norm.load(sp)

            def load_gate_up(c):
                sp.dma_start(raw_gate[:], gate_v[:, :, bass.ds(c * (2 * P), 2 * P)]).then_inc(gate_loaded, 16)
                sp.dma_start(raw_up[:], up_v[:, :, bass.ds(c * (2 * P), 2 * P)]).then_inc(up_loaded, 16)

            def load_down(c):
                sp.dma_start(raw_down[:], down_v[:, bass.ds(c * 2, 2), :]).then_inc(down_loaded, 16)

            load_gate_up(0)
            load_down(0)

            def step(c, parity, first):
                sp.wait_ge(gate_up_split, 2 * c)
                load_gate_up(c)
                sp.wait_ge(down_split, c)
                load_down(c)
            chunks(sp, step)
            if x_scratch is not None:
                sp.wait_ge(added, OUT * NCH)
                for t in range(TT):
                    sp.dma_start(x_scratch[t * P:(t + 1) * P, :], x[:, t, :]).then_inc(stored, 16)
                sp.wait_ge(stored, 16 * TT)

        @block.scalar
        def _(a):
            norm.on_scalar(a, (lambda eng, t: eng.wait_ge(x_loaded[t], 16)) if x_dram is not None else (lambda eng, t: None))

            def split_gate_up(j, k, chunk_done):
                if chunk_done is not None:
                    a.wait_ge(gate_up_done, chunk_done)
                a.wait_ge(gate_loaded, 16 * (j // 2 + 1) if isinstance(j, int) else j * 8 + (16 - 8 * k))
                a.activation(w_hi[:, k, 0], raw_gate[:, :, k * P:(k + 1) * P], ACT.Copy).then_inc(gate_up_hi, 1)
                a.wait_ge(up_loaded, 16 * (j // 2 + 1) if isinstance(j, int) else j * 8 + (16 - 8 * k))
                a.activation(w_hi[:, k, 1], raw_up[:, :, k * P:(k + 1) * P], ACT.Copy).then_inc(gate_up_hi, 1)

            def activate(j, slot):
                for half in range(HALVES):
                    n = j * 2 + half
                    a.wait_ge(gate_up_done, n + 1)
                    if not (isinstance(n, int) and n < 1):
                        a.wait_ge(act_ready, n)
                    a.activation(silu[:], banks[half][:], ACT.Silu).then_inc(silu_ready, 1)
                    a.wait_ge(act_ready, n + 1)
                    a.activation(act_hi[:, slot, half * BANK:(half + 1) * BANK], act[:], ACT.Copy)\
                     .then_inc(act_hi_ready, 1)

            def split_down(c, first):
                if not first:
                    a.wait_ge(down_done, c * OUT)
                a.wait_ge(down_loaded, c * 16 + 16)
                a.activation(down_hi[:], raw_down[:], ACT.Copy).then_inc(down_hi_ready, 1)

            split_gate_up(0, 0, None)
            split_gate_up(1, 1, None)
            activate(0, 0)

            def step(c, parity, first):
                split_gate_up(c * 2, 0, c * 4 - 2)
                activate(c * 2 - 1, 2 * (1 - parity) + 1)
                split_down(c - 1, first)
                split_gate_up(c * 2 + 1, 1, c * 4)
                activate(c * 2, 2 * parity)
            chunks(a, step)
            activate(NF - 1, (NF - 1) % 4)
            split_down(NCH - 1, False)

        @block.vector
        def _(dve):
            norm.on_vector(dve)

            def split_gate_up(j, k):
                for m, raw in ((0, raw_gate), (1, raw_up)):
                    dve.wait_ge(gate_up_hi, j * 2 + (m + 1))
                    low = dve.tensor_tensor(w_lo[:, k, m], raw[:, :, k * P:(k + 1) * P], w_hi[:, k, m].bitcast(F32),
                                            ALU.subtract)
                low.then_inc(gate_up_split, 1)

            def activate(j, slot):
                for half in range(HALVES):
                    n = j * 2 + half
                    cols = slice(half * BANK, (half + 1) * BANK)
                    dve.wait_ge(silu_ready, n + 1)
                    if not (isinstance(n, int) and n < 1):
                        dve.wait_ge(act_split, n)
                    dve.tensor_tensor(act[:], silu[:], banks[2 + half][:], ALU.mult).then_inc(act_ready, 1)
                    dve.wait_ge(act_hi_ready, n + 1)
                    dve.tensor_tensor(act_lo[:, slot, cols], act[:], act_hi[:, slot, cols].bitcast(F32),
                                      ALU.subtract).then_inc(act_split, 1)

            def add(c):
                for k in range(OUT):
                    t, half = divmod(k, HALVES)
                    part = x[:, t, half * BANK:(half + 1) * BANK]
                    dve.wait_ge(down_done, c * OUT + (k + 1))
                    dve.scalar_tensor_tensor(out=part, in0=banks[4 + k % 4][:], scalar=0.5, in1=part,
                                             op0=ALU.mult, op1=ALU.add).then_inc(added, 1)

            def split_down(c):
                dve.wait_ge(down_hi_ready, c + 1)
                dve.tensor_tensor(down_lo[:], raw_down[:], down_hi[:].bitcast(F32), ALU.subtract)\
                   .then_inc(down_split, 1)

            split_gate_up(0, 0)
            split_gate_up(1, 1)
            activate(0, 0)

            def step(c, parity, first):
                split_gate_up(c * 2, 0)
                activate(c * 2 - 1, 2 * (1 - parity) + 1)
                if not first:
                    add(c - 2)
                split_down(c - 1)
                split_gate_up(c * 2 + 1, 1)
                activate(c * 2, 2 * parity)
            chunks(dve, step)
            activate(NF - 1, (NF - 1) % 4)
            add(NCH - 2)
            split_down(NCH - 1)
            add(NCH - 1)

        @block.tensor
        def _(pe):
            norm.on_tensor(pe)

            def gate_up(j, k, first):
                pe.wait_ge(gate_up_split, j + 1)
                for half in range(HALVES):
                    cols = slice(half * BANK, (half + 1) * BANK)
                    if not first:
                        pe.wait_ge(act_ready, j * 2 + (half - 1))
                    for m in range(2):
                        for kd in range(KD):
                            last = split_product(pe, banks[2 * m + half][:], w_hi[:, k, m, kd], w_lo[:, k, m, kd],
                                                 norm.h_hi[:, kd, cols], norm.h_lo[:, kd, cols],
                                                 kd == 0, kd == KD - 1)
                    last.then_inc(gate_up_done, 1)

            def down(c, parity, first):
                pe.wait_ge(act_split, c * 4 + 4)
                pe.wait_ge(down_split, c + 1)
                for k in range(OUT):
                    t, half = divmod(k, HALVES)
                    if not (first and k < 4):
                        pe.wait_ge(added, c * OUT + (k - 3))
                    for f in range(2):
                        rows = act_hi[:, 2 * parity + f, t * P:(t + 1) * P], act_lo[:, 2 * parity + f, t * P:(t + 1) * P]
                        cols = slice(half * BANK, (half + 1) * BANK)
                        last = split_product(pe, banks[4 + k % 4][:], *rows, down_hi[:, f, cols], down_lo[:, f, cols],
                                             f == 0, f == 1)
                    last.then_inc(down_done, 1)

            gate_up(0, 0, True)
            gate_up(1, 1, False)

            def step(c, parity, first):
                gate_up(c * 2, 0, False)
                gate_up(c * 2 + 1, 1, False)
                down(c - 1, 1 - parity, first)
            chunks(pe, step)
            down(NCH - 1, (NCH - 1) % 2, False)


class Projected:

    def __init__(self, nc, mem):
        self.c = mem.at("conv_in", AT_X, [P, MLH, T + TAPS - 1])
        self.gates = mem.at("gates", AT_X + 17, [NGATE, T])
        self.stage = mem.at("stage", AT_X + 21, [P, 4, BANK])
        self.q = mem.at("q_na", AT_REST, [P, TT, NAW])
        self.k = mem.at("k_na", AT_REST + 16, [P, TT, NAW])
        self.v = mem.at("v_ml", AT_REST + 32, [P, TT, MLH, MLD + 1])
        self.o_dram = nc.dram_tensor("o_scratch", [T, MLW], F32, kind="Internal").ap()
        self.v_dram = nc.dram_tensor("v_scratch", [T, NAW], F32, kind="Internal").ap()


def project(nc, mem, x, gain, w_in, b_gates, ident, banks):
    sem = lambda s: mem.semaphore(f"proj_{s}")
    norm = Norm(nc, mem, "mix", x, gain, ident, banks, AT_REST)
    out = Projected(nc, mem)
    w_hi = mem.at("proj_w_hi", AT_W, [P, KD, BANK], F32R)
    w_lo = mem.at("proj_w_lo", AT_W + 16, [P, KD, BANK], F32R)
    raw = mem.at("proj_raw", AT_REST + 56, [P, KD, BANK])
    bias = mem.at("gate_bias", AT_SMALL + 1, [NGATE, 1])

    gate_col = 3 * MLW
    token_slabs = [MLW, 2 * MLW] + [gate_col + NGATE + NAW * n for n in range(3)]
    slabs = [(0, BANK), (gate_col, P)] + [(c, BANK) for c in token_slabs]
    w_v = w_in.rearrange("o (k p) c -> p (o k) c", p=P)

    raw_loaded = [sem(f"raw_loaded{k}") for k in range(KD)]
    bias_loaded = sem("bias_loaded")
    hi_ready = sem("hi_ready")
    w_split = sem("w_split")
    piece_used = sem("piece_used")
    tile_done = sem("tile_done")
    even_read = sem("even_read")
    odd_read = sem("odd_read")
    padded = sem("padded")
    stage_stored = [sem(f"stage_stored{k}") for k in range(4)]
    MT = 8

    with nc.Block() as block:
        @block.sync
        def _(sp):
            norm.load(sp)
            with nc.allow_non_contiguous_dma(reason="a bias per partition"):
                sp.dma_start(bias[:], b_gates.rearrange("o g -> g o")).then_inc(bias_loaded, 16)
            for s, (col, width) in enumerate(slabs):
                for kd in range(KD):
                    if s:
                        sp.wait_ge(w_split, KD * (s - 1) + kd + 1)
                    sp.dma_start(raw[:, kd, 0:width], w_v[:, kd, col:col + width]).then_inc(raw_loaded[kd], 16)

        @block.gpsimd
        def _(pool):
            pool.wait_ge(norm.lo_ready, HALVES * KD)
            pool.memset(out.c[:, :, 0:2], 0.0).then_inc(padded, 1)
            pool.memset(out.c[:, :, T + 2:T + 4], 0.0).then_inc(padded, 1)
            pool.memset(out.v[:, :, :, MLD:MLD + 1], 1.0).then_inc(padded, 1)
            for n, (s, dram) in enumerate(((3, out.o_dram), (6, out.v_dram))):
                for t in range(TT):
                    read = 5 + 4 * (s - 2) + t // 2 + 1
                    pool.wait_ge(odd_read if t % 2 else even_read, read)
                    pool.dma_start(dram[t * P:(t + 1) * P, :], out.stage[:, t % 4, :])\
                        .then_inc(stage_stored[t % 4], 16)
            for k in range(4):
                pool.wait_ge(stage_stored[k], 16 * 4)
            pool.wait_ge(padded, 3)

        def destination(s, t):
            if s == 0:
                m, half = divmod(t, HALVES)
                return out.c[:, m, 2 + half * BANK:2 + (half + 1) * BANK]
            if s == 2:
                return out.v[:, t, :, 0:MLD]
            if s in (4, 5):
                return (out.q if s == 4 else out.k)[:, t, :]
            return out.stage[:, t % 4, :]

        def source(s, t):
            b = banks[t][:]
            return b.rearrange("p (h d) -> p h d", h=MLH) if s == 2 else b

        def wait_stage(eng, s, t):
            if s in (3, 6) and (s, t // 4) != (3, 0):
                eng.wait_ge(stage_stored[t % 4], 16 * (t // 4 if s == 3 else 2 + t // 4))

        first_tile = lambda s: 0 if s == 0 else 8 if s == 1 else 10 + MT * (s - 2)

        @block.scalar
        def _(a):
            norm.on_scalar(a, lambda eng, t: None)

            def split(s):
                for kd in range(KD):
                    width = slabs[s][1]
                    if s and kd < KD - 1:
                        a.wait_ge(piece_used, (KD - 1) * (s - 1) + kd + 1)
                    elif s:
                        a.wait_ge(tile_done, first_tile(s))
                    a.wait_ge(raw_loaded[kd], 16 * (s + 1))
                    a.activation(w_hi[:, kd, 0:width], raw[:, kd, 0:width], ACT.Copy).then_inc(hi_ready, 1)

            def read(s, t):
                a.wait_ge(tile_done, first_tile(s) + t + 1)
                wait_stage(a, s, t)
                a.activation(destination(s, t), source(s, t), ACT.Copy).then_inc(even_read, 1)

            split(0)
            for t in range(0, MT - 2, 2):
                read(0, t)
            split(1)
            read(0, MT - 2)
            split(2)
            a.wait_ge(tile_done, first_tile(1) + 1)
            a.wait_ge(bias_loaded, 16)
            a.activation(out.gates[:, 0:BANK], banks[0][0:NGATE, :], ACT.Identity, bias=bias[:]).then_inc(even_read, 1)
            for s in range(2, len(slabs)):
                for t in range(0, MT, 2):
                    if t == MT - 2 and s + 1 < len(slabs):
                        split(s + 1)
                    read(s, t)

        @block.vector
        def _(dve):
            norm.on_vector(dve)

            def split(s):
                for kd in range(KD):
                    width = slabs[s][1]
                    dve.wait_ge(hi_ready, KD * s + kd + 1)
                    dve.tensor_tensor(w_lo[:, kd, 0:width], raw[:, kd, 0:width], w_hi[:, kd, 0:width].bitcast(F32),
                                      ALU.subtract).then_inc(w_split, 1)

            def read(s, t):
                dve.wait_ge(tile_done, first_tile(s) + t + 1)
                wait_stage(dve, s, t)
                dve.tensor_copy(destination(s, t), source(s, t)).then_inc(odd_read, 1)

            split(0)
            for t in range(1, MT - 2, 2):
                read(0, t)
            split(1)
            read(0, MT - 1)
            split(2)
            dve.wait_ge(tile_done, first_tile(1) + 2)
            dve.wait_ge(bias_loaded, 16)
            dve.tensor_scalar(out.gates[:, BANK:T], banks[1][0:NGATE, :], bias[:], None, ALU.add).then_inc(odd_read, 1)
            for s in range(2, len(slabs)):
                for t in range(1, MT, 2):
                    if t == MT - 1 and s + 1 < len(slabs):
                        split(s + 1)
                    read(s, t)

        @block.tensor
        def _(pe):
            norm.on_tensor(pe)
            cols = [slice(half * BANK, (half + 1) * BANK) for half in range(HALVES)]
            for t in range(MT):
                m, half = divmod(t, HALVES)
                for kd in range(KD):
                    if t == 0:
                        pe.wait_ge(w_split, kd + 1)
                    last = split_product(pe, banks[t][:], w_hi[:, kd, m * P:(m + 1) * P], w_lo[:, kd, m * P:(m + 1) * P],
                                         norm.h_hi[:, kd, cols[half]], norm.h_lo[:, kd, cols[half]],
                                         kd == 0, kd == KD - 1)
                    if t == MT - 1 and kd < KD - 1:
                        last.then_inc(piece_used, 1)
                last.then_inc(tile_done, 1)
            for half in range(HALVES):
                pe.wait_ge(odd_read if half else even_read, 1)
                for kd in range(KD):
                    if half == 0:
                        pe.wait_ge(w_split, KD + kd + 1)
                    last = split_product(pe, banks[half][:], w_hi[:, kd, 0:P], w_lo[:, kd, 0:P],
                                         norm.h_hi[:, kd, cols[half]], norm.h_lo[:, kd, cols[half]],
                                         kd == 0, kd == KD - 1)
                    if half and kd < KD - 1:
                        last.then_inc(piece_used, 1)
                last.then_inc(tile_done, 1)
            pe.wait_ge(even_read, 5)
            pe.wait_ge(odd_read, 5)
            with pe.Fori(0, len(token_slabs)) as s:
                for t in range(TT):
                    pe.wait_ge(odd_read if t % 2 else even_read, s * 4 + (t // 2 + 2))
                    for kd in range(KD):
                        if t == 0:
                            pe.wait_ge(w_split, s * KD + (2 * KD + kd + 1))
                        rows = slice(t * P, (t + 1) * P)
                        last = split_product(pe, banks[t][:], norm.h_hi[:, kd, rows], norm.h_lo[:, kd, rows],
                                             w_hi[:, kd, :], w_lo[:, kd, :], kd == 0, kd == KD - 1)
                        if t == TT - 1 and kd < KD - 1:
                            last.then_inc(piece_used, 1)
                    last.then_inc(tile_done, 1)
    return out


def attend(nc, mem, pr, gq, gk, rpb, ident, banks):
    sem = lambda s: mem.semaphore(f"na_{s}")
    q_t = mem.at("na_qT", AT_H, [P, PAIRS, T])
    k_t = mem.at("na_kT", AT_H + 16, [P, PAIRS, T])
    v_even = mem.at("na_v_even", AT_H + 32, [P, TT, NAW])
    v_odd = mem.at("na_v_odd", AT_H + 48, [P, TT - 1, NAW])
    y_t = mem.at("na_yT", AT_REST + 32, [P, PAIRS, T])
    bias = mem.at("na_bias", AT_W + 16, [P, PAIRS, NDR, GRID_W])
    v_pair = mem.at("na_v_pair", AT_X, [P, 2 * TT - 1, P])
    negs = mem.at("na_negs", AT_X + 8, [P, 4, BANK])
    probs = mem.at("na_probs", AT_X + 16, [P, 4, BANK])
    probs_t = mem.at("na_probsT", AT_X + 24, [P, 4, BANK])
    q_diag = mem.at("na_q_diag", AT_W + 1, [P, 4, P])
    squares = mem.at("na_squares", AT_W + 4, [P, 2, NAW])
    bias_pair = mem.at("na_bias_pair", AT_W + 8, [P, NDR, GRID_W])
    pad = mem.at("na_pad", AT_W, [NAH * NDR, 2 * GRID_W - 1])
    gains = mem.at("na_gains", AT_SMALL + 1, [P, 2])
    gain_q = mem.at("na_gain_q", AT_SMALL + 1.0625, [P, 1])
    sumsq = mem.at("na_sumsq", AT_SMALL + 1.5, [P, 2, TT, NAH])
    meansq = mem.at("na_meansq", AT_SMALL + 2, [P, 2, TT, NAH])
    root = mem.at("na_root", AT_SMALL + 2.5, [P, 2, TT, NAH])
    rstd = mem.at("na_rstd", AT_SMALL + 3, [P, 2, TT, NAH])
    neg_max = mem.at("na_neg_max", AT_SMALL + 3.5, [P, 4])
    row_sum = mem.at("na_row_sum", AT_SMALL + 3.5625, [P, 4])
    inv_sum = mem.at("na_inv_sum", AT_SMALL + 3.625, [P, 4])
    pad_dram = nc.dram_tensor("rpb_scratch", [NAH * NDR, 2 * GRID_W - 1], F32, kind="Internal").ap()

    gains_loaded = sem("gains_loaded")
    v_loaded = sem("v_loaded")
    pad_zeroed = sem("pad_zeroed")
    pad_loaded = sem("pad_loaded")
    pad_stored = sem("pad_stored")
    bias_loaded = sem("bias_loaded")
    bias_masked = sem("bias_masked")
    gain_scaled = sem("gain_scaled")
    bias_ready = sem("bias_ready")
    squared = sem("squared")
    summed = sem("summed")
    mean_ready = sem("mean_ready")
    root_ready = sem("root_ready")
    rstd_ready = sem("rstd_ready")
    normed = sem("normed")
    transposed = sem("transposed")
    qk_ready = sem("qk_ready")
    diag_zeroed = sem("diag_zeroed")
    diag_ready = sem("diag_ready")
    v_pair_ready = sem("v_pair_ready")
    scores_ready = sem("scores_ready")
    negs_ready = sem("negs_ready")
    probs_ready = sem("probs_ready")
    inv_ready = sem("inv_ready")
    probs_scaled = sem("probs_scaled")
    probs_turned = sem("probs_turned")
    probs_t_ready = sem("probs_t_ready")
    out_ready = sem("out_ready")
    out_read = sem("out_read")

    row_start = [min(max(r - WIN_H // 2, 0), GRID_H - WIN_H) for r in range(GRID_H)]
    R = GRID_H
    GROUPS = R // 4

    def pairs(eng, pair):
        pair(0, True)
        with eng.Fori(1, PAIRS) as p:
            pair(p, False)

    with nc.Block() as block:
        @block.sync
        def _(sp):
            for h in range(2):
                with nc.allow_non_contiguous_dma(reason="a gain per partition"):
                    for n, g in enumerate((gq, gk)):
                        sp.dma_start(gains[h * NAD:(h + 1) * NAD, n:n + 1], g.rearrange("o d -> d o"))\
                          .then_inc(gains_loaded, 16)
            sp.wait_ge(pad_zeroed, 1)
            sp.dma_start(pad[:, GRID_W - WIN_W:GRID_W - WIN_W + NDC], rpb.rearrange("o h r c -> (o h r) c"))\
              .then_inc(pad_loaded, 16)
            sp.wait_ge(pad_loaded, 16)
            sp.dma_start(pad_dram, pad[:]).then_inc(pad_stored, 16)
            sp.wait_ge(pad_stored, 16)
            width = 2 * GRID_W - 1
            for pair in range(PAIRS):
                for h in range(2):
                    first = (2 * pair + h) * NDR * width
                    sp.dma_start(bias[h * GRID_W:(h + 1) * GRID_W, pair],
                                 bass.AP(tensor=pad_dram.tensor, offset=first,
                                         ap=[[1, GRID_W], [width, NDR], [1, GRID_W]])).then_inc(bias_loaded, 16)
            sp.dma_start(v_even[:], pr.v_dram.rearrange("(t p) c -> p t c", p=P)).then_inc(v_loaded, 16)
            sp.dma_start(v_odd[:], pr.v_dram[GRID_W:T - GRID_W, :].rearrange("(t p) c -> p t c", p=P))\
              .then_inc(v_loaded, 16)

        @block.gpsimd
        def _(pool):
            pool.memset(pad[:], 0.0).then_inc(pad_zeroed, 1)
            for slot in range(4):
                pool.memset(q_diag[:, slot], 0.0).then_inc(diag_zeroed, 1)
            pool.wait_ge(bias_loaded, 16 * NAH)
            for h in range(2):
                view = bias[h * GRID_W:(h + 1) * GRID_W].rearrange("c a r k -> c (a r) k")
                low, high = view[:, :, 0:GRID_W - WIN_W], view[:, :, WIN_W:GRID_W]
                n = GRID_W - WIN_W
                pool.affine_select(out=low, in_=low, compare_op=ALU.is_ge, fill=NEG,
                                   base=WIN_W // 2 - (GRID_W - 1), pattern=[[0, PAIRS * NDR], [1, n]],
                                   channel_multiplier=1).then_inc(bias_masked, 1)
                pool.wait_ge(bias_masked, 2 * h + 1)
                pool.affine_select(out=high, in_=high, compare_op=ALU.is_ge, fill=NEG,
                                   base=WIN_W // 2 - 1 - WIN_W + GRID_W - 1,
                                   pattern=[[0, PAIRS * NDR], [-1, n]], channel_multiplier=-1).then_inc(bias_masked, 1)
            pool.wait_ge(v_loaded, 32)
            pool.wait_ge(qk_ready, 2 * PAIRS * HALVES)
            pool.wait_ge(diag_zeroed, 4)

            def pair(p, first):
                for r in range(R):
                    if not (first and r < 4):
                        pool.wait_ge(scores_ready, p * R + (r - 3))
                    for h in range(2):
                        rows = slice(h * NAD, (h + 1) * NAD)
                        pool.tensor_copy(q_diag[rows, r % 4, h * GRID_W:(h + 1) * GRID_W],
                                         q_t[rows, p, r * GRID_W:(r + 1) * GRID_W]).then_inc(diag_ready, 1)
                    if r == 3:
                        if not first:
                            pool.wait_ge(out_ready, p * GROUPS)
                        pool.wait_ge(diag_ready, p * (2 * R) + 8)
                        pool.tensor_copy(v_pair[:, 0:TT], v_even[:, :, bass.ds(p * P, P)]).then_inc(v_pair_ready, 1)
                        pool.tensor_copy(v_pair[:, TT:], v_odd[:, :, bass.ds(p * P, P)]).then_inc(v_pair_ready, 1)
                        pool.wait_ge(v_pair_ready, p * 2 + 2)
            pairs(pool, pair)

        @block.scalar
        def _(a):
            for n in range(2 * TT):
                src = pr.q if n < TT else pr.k
                if n >= 2:
                    a.wait_ge(summed, n - 1)
                a.activation(squares[:, n % 2], src[:, n % TT], ACT.Square).then_inc(squared, 1)
            for w in range(2):
                a.wait_ge(mean_ready, w + 1)
                a.activation(root[:, w], meansq[:, w], ACT.Sqrt).then_inc(root_ready, 1)
            a.wait_ge(gains_loaded, 64)
            a.wait_ge(gain_scaled, 1)
            for m in range(2 * PAIRS * HALVES):
                w, pair, half = m // (PAIRS * HALVES), m // HALVES % PAIRS, m % HALVES
                a.wait_ge(transposed, m + 1)
                to, turned = (q_t, k_t)[w][:, pair, half * BANK:(half + 1) * BANK], banks[m % 4][:]
                if w == 0:
                    to = to.rearrange("d (r q) -> d r q", q=GRID_W)
                    turned = turned.rearrange("d (r q) -> d r q", q=GRID_W)[:, :, ::-1]
                a.activation(to, turned, ACT.Copy, scale=(gains[:, 1:2] if w else gain_q[:])).then_inc(qk_ready, 1)

            def exponentials(p, r, first):
                a.wait_ge(negs_ready, p * R + (r + 1))
                if not (first and r < 4):
                    a.wait_ge(probs_turned, p * R + (r - 3))
                a.activation(probs[:, r % 4], negs[:, r % 4], ACT.Exp, scale=-1.0, bias=neg_max[:, r % 4:r % 4 + 1],
                             accum_out=row_sum[:, r % 4:r % 4 + 1]).then_inc(probs_ready, 1)

            def read_turned(p, r):
                a.wait_ge(probs_turned, p * R + (r + 1))
                a.activation(probs_t[:, r % 4], banks[4 + r % 2][:], ACT.Copy).then_inc(probs_t_ready, 1)

            def pair(p, first):
                for i in range(R + 2):
                    if i < R:
                        exponentials(p, i, first)
                    if i >= 2:
                        read_turned(p, i - 2)
            pairs(a, pair)

        @block.vector
        def _(dve):
            dve.wait_ge(gains_loaded, 64)
            dve.tensor_scalar(gain_q[:], gains[:, 0:1], NAD ** -0.5, None, ALU.mult).then_inc(gain_scaled, 1)
            for n in range(2 * TT):
                w, t = divmod(n, TT)
                dve.wait_ge(squared, n + 1)
                dve.tensor_reduce(sumsq[:, w, t], squares[:, n % 2].rearrange("p (h d) -> p h d", d=NAD), AX.X,
                                  ALU.add).then_inc(summed, 1)
                if t == TT - 1:
                    dve.wait_ge(summed, n + 1)
                    dve.tensor_scalar(meansq[:, w], sumsq[:, w], 1.0 / NAD, EPS, ALU.mult, ALU.add).then_inc(mean_ready, 1)
            for w in range(2):
                dve.wait_ge(root_ready, w + 1)
                dve.reciprocal(rstd[:, w], root[:, w]).then_inc(rstd_ready, 1)
            for n in range(2 * TT):
                w, t = divmod(n, TT)
                dve.wait_ge(rstd_ready, w + 1)
                tile = (pr.k if w else pr.q)[:, t].rearrange("p (h d) -> p h d", d=NAD)
                dve.tensor_tensor(tile, tile, rstd[:, w, t].unsqueeze(2).to_broadcast([P, NAH, NAD]), ALU.mult)\
                   .then_inc(normed, 1)
            dve.wait_ge(bias_masked, 4)

            def bias_of_pair(p):
                dve.tensor_copy(bias_pair[:, WIN_H - 1:], bias[:, p, WIN_H - 1:]).then_inc(bias_ready, 1)
                dve.wait_ge(bias_ready, p * 2 + 1)
                dve.wait_ge(scores_ready, p * R + 1)
                dve.tensor_copy(bias_pair[:, 0:WIN_H - 1], bias[:, p, 0:WIN_H - 1]).then_inc(bias_ready, 1)

            def negate_and_max(p, r):
                dr = row_start[r] - r + WIN_H - 1
                dve.tensor_tensor_reduce(negs[:, r % 4], banks[r % 4][:],
                                         bias_pair[:, dr:dr + WIN_H].rearrange("c r k -> c (r k)"), -1.0, 3.0e38,
                                         ALU.add, ALU.min, neg_max[:, r % 4:r % 4 + 1]).then_inc(negs_ready, 1)

            def rows(p, i):
                if i == 0:
                    bias_of_pair(p)
                    negate_and_max(p, 0)
                    return
                r = i - 1
                if i == 1:
                    dve.wait_ge(bias_ready, p * 2 + 2)
                if i < R:
                    dve.wait_ge(scores_ready, p * R + (i + 1))
                dve.wait_ge(probs_ready, p * R + i)
                dve.reciprocal(inv_sum[:, r % 4:r % 4 + 1], row_sum[:, r % 4:r % 4 + 1]).then_inc(inv_ready, 1)
                if i < R:
                    negate_and_max(p, i)
                dve.wait_ge(inv_ready, p * R + i)
                dve.tensor_scalar(probs[:, r % 4], probs[:, r % 4], inv_sum[:, r % 4:r % 4 + 1], None, ALU.mult)\
                   .then_inc(probs_scaled, 1)

            def read_out(p, g):
                dve.wait_ge(out_ready, p * GROUPS + (g + 1))
                for h in range(2):
                    rows = slice(h * NAD, (h + 1) * NAD)
                    dve.tensor_copy(y_t[rows, p, g * 4 * GRID_W:(g + 1) * 4 * GRID_W].rearrange("d (r q) -> d r q", r=4),
                                    banks[6 + g % 2][rows, :].rearrange("d (r q) -> d r q", r=4)[
                                        :, :, h * GRID_W:(h + 1) * GRID_W][:, :, ::-1]).then_inc(out_read, 1)

            def pair(p, first):
                for i in range(R + 4):
                    if i <= R:
                        rows(p, i)
                    if i >= 7 and i % 4 == 3:
                        read_out(p, i // 4 - 1)
            pairs(dve, pair)

        @block.tensor
        def _(pe):
            for m in range(2 * PAIRS * HALVES):
                w, pair, half = m // (PAIRS * HALVES), m // HALVES % PAIRS, m % HALVES
                pe.wait_ge(normed, w * TT + 4 * half + 4)
                if m >= 4:
                    pe.wait_ge(qk_ready, m - 3)
                for j in range(4):
                    last = pe.transpose(banks[m % 4][:, j * P:(j + 1) * P],
                                        (pr.k if w else pr.q)[:, 4 * half + j, pair * P:(pair + 1) * P], ident[:])
                last.then_inc(transposed, 1)
            pe.wait_ge(qk_ready, 2 * PAIRS * HALVES)

            def scores(p, r, first):
                pe.wait_ge(diag_ready, p * (2 * R) + (2 * r + 2))
                if not (first and r < 4):
                    pe.wait_ge(negs_ready, p * R + (r - 3))
                start = row_start[r] * GRID_W
                pe.matmul(banks[r % 4][:], q_diag[:, r % 4], k_t[:, p, start:start + WIN_H * GRID_W], start=True,
                          stop=True).then_inc(scores_ready, 1)

            def turn(p, r, first):
                pe.wait_ge(probs_scaled, p * R + (r + 1))
                if not (first and r < 2):
                    pe.wait_ge(probs_t_ready, p * R + (r - 1))
                for j in range(4):
                    last = pe.transpose(banks[4 + r % 2][:, j * P:(j + 1) * P], probs[:, r % 4, j * P:(j + 1) * P],
                                        ident[:])
                last.then_inc(probs_turned, 1)

            def values(p, r, first):
                g = r // 4
                pe.wait_ge(probs_t_ready, p * R + (r + 1))
                if r == 0:
                    pe.wait_ge(v_pair_ready, p * 2 + 2)
                if r % 4 == 0 and not (first and g < 2):
                    pe.wait_ge(out_read, p * (2 * GROUPS) + 2 * (g - 1))
                tile = row_start[r] // 2 + (TT if row_start[r] % 2 else 0)
                for j in range(4):
                    last = pe.matmul(banks[6 + g % 2][:, (r % 4) * P:(r % 4 + 1) * P], v_pair[:, tile + j],
                                     probs_t[:, r % 4, j * P:(j + 1) * P], start=(j == 0), stop=(j == 3))
                if r % 4 == 3:
                    last.then_inc(out_ready, 1)

            def pair(p, first):
                for i in range(R + 3):
                    if i < R:
                        scores(p, i, first)
                    if 2 <= i < R + 2:
                        turn(p, i - 2, first)
                    if i >= 3:
                        values(p, i - 3, first)
            pairs(pe, pair)
    return y_t


def mlstm(nc, mem, pr, conv_w, conv_b, w_q, w_k, gn, ident, banks):
    sem = lambda s: mem.semaphore(f"ml_{s}")
    NC, DIRS = T // P, 2
    UD = MLH * NC
    U = DIRS * UD
    SCALE = MLD ** -0.5
    MAXLOW = -3.0e38
    FWD, BWD = slice(0, UD), slice(UD, U)

    u_t = mem.at("ml_uT", AT_H, [P, MLH, T])
    q_t = mem.at("ml_qT", AT_H + 16, [P, MLH, T])
    k_t = mem.at("ml_kT", AT_H + 32, [P, MLH, T])
    k_tok = mem.at("ml_k", AT_H + 48, [P, NC, MLH, MLD])
    m_all = [mem.at("ml_M_fwd", AT_X, [P, MLH, NC, P]),
             mem.at("ml_M_bwd", AT_H, [P, MLH, NC, P])]
    hs = mem.at("ml_h", AT_REST + 49, [P, NC, MLH, MLD])
    state = mem.at("ml_state", AT_REST + 65, [P, DIRS, MLH, MLD + 1])
    w_qk = mem.at("ml_w_qk", AT_W, [P, 2, MLH, MLD])
    conv = mem.at("ml_conv", AT_W + 4, [P, 2, T])
    taps = mem.at("ml_taps", AT_W + 12, [P, MLH, TAPS])
    conv_bias = mem.at("ml_conv_bias", AT_W + 12.25, [P, MLH])
    names = "li f neg_abs expf lnf lf b z runmax M m floor weights ones m0_rows decay_rows".split()
    row = {n: mem.at(f"ml_{n}", AT_W + 13 + 0.5 * i, [U, P]) for i, n in enumerate(names)}
    col = {n: mem.at(f"ml_{n}", AT_W + 22 + 0.0625 * i, [U, 1])
           for i, n in enumerate("g mloc m0 end neg_end decay".split())}
    line = mem.at("ml_line", AT_W + 23, [1, 4, U])
    one = mem.at("ml_one", AT_W + 24, [1, 1])
    unit_cols = mem.at("ml_unit_cols", AT_SMALL + 1, [P, 5, U])
    z_cols, w_cols, floor_cols, m0_cols, decay_cols = (unit_cols[:, i] for i in range(5))
    mask = mem.at("ml_mask", AT_SMALL + 2.5, [P, DIRS, P])
    ring = lambda n, kib: mem.at(f"ml_{n}", AT_W + kib, [P, DIRS, MLH, P])
    arg, weight, weighted = ring("arg", 0), ring("weight", 4), ring("weighted", 8)
    carry, q_scaled = ring("carry", 12), ring("q_scaled", 16)
    k_chunk, k_weighted = ring("k_chunk", 20), ring("k_weighted", 24)
    den = mem.at("ml_den", AT_SMALL + 4, [P, DIRS, MLH])
    den_max = mem.at("ml_den_max", AT_SMALL + 4.0625, [P, DIRS, MLH])
    den_inv = mem.at("ml_den_inv", AT_SMALL + 4.125, [P, DIRS, MLH])
    o = mem.at("ml_o", AT_X, [P, NC, MLH, MLD])
    squares = mem.at("ml_squares", AT_W, [P, NC, MLH, MLD])
    gn_all = mem.at("ml_gn_all", AT_W + 16, [P, MLH, MLD])
    sumsq = mem.at("ml_sumsq", AT_SMALL + 4.25, [P, NC, MLH])
    meansq = mem.at("ml_meansq", AT_SMALL + 4.375, [P, NC, MLH])
    root = mem.at("ml_root", AT_SMALL + 4.5, [P, NC, MLH])
    rstd = mem.at("ml_rstd", AT_SMALL + 4.625, [P, NC, MLH])
    gates_dram = nc.dram_tensor("gates_scratch", [NGATE * NC, P], F32, kind="Internal").ap()
    m_dram = nc.dram_tensor("m_scratch", [U, P], F32, kind="Internal").ap()

    gates_stored, units_loaded = sem("gates_stored"), sem("units_loaded")
    weights_loaded, taps_loaded = sem("weights_loaded"), sem("taps_loaded")
    chain = sem("chain")
    abs_ready, exp_ready, one_plus_ready, ln_ready = sem("abs"), sem("exp"), sem("one_plus"), sem("ln")
    ends_ready, ends_turned = sem("ends_ready"), sem("ends_turned")
    m0_line_ready, m0_turned = sem("m0_line_ready"), sem("m0_turned")
    m_ready, unit_vectors_ready = sem("m_ready"), sem("unit_vectors_ready")
    exps_ready, rows_ready, cols_turned, cols_ready = sem("exps"), sem("rows"), sem("cols_turned"), sem("cols_ready")
    ones_ready, masked, hs_zeroed = sem("ones_ready"), sem("masked"), sem("hs_zeroed")
    conv_ready, u_ready, qk_done, q_read, k_read = (sem(s) for s in "conv u qk_done q_read k_read".split())
    m_stored, m_loaded = sem("m_stored"), sem("m_loaded")

    with nc.Block() as block:
        @block.sync
        def _(sp):
            sp.dma_start(gates_dram.rearrange("(g c) l -> g (c l)", g=NGATE), pr.gates[:]).then_inc(gates_stored, 16)
            with nc.allow_non_contiguous_dma(reason="taps and biases per channel"):
                for h in range(MLH):
                    sp.dma_start(taps[:, h], conv_w[0, :, h * P:(h + 1) * P].rearrange("j p -> p j"))\
                      .then_inc(taps_loaded, 16)
                sp.dma_start(conv_bias[:], conv_b.rearrange("o (h p) -> p (o h)", p=P)).then_inc(taps_loaded, 16)
            sp.wait_ge(gates_stored, 16)
            for d in range(DIRS):
                for n, name in enumerate(("li", "f")):
                    first = (2 * d + n) * UD
                    sp.dma_start(row[name][d * UD:(d + 1) * UD, :], gates_dram[first:first + UD, :])\
                      .then_inc(units_loaded, 16)
            sp.dma_start(w_qk[:, 0], w_q.rearrange("o h d e -> d (o h) e")).then_inc(weights_loaded, 16)
            sp.dma_start(w_qk[:, 1], w_k.rearrange("o h d e -> d (o h) e")).then_inc(weights_loaded, 16)
            sp.wait_ge(m_ready, 1)
            sp.dma_start(m_dram, row["M"][:]).then_inc(m_stored, 16)
            sp.wait_ge(m_stored, 16)
            for d in range(DIRS):
                if d == 0:
                    sp.wait_ge(u_ready, MLH)
                else:
                    sp.wait_ge(qk_done, 4 * MLH + NC)
                sp.dma_start(m_all[d][:].rearrange("p h c l -> p (h c l)"),
                             m_dram[d * UD:(d + 1) * UD, :].rearrange("u l -> (u l)").partition_broadcast(P))\
                  .then_inc(m_loaded, 16)
            sp.wait_ge(m_loaded, 32)

        @block.gpsimd
        def _(pool):
            pool.memset(row["ones"][:], 1.0).then_inc(ones_ready, 1)
            pool.memset(one[:], 1.0).then_inc(ones_ready, 1)
            pool.memset(line[:], 0.0).then_inc(ones_ready, 1)
            pool.memset(mask[:], 0.0).then_inc(ones_ready, 1)
            pool.wait_ge(ones_ready, 4)
            pool.affine_select(out=mask[:, 0], in_=mask[:, 0], compare_op=ALU.is_ge, fill=-NEG, base=0,
                               pattern=[[1, P]], channel_multiplier=-1).then_inc(masked, 1)
            pool.affine_select(out=mask[:, 1], in_=mask[:, 1], compare_op=ALU.is_ge, fill=-NEG, base=0,
                               pattern=[[-1, P]], channel_multiplier=1).then_inc(masked, 1)
            pool.memset(hs[:], 0.0).then_inc(hs_zeroed, 1)
            pool.memset(state[:], 0.0).then_inc(hs_zeroed, 1)
            pool.wait_ge(masked, 2)
            pool.wait_ge(hs_zeroed, 2)

        @block.vector
        def _(dve):
            steps = [0]

            def step(instruction):
                steps[0] += 1
                instruction.then_inc(chain, 1)
                dve.wait_ge(chain, steps[0])

            dve.wait_ge(taps_loaded, 16 * (MLH + 1))
            for h in range(MLH):
                acc = conv[:, h % 2]
                if h >= 2:
                    dve.wait_ge(u_ready, h - 1)
                step(dve.tensor_scalar(acc, pr.c[:, h, 0:T], taps[:, h, 0:1], conv_bias[:, h:h + 1], ALU.mult, ALU.add))
                for j in range(1, TAPS):
                    tap = dve.scalar_tensor_tensor(out=acc, in0=pr.c[:, h, j:j + T], scalar=taps[:, h, j:j + 1],
                                                   in1=acc, op0=ALU.mult, op1=ALU.add)
                    if j < TAPS - 1:
                        step(tap)
                tap.then_inc(conv_ready, 1)
            dve.wait_ge(units_loaded, 64)
            dve.wait_ge(ones_ready, 3)
            dve.scalar_tensor_tensor(out=row["neg_abs"][:], in0=row["f"][:], scalar=-1.0, in1=row["f"][:],
                                     op0=ALU.mult, op1=ALU.min).then_inc(abs_ready, 1)
            dve.wait_ge(exp_ready, 1)
            dve.tensor_scalar(row["expf"][:], row["expf"][:], 1.0, None, ALU.add).then_inc(one_plus_ready, 1)
            dve.wait_ge(ln_ready, 1)
            step(dve.scalar_tensor_tensor(out=row["lf"][:], in0=row["f"][:], scalar=0.0, in1=row["lnf"][:],
                                          op0=ALU.min, op1=ALU.subtract))
            ones, lf, b, z, runmax = (row[n] for n in ("ones", "lf", "b", "z", "runmax"))
            step(dve.tensor_tensor_scan(b[FWD], ones[FWD], lf[FWD], 0.0, ALU.mult, ALU.add))
            step(dve.tensor_tensor_scan(b[BWD, ::-1], ones[BWD], lf[BWD, ::-1], 0.0, ALU.mult, ALU.add))
            step(dve.tensor_tensor(z[:], row["li"][:], b[:], ALU.subtract))
            step(dve.tensor_tensor_scan(runmax[FWD], ones[FWD], z[FWD], MAXLOW, ALU.mult, ALU.max))
            step(dve.tensor_tensor_scan(runmax[BWD, ::-1], ones[BWD], z[BWD, ::-1], MAXLOW, ALU.mult, ALU.max))
            for part, last in ((FWD, slice(P - 1, P)), (BWD, slice(0, 1))):
                step(dve.tensor_copy(col["g"][part], b[part, last]))
                dve.tensor_tensor(col["mloc"][part], b[part, last], runmax[part, last], ALU.add).then_inc(ends_ready, 1)
            dve.wait_ge(ends_turned, 1)
            step(dve.tensor_copy(line[:, 0:2], banks[4][0:1, 0:2 * U].rearrange("p (a u) -> p a u", a=2)))
            for d in range(DIRS):
                for h in range(MLH):
                    first = d * UD + h * NC
                    g, mloc, m = (line[:, i, first:first + NC] for i in range(3))
                    if d:
                        g, mloc, m = g[:, ::-1], mloc[:, ::-1], m[:, ::-1]
                    step(dve.tensor_tensor_scan(m, g, mloc, 0.0, ALU.add, ALU.max))
            by_head = lambda i, d: line[:, i, d * UD:(d + 1) * UD].rearrange("p (h c) -> p h c", h=MLH)
            step(dve.tensor_copy(by_head(3, 0)[:, :, 1:NC], by_head(2, 0)[:, :, 0:NC - 1]))
            dve.tensor_copy(by_head(3, 1)[:, :, 0:NC - 1], by_head(2, 1)[:, :, 1:NC]).then_inc(m0_line_ready, 1)
            dve.wait_ge(m0_turned, 1)
            step(dve.tensor_copy(col["m0"][:], banks[5][0:U, 0:1]))
            dve.tensor_scalar(row["M"][:], runmax[:], col["m0"][:], None, ALU.max).then_inc(m_ready, 1)
            dve.wait_ge(m_ready, 1)
            step(dve.tensor_tensor(row["m"][:], b[:], row["M"][:], ALU.add))
            for part, last in ((FWD, slice(P - 1, P)), (BWD, slice(0, 1))):
                dve.tensor_scalar(col["neg_end"][part], row["M"][part, last], -1.0, None, ALU.mult)\
                   .then_inc(unit_vectors_ready, 1)
            dve.tensor_scalar(row["m0_rows"][:], ones[:], col["m0"][:], None, ALU.mult).then_inc(rows_ready, 1)
            dve.wait_ge(exps_ready, 3)
            dve.tensor_scalar(row["decay_rows"][:], ones[:], col["decay"][:], None, ALU.mult).then_inc(rows_ready, 1)
            dve.wait_ge(cols_turned, 1)
            dve.tensor_copy(unit_cols[:].rearrange("p a u -> p (a u)"), banks[6][:, 0:5 * U]).then_inc(cols_ready, 1)
            dve.wait_ge(cols_ready, 1)
            for n in range(2 * MLH):
                dve.wait_ge(qk_done, 2 * n + 2)
                dve.tensor_scalar(k_t[:, n // 2, n % 2 * BANK:(n % 2 + 1) * BANK], banks[2 * (n % 2) + 1][:], SCALE,
                                  None, ALU.mult).then_inc(k_read, 1)

        @block.scalar
        def _(a):
            for h in range(MLH):
                a.wait_ge(conv_ready, h + 1)
                a.activation(u_t[:, h], conv[:, h % 2], ACT.Silu).then_inc(u_ready, 1)
            a.wait_ge(abs_ready, 1)
            a.activation(row["expf"][:], row["neg_abs"][:], ACT.Exp).then_inc(exp_ready, 1)
            a.wait_ge(one_plus_ready, 1)
            a.activation(row["lnf"][:], row["expf"][:], ACT.Ln).then_inc(ln_ready, 1)
            a.wait_ge(unit_vectors_ready, 2)
            a.activation(row["floor"][:], row["m"][:], ACT.Exp, scale=-1.0).then_inc(exps_ready, 1)
            a.activation(row["weights"][:], row["z"][:], ACT.Exp, bias=col["neg_end"][:]).then_inc(exps_ready, 1)
            a.activation(col["decay"][:], col["m0"][:], ACT.Exp, bias=col["neg_end"][:]).then_inc(exps_ready, 1)
            for n in range(2 * MLH):
                a.wait_ge(qk_done, 2 * n + 1)
                a.activation(q_t[:, n // 2, n % 2 * BANK:(n % 2 + 1) * BANK], banks[2 * (n % 2)][:], ACT.Copy)\
                 .then_inc(q_read, 1)
            for c in range(NC):
                a.wait_ge(qk_done, 4 * MLH + c + 1)
                a.activation(k_tok[:, c].rearrange("p h e -> p (h e)"), banks[2 * (c % 2)][:], ACT.Copy, scale=SCALE)\
                 .then_inc(q_read, 1)

        @block.tensor
        def _(pe):
            pe.wait_ge(ends_ready, 2)
            pe.matmul(banks[4][0:1, 0:U], col["g"][:], ident[0:U, 0:U], start=True, stop=True)
            pe.matmul(banks[4][0:1, U:2 * U], col["mloc"][:], ident[0:U, 0:U], start=True, stop=True)\
              .then_inc(ends_turned, 1)
            pe.wait_ge(m0_line_ready, 1)
            pe.matmul(banks[5][0:U, 0:1], line[:, 3, :], one[:], start=True, stop=True).then_inc(m0_turned, 1)
            pe.wait_ge(rows_ready, 2)
            for i, name in enumerate(("z", "weights", "floor")):
                pe.transpose(banks[6][:, i * U:(i + 1) * U], row[name][:], ident[0:U, 0:U])
            for i, name in ((3, "m0_rows"), (4, "decay_rows")):
                last = pe.matmul(banks[6][:, i * U:(i + 1) * U], row[name][:], ident[0:U, 0:U], start=True, stop=True)
            last.then_inc(cols_turned, 1)
            pe.wait_ge(weights_loaded, 32)
            for n in range(2 * MLH):
                h, half = divmod(n, 2)
                pe.wait_ge(u_ready, h + 1)
                if n >= 2:
                    pe.wait_ge(q_read, n - 1)
                    pe.wait_ge(k_read, n - 1)
                for w in range(2):
                    pe.matmul(banks[2 * half + w][:], w_qk[:, w, h], u_t[:, h, half * BANK:(half + 1) * BANK],
                              start=True, stop=True).then_inc(qk_done, 1)
            for c in range(NC):
                pe.wait_ge(q_read, 2 * MLH + c - 1)
                for h in range(MLH):
                    last = pe.matmul(banks[2 * (c % 2)][:, h * P:(h + 1) * P], u_t[:, h, c * P:(c + 1) * P], w_qk[:, 1, h],
                                     start=True, stop=True)
                last.then_inc(qk_done, 1)

    k_copied, k_scaled, q_carried = sem("k_copied"), sem("k_scaled"), sem("q_carried")
    arg_ready, weight_ready, carry_ready = sem("arg_ready"), sem("weight_ready"), sem("carry_ready")
    scores_done, weighted_ready, sums_done, update_done = (
        sem(s) for s in "scores_done weighted_ready sums_done update_done".split())
    updated, den_step, h_added = sem("updated"), sem("den_step"), sem("h_added")

    def chunks(eng, chunk_step):
        chunk_step(0, True)
        with eng.Fori(1, NC) as i:
            chunk_step(i, False)


    def chunks_of(eng, i):
        return [i, i * -1 + (NC - 1)]

    units_of = lambda cols, c, d: cols[:, d * UD:(d + 1) * UD].rearrange("p (h c) -> p h c", h=MLH)[:, :, c]
    head_bank = lambda d, h: banks[2 + 2 * d + h // 2][:, (h % 2) * (MLD + 1):(h % 2 + 1) * (MLD + 1)]
    update_bank = lambda h: banks[6 + h // 2][:, (h % 2) * (MLD + 1):(h % 2 + 1) * (MLD + 1)]

    with nc.Block() as block:
        @block.gpsimd
        def _(pool):
            def chunk_step(i, first):
                at = chunks_of(pool, i)
                for d in range(DIRS):
                    n, c = i * 2 + d, at[d]
                    if not first:
                        pool.wait_ge(scores_done, n - 1)
                    pool.tensor_copy(k_chunk[:, d], k_t[:, :, bass.ds(c * P, P)]).then_inc(k_copied, 1)
                    if not first:
                        pool.wait_ge(update_done, n - 1)
                    pool.tensor_tensor(k_weighted[:, d], k_tok[:, c],
                                       units_of(w_cols, c, d).unsqueeze(2).to_broadcast([P, MLH, P]), ALU.mult)\
                        .then_inc(k_scaled, 1)
                for d in range(DIRS):
                    n, c = i * 2 + d, at[d]
                    pool.wait_ge(carry_ready, n + 1)
                    if not first:
                        pool.wait_ge(sums_done, n - 1)
                    pool.tensor_tensor(q_scaled[:, d], q_t[:, :, bass.ds(c * P, P)], carry[:, d], ALU.mult)\
                        .then_inc(q_carried, 1)
            chunks(pool, chunk_step)

        @block.scalar
        def _(a):
            def chunk_step(i, first):
                at = chunks_of(a, i)
                for d in range(DIRS):
                    n, c = i * 2 + d, at[d]
                    a.wait_ge(arg_ready, n + 1)
                    if not first:
                        a.wait_ge(weighted_ready, n - 1)
                    for h in range(MLH):
                        unit = d * UD + h * NC + c
                        last = a.activation(weight[:, d, h], arg[:, d, h], ACT.Exp, scale=-1.0,
                                            bias=z_cols[:, bass.ds(unit, 1)])
                    last.then_inc(weight_ready, 1)
                    if not first:
                        a.wait_ge(q_carried, n - 1)
                    for h in range(MLH):
                        unit = d * UD + h * NC + c
                        last = a.activation(carry[:, d, h], m_all[d][:, h, c], ACT.Exp, scale=-1.0,
                                            bias=m0_cols[:, bass.ds(unit, 1)])
                    last.then_inc(carry_ready, 1)
            chunks(a, chunk_step)

        @block.vector
        def _(dve):
            def chunk_step(i, first):
                at = chunks_of(dve, i)
                for d in range(DIRS):
                    n, c = i * 2 + d, at[d]
                    if not first:
                        dve.wait_ge(weight_ready, n - 1)
                    dve.tensor_tensor(arg[:, d], m_all[d][:, :, c], mask[:, d].unsqueeze(1).to_broadcast([P, MLH, P]),
                                      ALU.add).then_inc(arg_ready, 1)
                for d in range(DIRS):
                    n = i * 2 + d
                    dve.wait_ge(weight_ready, n + 1)
                    if not first:
                        dve.wait_ge(sums_done, n - 1)
                    dve.wait_ge(scores_done, n + 1)
                    dve.tensor_tensor(weighted[:, d], weight[:, d], banks[d][:].rearrange("p (h l) -> p h l", h=MLH),
                                      ALU.mult).then_inc(weighted_ready, 1)
                for d in range(DIRS):
                    n, c = i * 2 + d, at[d]
                    dve.wait_ge(sums_done, n + 1)
                    dve.wait_ge(update_done, n + 1)
                    for h in range(MLH):
                        unit = d * UD + h * NC + c
                        last = dve.scalar_tensor_tensor(out=state[:, d, h], in0=state[:, d, h],
                                                        scalar=decay_cols[:, bass.ds(unit, 1)], in1=update_bank(h),
                                                        op0=ALU.mult, op1=ALU.add)
                    last.then_inc(updated, 1)
                    floors = units_of(floor_cols, c, d)
                    dens = [banks[2 + 2 * d + half][:, 0:2 * (MLD + 1)].rearrange("p (h e) -> p h e", h=2)[:, :, MLD]
                            for half in range(2)]
                    for half in range(2):
                        pair = slice(2 * half, 2 * half + 2)
                        last = dve.scalar_tensor_tensor(out=den[:, d, pair], in0=dens[half], scalar=-1.0,
                                                        in1=floors[:, pair], op0=ALU.mult, op1=ALU.max)
                    last.then_inc(den_step, 1)
                    dve.wait_ge(den_step, n * 3 + 1)
                    for half in range(2):
                        pair = slice(2 * half, 2 * half + 2)
                        last = dve.tensor_tensor(den_max[:, d, pair], dens[half], den[:, d, pair], ALU.max)
                    last.then_inc(den_step, 1)
                    dve.wait_ge(den_step, n * 3 + 2)
                    dve.reciprocal(den_inv[:, d], den_max[:, d]).then_inc(den_step, 1)
                    dve.wait_ge(den_step, n * 3 + 3)
                    for h in range(MLH):
                        last = dve.scalar_tensor_tensor(out=hs[:, c, h], in0=head_bank(d, h)[:, 0:MLD],
                                                        scalar=den_inv[:, d, h:h + 1], in1=hs[:, c, h],
                                                        op0=ALU.mult, op1=ALU.add)
                    last.then_inc(h_added, 1)
            chunks(dve, chunk_step)

        @block.tensor
        def _(pe):
            def chunk_step(i, first):
                at = chunks_of(pe, i)
                for d in range(DIRS):
                    n, c = i * 2 + d, at[d]
                    pe.wait_ge(k_copied, n + 1)
                    if not first:
                        pe.wait_ge(weighted_ready, n - 1)
                    for h in range(MLH):
                        last = pe.matmul(banks[d][:, h * P:(h + 1) * P], k_chunk[:, d, h], q_t[:, h, bass.ds(c * P, P)],
                                         start=True, stop=True)
                    last.then_inc(scores_done, 1)
                for d in range(DIRS):
                    n, c = i * 2 + d, at[d]
                    pe.wait_ge(weighted_ready, n + 1)
                    pe.wait_ge(q_carried, n + 1)
                    if not first:
                        pe.wait_ge(updated, n - 1)
                        pe.wait_ge(h_added, n - 1)
                    for h in range(MLH):
                        pe.matmul(head_bank(d, h), weighted[:, d, h], pr.v[:, c, h], start=True, stop=False)
                        last = pe.matmul(head_bank(d, h), q_scaled[:, d, h], state[:, d, h], start=False, stop=True)
                    last.then_inc(sums_done, 1)
                    pe.wait_ge(k_scaled, n + 1)
                    if not (first and d == 0):
                        pe.wait_ge(updated, n)
                    for h in range(MLH):
                        last = pe.matmul(update_bank(h), k_weighted[:, d, h], pr.v[:, c, h], start=True, stop=True)
                    last.then_inc(update_done, 1)
            chunks(pe, chunk_step)

    o_loaded, gn_loaded = sem("o_loaded"), sem("gn_loaded")
    squared, mean_ready, root_ready, y_step, sigmoid_ready = (
        sem(s) for s in "squared mean_ready root_ready y_step sigmoid_ready".split())

    with nc.Block() as block:
        @block.sync
        def _(sp):
            sp.dma_start(o[:].rearrange("p c h e -> p c (h e)"), pr.o_dram.rearrange("(c p) w -> p c w", p=P))\
              .then_inc(o_loaded, 16)
            sp.dma_start(gn_all[:].rearrange("p h e -> p (h e)"), gn.rearrange("o h e -> (o h e)").partition_broadcast(P))\
              .then_inc(gn_loaded, 16)

        @block.scalar
        def _(a):
            for c in range(NC):
                a.activation(squares[:, c], hs[:, c], ACT.Square).then_inc(squared, 1)
            a.wait_ge(mean_ready, 1)
            a.activation(root[:], meansq[:], ACT.Sqrt).then_inc(root_ready, 1)
            a.wait_ge(o_loaded, 16)
            for c in range(NC):
                a.activation(o[:, c], o[:, c], ACT.Sigmoid).then_inc(sigmoid_ready, 1)

        @block.vector
        def _(dve):
            for c in range(NC):
                dve.wait_ge(squared, c + 1)
                dve.tensor_reduce(sumsq[:, c], squares[:, c], AX.X, ALU.add).then_inc(y_step, 1)
            dve.wait_ge(y_step, NC)
            dve.tensor_scalar(meansq[:], sumsq[:], 1.0 / MLD, EPS, ALU.mult, ALU.add).then_inc(mean_ready, 1)
            dve.wait_ge(root_ready, 1)
            dve.reciprocal(rstd[:], root[:]).then_inc(y_step, 1)
            dve.wait_ge(y_step, NC + 1)
            dve.wait_ge(gn_loaded, 16)
            for c in range(NC):
                dve.tensor_tensor(hs[:, c], hs[:, c], rstd[:, c].unsqueeze(2).to_broadcast([P, MLH, MLD]), ALU.mult)\
                   .then_inc(y_step, 1)
                dve.wait_ge(y_step, NC + 2 + 3 * c)
                dve.tensor_tensor(hs[:, c], hs[:, c], gn_all[:], ALU.mult).then_inc(y_step, 1)
                dve.wait_ge(y_step, NC + 3 + 3 * c)
                dve.wait_ge(sigmoid_ready, c + 1)
                dve.tensor_tensor(hs[:, c], hs[:, c], o[:, c], ALU.mult).then_inc(y_step, 1)
            dve.wait_ge(y_step, NC + 1 + 3 * NC)
    return hs


def mix_out(nc, mem, x, x_scratch, y_ml, y_na, w_out, ident, banks):
    sem = lambda s: mem.semaphore(f"out_{s}")
    y_hi = mem.at("out_y_hi", AT_H, [P, KD, T], F32R)
    y_lo = mem.at("out_y_lo", AT_H + 32, [P, KD, T], F32R)
    w_hi = mem.at("out_w_hi", AT_W, [P, KD, BANK], F32R)
    w_lo = mem.at("out_w_lo", AT_W + 16, [P, KD, BANK], F32R)
    raw = mem.at("out_raw", AT_REST, [P, HALVES, KD, BANK])
    w_v = w_out.rearrange("o (k p) (s c) -> p (o k) s c", p=P, s=HALVES)

    x_loaded = [sem(f"x_loaded{t}") for t in range(TT)]
    raw_loaded = [sem(f"raw_loaded{s}") for s in range(HALVES)]
    hi_ready, w_split = sem("hi_ready"), sem("w_split")
    piece_used = sem("piece_used")
    transposed = sem("transposed")
    y_hi_ready, y_split = sem("y_hi_ready"), sem("y_split")
    tile_done, added = sem("tile_done"), sem("added")
    STEPS = [(half, kd) for half in range(HALVES) for kd in range(KD)]
    turned_before = lambda half, kd: half * MLH + min(kd, MLH)

    with nc.Block() as block:
        @block.sync
        def _(sp):
            for kd in range(KD):
                sp.dma_start(raw[:, 0, kd], w_v[:, kd, 0]).then_inc(raw_loaded[0], 16)
            for t in range(TT):
                sp.dma_start(x[:, t, :], x_scratch[t * P:(t + 1) * P, :]).then_inc(x_loaded[t], 16)
            for kd in range(KD):
                sp.dma_start(raw[:, 1, kd], w_v[:, kd, 1]).then_inc(raw_loaded[1], 16)

        def y_source(half, kd):
            if kd < MLH:
                return banks[4 + turned_before(half, kd) % 4][:]
            return y_na[:, kd - MLH, half * BANK:(half + 1) * BANK]

        @block.scalar
        def _(a):
            for half, kd in STEPS:
                if kd < MLH:
                    a.wait_ge(transposed, turned_before(half, kd) + 1)
                a.activation(y_hi[:, kd, half * BANK:(half + 1) * BANK], y_source(half, kd), ACT.Copy)\
                 .then_inc(y_hi_ready, 1)
            for s in range(HALVES):
                a.wait_ge(raw_loaded[s], 16 * KD)
                for kd in range(KD):
                    if s and kd < KD - 1:
                        a.wait_ge(piece_used, kd + 1)
                    elif s:
                        a.wait_ge(tile_done, TT)
                    a.activation(w_hi[:, kd], raw[:, s, kd], ACT.Copy).then_inc(hi_ready, 1)

        @block.vector
        def _(dve):
            for n, (half, kd) in enumerate(STEPS):
                dve.wait_ge(y_hi_ready, n + 1)
                cols = slice(half * BANK, (half + 1) * BANK)
                dve.tensor_tensor(y_lo[:, kd, cols], y_source(half, kd), y_hi[:, kd, cols].bitcast(F32),
                                  ALU.subtract).then_inc(y_split, 1)
            for s in range(HALVES):
                for kd in range(KD):
                    dve.wait_ge(hi_ready, KD * s + kd + 1)
                    dve.tensor_tensor(w_lo[:, kd], raw[:, s, kd], w_hi[:, kd].bitcast(F32), ALU.subtract)\
                       .then_inc(w_split, 1)
                for t in range(TT):
                    part = x[:, t, s * BANK:(s + 1) * BANK]
                    if s == 0:
                        dve.wait_ge(x_loaded[t], 16)
                    dve.wait_ge(tile_done, TT * s + t + 1)
                    dve.tensor_tensor(part, banks[t][:], part, ALU.add).then_inc(added, 1)
            dve.wait_ge(added, TT * HALVES)

        @block.tensor
        def _(pe):
            for half in range(HALVES):
                for h in range(MLH):
                    n = half * MLH + h
                    if n >= 4:
                        pe.wait_ge(y_split, n - 3)
                    for j in range(4):
                        last = pe.transpose(banks[4 + n % 4][:, j * P:(j + 1) * P], y_ml[:, 4 * half + j, h], ident[:])
                    last.then_inc(transposed, 1)
            for s in range(HALVES):
                for t in range(TT):
                    if s:
                        pe.wait_ge(added, t + 1)
                    elif t % 4 == 0:
                        pe.wait_ge(y_split, KD * (t // 4 + 1))
                    for kd in range(KD):
                        if t == 0:
                            pe.wait_ge(w_split, KD * s + kd + 1)
                        rows = slice(t * P, (t + 1) * P)
                        last = split_product(pe, banks[t][:], y_hi[:, kd, rows], y_lo[:, kd, rows],
                                             w_hi[:, kd], w_lo[:, kd], kd == 0, kd == KD - 1)
                        if s == 0 and t == TT - 1 and kd < KD - 1:
                            last.then_inc(piece_used, 1)
                    last.then_inc(tile_done, 1)


def final_norm(nc, mem, x, gain, out):
    sem = lambda s: mem.semaphore(f"final_{s}")
    g = mem.at("final_g", AT_H, [P, D])
    result = mem.at("final_result", AT_H + 8, [P, TT, D])
    sumsq, meansq, root, rstd = (mem.at(f"final_{n}", AT_SMALL + 1 + 0.0625 * i, [P, TT])
                                 for i, n in enumerate("sumsq meansq root rstd".split()))
    gain_loaded, squared, mean_ready, root_ready, rstd_ready, result_ready, stored = (
        sem(s) for s in "gain_loaded squared mean_ready root_ready rstd_ready result_ready stored".split())

    with nc.Block() as block:
        @block.sync
        def _(sp):
            sp.dma_start(g[:], gain.rearrange("o d -> (o d)").partition_broadcast(P)).then_inc(gain_loaded, 16)
            for t in range(TT):
                sp.wait_ge(result_ready, t + 1)
                sp.dma_start(out[t * P:(t + 1) * P, :], result[:, t]).then_inc(stored, 16)
            sp.wait_ge(stored, 16 * TT)

        @block.scalar
        def _(a):
            for t in range(TT):
                a.activation(result[:, t], x[:, t], ACT.Square, accum_out=sumsq[:, t:t + 1]).then_inc(squared, 1)
            for half in range(HALVES):
                tiles = slice(4 * half, 4 * half + 4)
                a.wait_ge(mean_ready, half + 1)
                a.activation(root[:, tiles], meansq[:, tiles], ACT.Sqrt).then_inc(root_ready, 1)

        @block.vector
        def _(dve):
            dve.wait_ge(gain_loaded, 16)
            for half in range(HALVES):
                tiles = slice(4 * half, 4 * half + 4)
                dve.wait_ge(squared, 4 * half + 4)
                dve.tensor_scalar(meansq[:, tiles], sumsq[:, tiles], 1.0 / D, EPS, ALU.mult, ALU.add)\
                   .then_inc(mean_ready, 1)
                dve.wait_ge(root_ready, half + 1)
                dve.reciprocal(rstd[:, tiles], root[:, tiles]).then_inc(rstd_ready, 1)
                dve.wait_ge(rstd_ready, half + 1)
                for t in range(4 * half, 4 * half + 4):
                    dve.scalar_tensor_tensor(out=result[:, t], in0=x[:, t], scalar=rstd[:, t:t + 1], in1=g[:],
                                             op0=ALU.mult, op1=ALU.mult).then_inc(result_ready, 1)


def hybrid_mlstm_natten_macaron_encoder_kernel(
        nc, x, norm_ffn1, w1_gate, w1_up, w1_down, norm_mix, w_in, b_gates, conv_w, conv_b, w_q_ml, w_k_ml, gn_ml,
        gq_na, gk_na, rpb, w_out, norm_ffn2, w2_gate, w2_up, w2_down, norm_final, out):
    mem = Memory(nc)
    banks = [nc.alloc_psum_tensor(f"bank{k}", [P, BANK], F32) for k in range(8)]
    x_scratch = nc.dram_tensor("x_scratch", [T, D], F32, kind="Internal").ap()
    resident = mem.at("x_resident", AT_X, [P, TT, D])
    ident = make_identity(nc, mem)
    feed_forward(nc, mem, "ffn1", resident, x.rearrange("o t d -> (o t) d"), x_scratch, norm_ffn1,
                 w1_gate, w1_up, w1_down, ident, banks)
    projected = project(nc, mem, resident, norm_mix, w_in, b_gates, ident, banks)
    y_ml = mlstm(nc, mem, projected, conv_w, conv_b, w_q_ml, w_k_ml, gn_ml, ident, banks)
    y_na = attend(nc, mem, projected, gq_na, gk_na, rpb, ident, banks)
    mem.clear_semaphores()
    mix_out(nc, mem, resident, x_scratch, y_ml, y_na, w_out, ident, banks)
    feed_forward(nc, mem, "ffn2", resident, None, None, norm_ffn2, w2_gate, w2_up, w2_down, ident, banks)
    final_norm(nc, mem, resident, norm_final, out.rearrange("o t d -> (o t) d"))


_INS = ["x", "norm_ffn1", "w1_gate", "w1_up", "w1_down", "norm_mix", "w_in", "b_gates", "conv_w", "conv_b", "w_q_ml",
        "w_k_ml", "gn_ml", "gq_na", "gk_na", "rpb", "w_out", "norm_ffn2", "w2_gate", "w2_up", "w2_down", "norm_final"]
_OUTS = [((1, T, D), "float32")]


def kernel(**inputs):
    import numpy as _np
    import concourse.bacc as _bacc
    from concourse import mybir as _mybir
    from concourse.bass_utils import run_bass_kernel_spmd as _run

    nc = _bacc.Bacc("TRN2", target_bir_lowering=False, num_devices=1)
    arrays, args = {}, []
    for name in _INS:
        a = _np.ascontiguousarray(inputs[name])
        arrays[f"in_{name}_dram"] = a
        args.append(nc.dram_tensor(f"in_{name}_dram", a.shape, _mybir.dt.from_np(a.dtype), kind="ExternalInput").ap())
    for i, (shape, dtype) in enumerate(_OUTS):
        dt = _mybir.dt.from_np(_np.dtype(dtype))
        args.append(nc.dram_tensor(f"out_{i}_dram", shape, dt, kind="ExternalOutput").ap())
    hybrid_mlstm_natten_macaron_encoder_kernel(nc, *args)
    r = _run(nc, [arrays], core_ids=[0])
    return r.results[0]["out_0_dram"]
```

```python
from contextlib import ExitStack

import concourse.bass as bass
from concourse import mybir

F32 = mybir.dt.float32
F32R = mybir.dt.float32r
ALU = mybir.AluOpType
ACT = mybir.ActivationFunctionType
AX = mybir.AxisListType

P = 128
KB = 1024
BANK = 512
EPS = 1e-6

T = 1024
D = 1024
DFF = 2816
TT = T // P
KD = D // P
HALVES = T // BANK
NF = DFF // P
NCH = NF // 2

GRID_W = 64
GRID_H = T // GRID_W
MLH, MLD = 4, 128
MLW = MLH * MLD
TAPS = 5
NAH, NAD = 8, 64
NAW = NAH * NAD
PAIRS = NAH // 2
WIN_H, WIN_W = 8, 16
NDR, NDC = 2 * WIN_H - 1, 2 * WIN_W - 1
NGATE = 4 * MLH
DIN = 3 * MLW + NGATE + 3 * NAW
NEG = -1.0e30


class Memory:

    def __init__(self, nc):
        self.nc = nc
        self.semaphores = []
        self.base = -(-nc.sbuf_base // 64) * 64

    def semaphore(self, name):
        self.semaphores.append(self.nc.alloc_semaphore(name))
        return self.semaphores[-1]

    def clear_semaphores(self):
        self.nc.all_engine_barrier()
        self.nc.clear_and_free_semaphores(self.semaphores)
        self.nc.all_engine_barrier()
        self.semaphores = []

    def at(self, name, kib, shape, dtype=F32):
        return self.nc.alloc_sbuf_tensor_at(name, shape, dtype, offset=self.base + int(kib * KB))


AT_SMALL = 0
AT_X = 7
AT_H = 39
AT_W = 103
AT_REST = 135


def make_identity(nc, mem):
    ident = mem.at("ident", AT_SMALL, [P, P])
    identity_zeroed = mem.semaphore("identity_zeroed")
    identity_made = mem.semaphore("identity_made")
    with nc.Block() as block:
        @block.gpsimd
        def _(pool):
            pool.memset(ident[:], 0.0).then_inc(identity_zeroed, 1)
            pool.wait_ge(identity_zeroed, 1)
            pool.affine_select(out=ident[:], in_=ident[:], compare_op=ALU.not_equal, fill=1.0, base=0,
                               pattern=[[-1, P]], channel_multiplier=1).then_inc(identity_made, 1)
            pool.wait_ge(identity_made, 1)
    return ident


class Norm:

    def __init__(self, nc, mem, tag, x, gain, ident, banks):
        sem = lambda s: mem.semaphore(f"{tag}_{s}")
        self.nc, self.x, self.gain, self.ident = nc, x, gain, ident
        self.banks = [banks[0:4], banks[4:8]]
        self.h_hi = mem.at(f"{tag}_h_hi", AT_H, [P, KD, T], F32R)
        self.h_lo = mem.at(f"{tag}_h_lo", AT_H + 32, [P, KD, T], F32R)
        scaled = [mem.at(f"{tag}_scaled{i}", AT_REST + kib, [P, 2, D]) for i, kib in enumerate((8, 24, 0, 16))]
        self.scaled = [scaled[t // 2][:, t % 2] for t in range(TT)]
        self.g = mem.at(f"{tag}_g", AT_SMALL + 0.5, [P, KD])
        self.sumsq = mem.at(f"{tag}_sumsq", AT_SMALL + 0.625, [P, TT])
        self.meansq = mem.at(f"{tag}_meansq", AT_SMALL + 0.6875, [P, TT])
        self.root = mem.at(f"{tag}_root", AT_SMALL + 0.75, [P, TT])
        self.rstd = mem.at(f"{tag}_rstd", AT_SMALL + 0.8125, [P, TT])
        self.gain_loaded = sem("gain_loaded")
        self.squared = sem("squared")
        self.mean_ready = sem("mean_ready")
        self.root_ready = sem("root_ready")
        self.rstd_ready = sem("rstd_ready")
        self.scaled_ready = sem("scaled_ready")
        self.transposed = sem("transposed")
        self.hi_ready = sem("hi_ready")
        self.lo_ready = sem("lo_ready")

    def load(self, sp):
        with self.nc.allow_non_contiguous_dma(reason="a gain per partition"):
            sp.dma_start(self.g[:], self.gain.rearrange("o (k p) -> p (o k)", p=P)).then_inc(self.gain_loaded, 16)

    def squares(self, act, half, x_here):
        for t in range(4 * half, 4 * half + 4):
            x_here(act, t)
            act.activation(self.scaled[t], self.x[:, t, :], ACT.Square,
                           accum_out=self.sumsq[:, t:t + 1]).then_inc(self.squared, 1)
        tiles = slice(4 * half, 4 * half + 4)
        act.wait_ge(self.mean_ready, half + 1)
        act.activation(self.root[:, tiles], self.meansq[:, tiles], ACT.Sqrt).then_inc(self.root_ready, 1)

    def hi_parts(self, act, half):
        act.wait_ge(self.gain_loaded, 16)
        for kd in range(KD):
            act.wait_ge(self.transposed, half * KD + kd + 1)
            act.activation(self.h_hi[:, kd, half * BANK:(half + 1) * BANK], self.banks[half][kd % 4][:], ACT.Copy,
                           scale=self.g[:, kd:kd + 1]).then_inc(self.hi_ready, 1)

    def mean(self, dve, half):
        tiles = slice(4 * half, 4 * half + 4)
        dve.wait_ge(self.squared, 4 * half + 4)
        dve.tensor_scalar(self.meansq[:, tiles], self.sumsq[:, tiles], 1.0 / D, EPS, ALU.mult,
                          ALU.add).then_inc(self.mean_ready, 1)
        dve.wait_ge(self.root_ready, half + 1)
        dve.reciprocal(self.rstd[:, tiles], self.root[:, tiles]).then_inc(self.rstd_ready, 1)
        dve.wait_ge(self.rstd_ready, half + 1)

    def scale(self, dve, t):
        dve.tensor_scalar(self.scaled[t], self.x[:, t, :], self.rstd[:, t:t + 1], None,
                          ALU.mult).then_inc(self.scaled_ready, 1)

    def lo_parts(self, dve, half):
        dve.wait_ge(self.gain_loaded, 16)
        for kd in range(KD):
            dve.wait_ge(self.hi_ready, half * KD + kd + 1)
            cols = slice(half * BANK, (half + 1) * BANK)
            dve.scalar_tensor_tensor(out=self.h_lo[:, kd, cols], in0=self.banks[half][kd % 4][:],
                                     scalar=self.g[:, kd:kd + 1], in1=self.h_hi[:, kd, cols].bitcast(F32),
                                     op0=ALU.mult, op1=ALU.subtract).then_inc(self.lo_ready, 1)

    def transposes(self, pe, half):
        pe.wait_ge(self.scaled_ready, 4 * half + 4)
        for kd in range(KD):
            if kd >= 4:
                pe.wait_ge(self.lo_ready, half * KD + kd - 3)
            for j in range(4):
                last = pe.transpose(self.banks[half][kd % 4][:, j * P:(j + 1) * P],
                                    self.scaled[4 * half + j][:, kd * P:(kd + 1) * P], self.ident[:])
            last.then_inc(self.transposed, 1)


    def scalar_tail(self, act, x_here):
        self.squares(act, 0, x_here)
        self.hi_parts(act, 0)

    def vector_after_tile(self, dve, t):
        if t == 4:
            self.mean(dve, 0)
        for tile in {4: (0,), 5: (1, 2), 6: (3,)}.get(t, ()):
            self.scale(dve, tile)

    def vector_tail(self, dve):
        self.lo_parts(dve, 0)

    def tensor_tail(self, pe):
        self.transposes(pe, 0)

    def sync_tail(self, sp):
        pass


def start(nc, x, x_dram, ffn):
    x_loaded = [ffn.mem.semaphore(f"x_loaded{t}") for t in range(TT)]
    norm = ffn.norm
    with nc.Block() as block:
        @block.sync
        def _(sp):
            for t in range(TT):
                if t == 4:
                    norm.load(sp)
                    ffn.prefetch(sp)
                sp.dma_start(x[:, t, :], x_dram[t * P:(t + 1) * P, :]).then_inc(x_loaded[t], 16)

        @block.scalar
        def _(act):
            norm.scalar_tail(act, lambda eng, t: eng.wait_ge(x_loaded[t], 16))

        @block.vector
        def _(dve):
            norm.mean(dve, 0)
            for t in range(4):
                norm.scale(dve, t)
            norm.vector_tail(dve)

        @block.tensor
        def _(pe):
            norm.tensor_tail(pe)
    return x_loaded


def split_product(pe, out, w_hi, w_lo, r_hi, r_lo, first, last):
    pe.matmul(out, w_hi, r_hi, start=first, stop=False)
    pe.matmul(out, w_hi, r_lo, start=False, stop=False)
    return pe.matmul(out, w_lo, r_hi, start=False, stop=last)


class FeedForward:

    def __init__(self, nc, mem, tag, x, gain, w_gate, w_up, w_down, ident, banks):
        self.nc, self.mem, self.tag, self.x, self.banks = nc, mem, tag, x, banks
        self.norm = Norm(nc, mem, tag, x, gain, ident, banks)
        self.raw_gate = mem.at(f"{tag}_raw_gate", AT_REST + 32, [P, KD, 2 * P])
        self.raw_up = mem.at(f"{tag}_raw_up", AT_REST + 40, [P, KD, 2 * P])
        self.raw_down = mem.at(f"{tag}_raw_down", AT_REST + 48, [P, 2, D])
        self.gate_v = w_gate.rearrange("o (k p) f -> p (o k) f", p=P)
        self.up_v = w_up.rearrange("o (k p) f -> p (o k) f", p=P)
        self.down_v = w_down.rearrange("o (f p) d -> p (o f) d", p=P)
        self.gate_loaded, self.up_loaded, self.down_loaded = (
            mem.semaphore(f"{tag}_{s}_loaded") for s in ("gate", "up", "down"))

    def load_gate_up(self, sp, c):
        cols = bass.ds(c * (2 * P), 2 * P)
        sp.dma_start(self.raw_gate[:], self.gate_v[:, :, cols]).then_inc(self.gate_loaded, 16)
        sp.dma_start(self.raw_up[:], self.up_v[:, :, cols]).then_inc(self.up_loaded, 16)

    def load_down(self, sp, c):
        sp.dma_start(self.raw_down[:], self.down_v[:, bass.ds(c * 2, 2), :]).then_inc(self.down_loaded, 16)

    def prefetch(self, sp):
        self.load_gate_up(sp, 0)
        self.load_down(sp, 0)

    def run(self, x_here, x_scratch, follower, prefetch):
        feed_forward(self, x_here, x_scratch, follower, prefetch)
        return self.stored


def feed_forward(ffn, x_here, x_scratch, follower, prefetch):
    nc, mem, tag, x, banks, norm = ffn.nc, ffn.mem, ffn.tag, ffn.x, ffn.banks, ffn.norm
    raw_gate, raw_up, raw_down = ffn.raw_gate, ffn.raw_up, ffn.raw_down
    gate_loaded, up_loaded, down_loaded = ffn.gate_loaded, ffn.up_loaded, ffn.down_loaded
    sem = lambda s: mem.semaphore(f"{tag}_{s}")

    w_hi = mem.at(f"{tag}_w_hi", AT_W, [P, 2, 2, KD, P], F32R)
    w_lo = mem.at(f"{tag}_w_lo", AT_W + 16, [P, 2, 2, KD, P], F32R)
    act_hi = mem.at(f"{tag}_act_hi", AT_REST, [P, 4, T], F32R)
    act_lo = mem.at(f"{tag}_act_lo", AT_REST + 16, [P, 4, T], F32R)
    down_hi = mem.at(f"{tag}_down_hi", AT_REST + 56, [P, 2, D], F32R)
    down_lo = mem.at(f"{tag}_down_lo", AT_REST + 64, [P, 2, D], F32R)
    last_down_hi = mem.at(f"{tag}_last_down_hi", AT_REST + 32, [P, 2, D], F32R)
    last_down_lo = mem.at(f"{tag}_last_down_lo", AT_REST + 40, [P, 2, D], F32R)
    silu = mem.at(f"{tag}_silu", AT_SMALL + 1, [P, BANK])
    act = mem.at(f"{tag}_act", AT_SMALL + 3, [P, BANK])

    gate_up_hi = sem("gate_up_hi")
    gate_up_split = sem("gate_up_split")
    down_hi_ready = sem("down_hi_ready")
    down_split = sem("down_split")
    gate_up_done = sem("gate_up_done")
    silu_ready = sem("silu_ready")
    act_ready = sem("act_ready")
    act_hi_ready = sem("act_hi_ready")
    act_split = sem("act_split")
    down_done = sem("down_done")
    added = sem("added")
    stored = ffn.stored = sem("stored")

    OUT = TT * HALVES

    def chunks(eng, step):
        step(1, 1, True)
        with eng.Fori(0, (NCH - 3) // 2) as i:
            for parity in range(2):
                step(2 * i + (2 + parity), parity, False)
        step(NCH - 1, (NCH - 1) % 2, False)

    LAST = OUT * (NCH - 1)
    x_added = lambda eng, t: eng.wait_ge(added, LAST + HALVES * (t + 1))

    with nc.Block() as block:
        @block.sync
        def _(sp):
            def step(c, parity, first):
                sp.wait_ge(gate_up_split, 2 * c)
                ffn.load_gate_up(sp, c)
                sp.wait_ge(down_split, c)
                ffn.load_down(sp, c)
            chunks(sp, step)
            sp.wait_ge(down_split, NCH)
            sp.wait_ge(down_done, LAST)
            follower.load(sp)
            prefetch(sp)
            if x_scratch is not None:
                for t in range(TT):
                    x_added(sp, t)
                    sp.dma_start(x_scratch[t * P:(t + 1) * P, :], x[:, t, :]).then_inc(stored, 16)
            follower.sync_tail(sp)

        @block.scalar
        def _(a):
            def split_gate_up(j, k, chunk_done):
                if chunk_done is not None:
                    a.wait_ge(gate_up_done, chunk_done)
                a.wait_ge(gate_loaded, 16 * (j // 2 + 1) if isinstance(j, int) else j * 8 + (16 - 8 * k))
                a.activation(w_hi[:, k, 0], raw_gate[:, :, k * P:(k + 1) * P], ACT.Copy).then_inc(gate_up_hi, 1)
                a.wait_ge(up_loaded, 16 * (j // 2 + 1) if isinstance(j, int) else j * 8 + (16 - 8 * k))
                a.activation(w_hi[:, k, 1], raw_up[:, :, k * P:(k + 1) * P], ACT.Copy).then_inc(gate_up_hi, 1)

            def activate(j, slot):
                for half in range(HALVES):
                    n = j * 2 + half
                    a.wait_ge(gate_up_done, n + 1)
                    if not (isinstance(n, int) and n < 1):
                        a.wait_ge(act_ready, n)
                    a.activation(silu[:], banks[half][:], ACT.Silu).then_inc(silu_ready, 1)
                    a.wait_ge(act_ready, n + 1)
                    a.activation(act_hi[:, slot, half * BANK:(half + 1) * BANK], act[:], ACT.Copy)\
                     .then_inc(act_hi_ready, 1)

            def split_down(c, first, hi):
                if not first:
                    a.wait_ge(down_done, c * OUT)
                a.wait_ge(down_loaded, c * 16 + 16)
                a.activation(hi[:], raw_down[:], ACT.Copy).then_inc(down_hi_ready, 1)

            split_gate_up(0, 0, None)
            norm.squares(a, 1, x_here)
            split_gate_up(1, 1, None)
            norm.hi_parts(a, 1)
            activate(0, 0)

            def step(c, parity, first):
                split_gate_up(c * 2, 0, c * 4 - 2)
                activate(c * 2 - 1, 2 * (1 - parity) + 1)
                split_down(c - 1, first, down_hi)
                split_gate_up(c * 2 + 1, 1, c * 4)
                activate(c * 2, 2 * parity)
            chunks(a, step)
            a.wait_ge(gate_up_split, NF)
            split_down(NCH - 1, True, last_down_hi)
            activate(NF - 1, (NF - 1) % 4)
            follower.scalar_tail(a, x_added)

        @block.vector
        def _(dve):
            def split_gate_up(j, k):
                for m, raw in ((0, raw_gate), (1, raw_up)):
                    dve.wait_ge(gate_up_hi, j * 2 + (m + 1))
                    low = dve.tensor_tensor(w_lo[:, k, m], raw[:, :, k * P:(k + 1) * P], w_hi[:, k, m].bitcast(F32),
                                            ALU.subtract)
                low.then_inc(gate_up_split, 1)

            def activate(j, slot):
                for half in range(HALVES):
                    n = j * 2 + half
                    cols = slice(half * BANK, (half + 1) * BANK)
                    dve.wait_ge(silu_ready, n + 1)
                    if not (isinstance(n, int) and n < 1):
                        dve.wait_ge(act_split, n)
                    dve.tensor_tensor(act[:], silu[:], banks[2 + half][:], ALU.mult).then_inc(act_ready, 1)
                    dve.wait_ge(act_hi_ready, n + 1)
                    dve.tensor_tensor(act_lo[:, slot, cols], act[:], act_hi[:, slot, cols].bitcast(F32),
                                      ALU.subtract).then_inc(act_split, 1)

            def add(c, follower=None):
                for k in range(OUT):
                    t, half = divmod(k, HALVES)
                    part = x[:, t, half * BANK:(half + 1) * BANK]
                    dve.wait_ge(down_done, c * OUT + (k + 1))
                    dve.scalar_tensor_tensor(out=part, in0=banks[4 + k % 4][:], scalar=0.5, in1=part,
                                             op0=ALU.mult, op1=ALU.add).then_inc(added, 1)
                    if follower and half and t >= 4:
                        follower.vector_after_tile(dve, t)

            def split_down(c, hi, lo):
                dve.wait_ge(down_hi_ready, c + 1)
                dve.tensor_tensor(lo[:], raw_down[:], hi[:].bitcast(F32), ALU.subtract).then_inc(down_split, 1)

            split_gate_up(0, 0)
            norm.mean(dve, 1)
            for t in range(4, TT):
                norm.scale(dve, t)
            split_gate_up(1, 1)
            norm.lo_parts(dve, 1)
            activate(0, 0)

            def step(c, parity, first):
                split_gate_up(c * 2, 0)
                activate(c * 2 - 1, 2 * (1 - parity) + 1)
                if not first:
                    add(c - 2)
                split_down(c - 1, down_hi, down_lo)
                split_gate_up(c * 2 + 1, 1)
                activate(c * 2, 2 * parity)
            chunks(dve, step)
            split_down(NCH - 1, last_down_hi, last_down_lo)
            activate(NF - 1, (NF - 1) % 4)
            add(NCH - 2)
            add(NCH - 1, follower)
            follower.vector_tail(dve)

        @block.tensor
        def _(pe):
            def gate_up(j, k, first):
                pe.wait_ge(gate_up_split, j + 1)
                for half in range(HALVES):
                    cols = slice(half * BANK, (half + 1) * BANK)
                    if first and half:
                        norm.transposes(pe, 1)
                        pe.wait_ge(norm.lo_ready, HALVES * KD)
                    if not first:
                        pe.wait_ge(act_ready, j * 2 + (half - 1))
                    for m in range(2):
                        for kd in range(KD):
                            last = split_product(pe, banks[2 * m + half][:], w_hi[:, k, m, kd], w_lo[:, k, m, kd],
                                                 norm.h_hi[:, kd, cols], norm.h_lo[:, kd, cols],
                                                 kd == 0, kd == KD - 1)
                    last.then_inc(gate_up_done, 1)

            def down(c, parity, first, hi, lo):
                pe.wait_ge(act_split, c * 4 + 4)
                pe.wait_ge(down_split, c + 1)
                for k in range(OUT):
                    t, half = divmod(k, HALVES)
                    if not (first and k < 4):
                        pe.wait_ge(added, c * OUT + (k - 3))
                    for f in range(2):
                        rows = act_hi[:, 2 * parity + f, t * P:(t + 1) * P], act_lo[:, 2 * parity + f, t * P:(t + 1) * P]
                        cols = slice(half * BANK, (half + 1) * BANK)
                        last = split_product(pe, banks[4 + k % 4][:], *rows, hi[:, f, cols], lo[:, f, cols],
                                             f == 0, f == 1)
                    last.then_inc(down_done, 1)

            pe.wait_ge(norm.lo_ready, KD)
            gate_up(0, 0, True)
            gate_up(1, 1, False)

            def step(c, parity, first):
                gate_up(c * 2, 0, False)
                gate_up(c * 2 + 1, 1, False)
                down(c - 1, 1 - parity, first, down_hi, down_lo)
            chunks(pe, step)
            down(NCH - 1, (NCH - 1) % 2, False, last_down_hi, last_down_lo)
            follower.tensor_tail(pe)


class Projected:

    def __init__(self, nc, mem):
        self.c = mem.at("conv_in", AT_X, [P, MLH, T + TAPS - 1])
        self.gates = mem.at("gates", AT_X + 17, [NGATE, T])
        self.stage = mem.at("stage", AT_X + 21, [P, 4, BANK])
        self.q = mem.at("q_na", AT_REST, [P, TT, NAW])
        self.k = mem.at("k_na", AT_REST + 16, [P, TT, NAW])
        self.v = mem.at("v_ml", AT_REST + 32, [P, TT, MLH, MLD + 1])
        self.o_dram = nc.dram_tensor("o_scratch", [T, MLW], F32, kind="Internal").ap()
        self.v_dram = nc.dram_tensor("v_scratch", [T, NAW], F32, kind="Internal").ap()


class Projection:

    def __init__(self, nc, mem, x, gain, w_in, ident, banks):
        self.norm = Norm(nc, mem, "mix", x, gain, ident, banks)
        self.raw = mem.at("proj_raw", AT_REST + 56, [P, KD, BANK])
        self.w_v = w_in.rearrange("o (k p) c -> p (o k) c", p=P)
        self.raw_loaded = [mem.semaphore(f"proj_raw_loaded{k}") for k in range(KD)]

    def load(self, sp, kd, col, width):
        sp.dma_start(self.raw[:, kd, 0:width], self.w_v[:, kd, col:col + width]).then_inc(self.raw_loaded[kd], 16)

    def prefetch(self, sp):
        for kd in range(KD):
            self.load(sp, kd, 0, BANK)


def project(nc, mem, projection, x_stored, b_gates, banks):
    sem = lambda s: mem.semaphore(f"proj_{s}")
    norm, raw, raw_loaded = projection.norm, projection.raw, projection.raw_loaded
    out = Projected(nc, mem)
    w_hi = mem.at("proj_w_hi", AT_W, [P, KD, BANK], F32R)
    w_lo = mem.at("proj_w_lo", AT_W + 16, [P, KD, BANK], F32R)
    bias = mem.at("gate_bias", AT_SMALL + 1, [NGATE, 1])

    gate_col = 3 * MLW
    token_slabs = [MLW, 2 * MLW] + [gate_col + NGATE + NAW * n for n in range(3)]
    slabs = [(0, BANK), (gate_col, P)] + [(c, BANK) for c in token_slabs]

    bias_loaded = sem("bias_loaded")
    hi_ready = sem("hi_ready")
    w_split = sem("w_split")
    piece_used = sem("piece_used")
    tile_done = sem("tile_done")
    even_read = sem("even_read")
    odd_read = sem("odd_read")
    padded = sem("padded")
    stage_stored = [sem(f"stage_stored{k}") for k in range(4)]
    MT = 8

    with nc.Block() as block:
        @block.sync
        def _(sp):
            with nc.allow_non_contiguous_dma(reason="a bias per partition"):
                sp.dma_start(bias[:], b_gates.rearrange("o g -> g o")).then_inc(bias_loaded, 16)
            for s, (col, width) in enumerate(slabs):
                for kd in range(KD if s else 0):
                    sp.wait_ge(w_split, KD * (s - 1) + kd + 1)
                    projection.load(sp, kd, col, width)
            sp.wait_ge(x_stored, 16 * TT)

        @block.gpsimd
        def _(pool):
            pool.wait_ge(x_stored, 16 * TT)
            pool.wait_ge(norm.lo_ready, HALVES * KD)
            pool.memset(out.c[:, :, 0:2], 0.0).then_inc(padded, 1)
            pool.memset(out.c[:, :, T + 2:T + 4], 0.0).then_inc(padded, 1)
            pool.memset(out.v[:, :, :, MLD:MLD + 1], 1.0).then_inc(padded, 1)
            for n, (s, dram) in enumerate(((3, out.o_dram), (6, out.v_dram))):
                for t in range(TT):
                    read = 5 + 4 * (s - 2) + t // 2 + 1
                    pool.wait_ge(odd_read if t % 2 else even_read, read)
                    pool.dma_start(dram[t * P:(t + 1) * P, :], out.stage[:, t % 4, :])\
                        .then_inc(stage_stored[t % 4], 16)
            for k in range(4):
                pool.wait_ge(stage_stored[k], 16 * 4)
            pool.wait_ge(padded, 3)

        def destination(s, t):
            if s == 0:
                half, m = divmod(t, MLH)
                return out.c[:, m, 2 + half * BANK:2 + (half + 1) * BANK]
            if s == 2:
                return out.v[:, t, :, 0:MLD]
            if s in (4, 5):
                return (out.q if s == 4 else out.k)[:, t, :]
            return out.stage[:, t % 4, :]

        def source(s, t):
            b = banks[t][:]
            return b.rearrange("p (h d) -> p h d", h=MLH) if s == 2 else b

        def wait_stage(eng, s, t):
            if s in (3, 6) and (s, t // 4) != (3, 0):
                eng.wait_ge(stage_stored[t % 4], 16 * (t // 4 if s == 3 else 2 + t // 4))

        first_tile = lambda s: 0 if s == 0 else 8 if s == 1 else 10 + MT * (s - 2)

        @block.scalar
        def _(a):
            def split(s):
                for kd in range(KD):
                    width = slabs[s][1]
                    if s and kd < KD - 1:
                        a.wait_ge(piece_used, (KD - 1) * (s - 1) + kd + 1)
                    elif s:
                        a.wait_ge(tile_done, first_tile(s))
                    a.wait_ge(raw_loaded[kd], 16 * (s + 1))
                    a.activation(w_hi[:, kd, 0:width], raw[:, kd, 0:width], ACT.Copy).then_inc(hi_ready, 1)

            def read(s, t):
                a.wait_ge(tile_done, first_tile(s) + t + 1)
                wait_stage(a, s, t)
                a.activation(destination(s, t), source(s, t), ACT.Copy).then_inc(even_read, 1)

            split(0)
            norm.squares(a, 1, lambda eng, t: None)
            a.wait_ge(x_stored, 16 * TT)
            for t in (0, 2):
                read(0, t)
            norm.hi_parts(a, 1)
            read(0, 4)
            split(1)
            read(0, MT - 2)
            split(2)
            a.wait_ge(tile_done, first_tile(1) + 1)
            a.wait_ge(bias_loaded, 16)
            a.activation(out.gates[:, 0:BANK], banks[0][0:NGATE, :], ACT.Identity, bias=bias[:]).then_inc(even_read, 1)
            for s in range(2, len(slabs)):
                for t in range(0, MT, 2):
                    if t == MT - 2 and s + 1 < len(slabs):
                        split(s + 1)
                    read(s, t)

        @block.vector
        def _(dve):
            def split(s):
                for kd in range(KD):
                    width = slabs[s][1]
                    dve.wait_ge(hi_ready, KD * s + kd + 1)
                    dve.tensor_tensor(w_lo[:, kd, 0:width], raw[:, kd, 0:width], w_hi[:, kd, 0:width].bitcast(F32),
                                      ALU.subtract).then_inc(w_split, 1)

            def read(s, t):
                dve.wait_ge(tile_done, first_tile(s) + t + 1)
                wait_stage(dve, s, t)
                dve.tensor_copy(destination(s, t), source(s, t)).then_inc(odd_read, 1)

            split(0)
            norm.mean(dve, 1)
            for t in range(4, TT):
                norm.scale(dve, t)
            dve.wait_ge(x_stored, 16 * TT)
            for t in (1, 3):
                read(0, t)
            norm.lo_parts(dve, 1)
            read(0, 5)
            split(1)
            read(0, MT - 1)
            split(2)
            dve.wait_ge(tile_done, first_tile(1) + 2)
            dve.wait_ge(bias_loaded, 16)
            dve.tensor_scalar(out.gates[:, BANK:T], banks[1][0:NGATE, :], bias[:], None, ALU.add).then_inc(odd_read, 1)
            for s in range(2, len(slabs)):
                for t in range(1, MT, 2):
                    if t == MT - 1 and s + 1 < len(slabs):
                        split(s + 1)
                    read(s, t)

        @block.tensor
        def _(pe):
            cols = [slice(half * BANK, (half + 1) * BANK) for half in range(HALVES)]
            pe.wait_ge(norm.lo_ready, KD)
            for t in range(MT):
                half, m = divmod(t, MLH)
                if t == MLH:
                    norm.transposes(pe, 1)
                    pe.wait_ge(norm.lo_ready, HALVES * KD)
                for kd in range(KD):
                    if t == 0:
                        pe.wait_ge(w_split, kd + 1)
                    last = split_product(pe, banks[t][:], w_hi[:, kd, m * P:(m + 1) * P], w_lo[:, kd, m * P:(m + 1) * P],
                                         norm.h_hi[:, kd, cols[half]], norm.h_lo[:, kd, cols[half]],
                                         kd == 0, kd == KD - 1)
                    if t == MT - 1 and kd < KD - 1:
                        last.then_inc(piece_used, 1)
                last.then_inc(tile_done, 1)
            for half in range(HALVES):
                pe.wait_ge(odd_read if half else even_read, 1)
                for kd in range(KD):
                    if half == 0:
                        pe.wait_ge(w_split, KD + kd + 1)
                    last = split_product(pe, banks[half][:], w_hi[:, kd, 0:P], w_lo[:, kd, 0:P],
                                         norm.h_hi[:, kd, cols[half]], norm.h_lo[:, kd, cols[half]],
                                         kd == 0, kd == KD - 1)
                    if half and kd < KD - 1:
                        last.then_inc(piece_used, 1)
                last.then_inc(tile_done, 1)
            pe.wait_ge(even_read, 5)
            pe.wait_ge(odd_read, 5)
            with pe.Fori(0, len(token_slabs)) as s:
                for t in range(TT):
                    pe.wait_ge(odd_read if t % 2 else even_read, s * 4 + (t // 2 + 2))
                    for kd in range(KD):
                        if t == 0:
                            pe.wait_ge(w_split, s * KD + (2 * KD + kd + 1))
                        rows = slice(t * P, (t + 1) * P)
                        last = split_product(pe, banks[t][:], norm.h_hi[:, kd, rows], norm.h_lo[:, kd, rows],
                                             w_hi[:, kd, :], w_lo[:, kd, :], kd == 0, kd == KD - 1)
                        if t == TT - 1 and kd < KD - 1:
                            last.then_inc(piece_used, 1)
                    last.then_inc(tile_done, 1)
    return out


def attend(nc, mem, pr, gq, gk, rpb, ident, banks):
    sem = lambda s: mem.semaphore(f"na_{s}")
    q_t = mem.at("na_qT", AT_H, [P, PAIRS, T])
    k_t = mem.at("na_kT", AT_H + 16, [P, PAIRS, T])
    v_even = mem.at("na_v_even", AT_H + 32, [P, TT, NAW])
    v_odd = mem.at("na_v_odd", AT_H + 48, [P, TT - 1, NAW])
    y_t = mem.at("na_yT", AT_REST + 32, [P, PAIRS, T])
    bias = mem.at("na_bias", AT_W + 16, [P, PAIRS, NDR, GRID_W])
    v_pair = mem.at("na_v_pair", AT_X, [P, 2 * TT - 1, P])
    negs = mem.at("na_negs", AT_X + 8, [P, 4, BANK])
    probs = mem.at("na_probs", AT_X + 16, [P, 4, BANK])
    probs_t = mem.at("na_probsT", AT_X + 24, [P, 4, BANK])
    q_diag = mem.at("na_q_diag", AT_W + 1, [P, 4, P])
    squares = mem.at("na_squares", AT_W + 4, [P, 2, NAW])
    bias_pair = mem.at("na_bias_pair", AT_W + 8, [P, NDR, GRID_W])
    pad = mem.at("na_pad", AT_W, [NAH * NDR, 2 * GRID_W - 1])
    gains = mem.at("na_gains", AT_SMALL + 1, [P, 2])
    gain_q = mem.at("na_gain_q", AT_SMALL + 1.0625, [P, 1])
    sumsq = mem.at("na_sumsq", AT_SMALL + 1.5, [P, 2, TT, NAH])
    meansq = mem.at("na_meansq", AT_SMALL + 2, [P, 2, TT, NAH])
    root = mem.at("na_root", AT_SMALL + 2.5, [P, 2, TT, NAH])
    rstd = mem.at("na_rstd", AT_SMALL + 3, [P, 2, TT, NAH])
    neg_max = mem.at("na_neg_max", AT_SMALL + 3.5, [P, 4])
    row_sum = mem.at("na_row_sum", AT_SMALL + 3.5625, [P, 4])
    inv_sum = mem.at("na_inv_sum", AT_SMALL + 3.625, [P, 4])
    pad_dram = nc.dram_tensor("rpb_scratch", [NAH * NDR, 2 * GRID_W - 1], F32, kind="Internal").ap()

    gains_loaded = sem("gains_loaded")
    v_loaded = sem("v_loaded")
    pad_zeroed = sem("pad_zeroed")
    pad_loaded = sem("pad_loaded")
    pad_stored = sem("pad_stored")
    bias_loaded = sem("bias_loaded")
    bias_masked = sem("bias_masked")
    gain_scaled = sem("gain_scaled")
    bias_ready = sem("bias_ready")
    squared = sem("squared")
    summed = sem("summed")
    mean_ready = sem("mean_ready")
    root_ready = sem("root_ready")
    rstd_ready = sem("rstd_ready")
    normed = sem("normed")
    transposed = sem("transposed")
    qk_ready = sem("qk_ready")
    diag_zeroed = sem("diag_zeroed")
    diag_ready = sem("diag_ready")
    v_pair_ready = sem("v_pair_ready")
    scores_ready = sem("scores_ready")
    negs_ready = sem("negs_ready")
    probs_ready = sem("probs_ready")
    inv_ready = sem("inv_ready")
    probs_scaled = sem("probs_scaled")
    probs_turned = sem("probs_turned")
    probs_t_ready = sem("probs_t_ready")
    out_ready = sem("out_ready")
    out_read = sem("out_read")

    row_start = [min(max(r - WIN_H // 2, 0), GRID_H - WIN_H) for r in range(GRID_H)]
    R = GRID_H
    GROUPS = R // 4

    def pairs(eng, pair):
        pair(0, True)
        with eng.Fori(1, PAIRS) as p:
            pair(p, False)

    with nc.Block() as block:
        @block.sync
        def _(sp):
            for h in range(2):
                with nc.allow_non_contiguous_dma(reason="a gain per partition"):
                    for n, g in enumerate((gq, gk)):
                        sp.dma_start(gains[h * NAD:(h + 1) * NAD, n:n + 1], g.rearrange("o d -> d o"))\
                          .then_inc(gains_loaded, 16)
            sp.wait_ge(pad_zeroed, 1)
            sp.dma_start(pad[:, GRID_W - WIN_W:GRID_W - WIN_W + NDC], rpb.rearrange("o h r c -> (o h r) c"))\
              .then_inc(pad_loaded, 16)
            sp.wait_ge(pad_loaded, 16)
            sp.dma_start(pad_dram, pad[:]).then_inc(pad_stored, 16)
            sp.wait_ge(pad_stored, 16)
            width = 2 * GRID_W - 1
            for pair in range(PAIRS):
                for h in range(2):
                    first = (2 * pair + h) * NDR * width
                    sp.dma_start(bias[h * GRID_W:(h + 1) * GRID_W, pair],
                                 bass.AP(tensor=pad_dram.tensor, offset=first,
                                         ap=[[1, GRID_W], [width, NDR], [1, GRID_W]])).then_inc(bias_loaded, 16)
            sp.dma_start(v_even[:], pr.v_dram.rearrange("(t p) c -> p t c", p=P)).then_inc(v_loaded, 16)
            sp.dma_start(v_odd[:], pr.v_dram[GRID_W:T - GRID_W, :].rearrange("(t p) c -> p t c", p=P))\
              .then_inc(v_loaded, 16)

        @block.gpsimd
        def _(pool):
            pool.memset(pad[:], 0.0).then_inc(pad_zeroed, 1)
            for slot in range(4):
                pool.memset(q_diag[:, slot], 0.0).then_inc(diag_zeroed, 1)
            pool.wait_ge(bias_loaded, 16 * NAH)
            for h in range(2):
                view = bias[h * GRID_W:(h + 1) * GRID_W].rearrange("c a r k -> c (a r) k")
                low, high = view[:, :, 0:GRID_W - WIN_W], view[:, :, WIN_W:GRID_W]
                n = GRID_W - WIN_W
                pool.affine_select(out=low, in_=low, compare_op=ALU.is_ge, fill=NEG,
                                   base=WIN_W // 2 - (GRID_W - 1), pattern=[[0, PAIRS * NDR], [1, n]],
                                   channel_multiplier=1).then_inc(bias_masked, 1)
                pool.wait_ge(bias_masked, 2 * h + 1)
                pool.affine_select(out=high, in_=high, compare_op=ALU.is_ge, fill=NEG,
                                   base=WIN_W // 2 - 1 - WIN_W + GRID_W - 1,
                                   pattern=[[0, PAIRS * NDR], [-1, n]], channel_multiplier=-1).then_inc(bias_masked, 1)
            pool.wait_ge(v_loaded, 32)
            pool.wait_ge(qk_ready, 2 * PAIRS * HALVES)
            pool.wait_ge(diag_zeroed, 4)

            def pair(p, first):
                for r in range(R):
                    if not (first and r < 4):
                        pool.wait_ge(scores_ready, p * R + (r - 3))
                    for h in range(2):
                        rows = slice(h * NAD, (h + 1) * NAD)
                        pool.tensor_copy(q_diag[rows, r % 4, h * GRID_W:(h + 1) * GRID_W],
                                         q_t[rows, p, r * GRID_W:(r + 1) * GRID_W]).then_inc(diag_ready, 1)
                    if r == 3:
                        if not first:
                            pool.wait_ge(out_ready, p * GROUPS)
                        pool.wait_ge(diag_ready, p * (2 * R) + 8)
                        pool.tensor_copy(v_pair[:, 0:TT], v_even[:, :, bass.ds(p * P, P)]).then_inc(v_pair_ready, 1)
                        pool.tensor_copy(v_pair[:, TT:], v_odd[:, :, bass.ds(p * P, P)]).then_inc(v_pair_ready, 1)
                        pool.wait_ge(v_pair_ready, p * 2 + 2)
            pairs(pool, pair)

        @block.scalar
        def _(a):
            for n in range(2 * TT):
                src = pr.q if n < TT else pr.k
                if n >= 2:
                    a.wait_ge(summed, n - 1)
                a.activation(squares[:, n % 2], src[:, n % TT], ACT.Square).then_inc(squared, 1)
            for w in range(2):
                a.wait_ge(mean_ready, w + 1)
                a.activation(root[:, w], meansq[:, w], ACT.Sqrt).then_inc(root_ready, 1)
            a.wait_ge(gains_loaded, 64)
            a.wait_ge(gain_scaled, 1)
            for m in range(2 * PAIRS * HALVES):
                w, pair, half = m // (PAIRS * HALVES), m // HALVES % PAIRS, m % HALVES
                a.wait_ge(transposed, m + 1)
                to, turned = (q_t, k_t)[w][:, pair, half * BANK:(half + 1) * BANK], banks[m % 4][:]
                if w == 0:
                    to = to.rearrange("d (r q) -> d r q", q=GRID_W)
                    turned = turned.rearrange("d (r q) -> d r q", q=GRID_W)[:, :, ::-1]
                a.activation(to, turned, ACT.Copy, scale=(gains[:, 1:2] if w else gain_q[:])).then_inc(qk_ready, 1)

            def exponentials(p, r, first):
                a.wait_ge(negs_ready, p * R + (r + 1))
                if not (first and r < 4):
                    a.wait_ge(probs_turned, p * R + (r - 3))
                a.activation(probs[:, r % 4], negs[:, r % 4], ACT.Exp, scale=-1.0, bias=neg_max[:, r % 4:r % 4 + 1],
                             accum_out=row_sum[:, r % 4:r % 4 + 1]).then_inc(probs_ready, 1)

            def read_turned(p, r):
                a.wait_ge(probs_turned, p * R + (r + 1))
                a.activation(probs_t[:, r % 4], banks[4 + r % 2][:], ACT.Copy).then_inc(probs_t_ready, 1)

            def pair(p, first):
                for i in range(R + 2):
                    if i < R:
                        exponentials(p, i, first)
                    if i >= 2:
                        read_turned(p, i - 2)
            pairs(a, pair)

        @block.vector
        def _(dve):
            dve.wait_ge(gains_loaded, 64)
            dve.tensor_scalar(gain_q[:], gains[:, 0:1], NAD ** -0.5, None, ALU.mult).then_inc(gain_scaled, 1)
            for n in range(2 * TT):
                w, t = divmod(n, TT)
                dve.wait_ge(squared, n + 1)
                dve.tensor_reduce(sumsq[:, w, t], squares[:, n % 2].rearrange("p (h d) -> p h d", d=NAD), AX.X,
                                  ALU.add).then_inc(summed, 1)
                if t == TT - 1:
                    dve.wait_ge(summed, n + 1)
                    dve.tensor_scalar(meansq[:, w], sumsq[:, w], 1.0 / NAD, EPS, ALU.mult, ALU.add).then_inc(mean_ready, 1)
            for w in range(2):
                dve.wait_ge(root_ready, w + 1)
                dve.reciprocal(rstd[:, w], root[:, w]).then_inc(rstd_ready, 1)
            for n in range(2 * TT):
                w, t = divmod(n, TT)
                dve.wait_ge(rstd_ready, w + 1)
                tile = (pr.k if w else pr.q)[:, t].rearrange("p (h d) -> p h d", d=NAD)
                dve.tensor_tensor(tile, tile, rstd[:, w, t].unsqueeze(2).to_broadcast([P, NAH, NAD]), ALU.mult)\
                   .then_inc(normed, 1)
            dve.wait_ge(bias_masked, 4)

            def bias_of_pair(p):
                dve.tensor_copy(bias_pair[:, WIN_H - 1:], bias[:, p, WIN_H - 1:]).then_inc(bias_ready, 1)
                dve.wait_ge(bias_ready, p * 2 + 1)
                dve.wait_ge(scores_ready, p * R + 1)
                dve.tensor_copy(bias_pair[:, 0:WIN_H - 1], bias[:, p, 0:WIN_H - 1]).then_inc(bias_ready, 1)

            def negate_and_max(p, r):
                dr = row_start[r] - r + WIN_H - 1
                dve.tensor_tensor_reduce(negs[:, r % 4], banks[r % 4][:],
                                         bias_pair[:, dr:dr + WIN_H].rearrange("c r k -> c (r k)"), -1.0, 3.0e38,
                                         ALU.add, ALU.min, neg_max[:, r % 4:r % 4 + 1]).then_inc(negs_ready, 1)

            def rows(p, i):
                if i == 0:
                    bias_of_pair(p)
                    negate_and_max(p, 0)
                    return
                r = i - 1
                if i == 1:
                    dve.wait_ge(bias_ready, p * 2 + 2)
                if i < R:
                    dve.wait_ge(scores_ready, p * R + (i + 1))
                dve.wait_ge(probs_ready, p * R + i)
                dve.reciprocal(inv_sum[:, r % 4:r % 4 + 1], row_sum[:, r % 4:r % 4 + 1]).then_inc(inv_ready, 1)
                if i < R:
                    negate_and_max(p, i)
                dve.wait_ge(inv_ready, p * R + i)
                dve.tensor_scalar(probs[:, r % 4], probs[:, r % 4], inv_sum[:, r % 4:r % 4 + 1], None, ALU.mult)\
                   .then_inc(probs_scaled, 1)

            def read_out(p, g):
                dve.wait_ge(out_ready, p * GROUPS + (g + 1))
                for h in range(2):
                    rows = slice(h * NAD, (h + 1) * NAD)
                    dve.tensor_copy(y_t[rows, p, g * 4 * GRID_W:(g + 1) * 4 * GRID_W].rearrange("d (r q) -> d r q", r=4),
                                    banks[6 + g % 2][rows, :].rearrange("d (r q) -> d r q", r=4)[
                                        :, :, h * GRID_W:(h + 1) * GRID_W][:, :, ::-1]).then_inc(out_read, 1)

            def pair(p, first):
                for i in range(R + 4):
                    if i <= R:
                        rows(p, i)
                    if i >= 7 and i % 4 == 3:
                        read_out(p, i // 4 - 1)
            pairs(dve, pair)

        @block.tensor
        def _(pe):
            for m in range(2 * PAIRS * HALVES):
                w, pair, half = m // (PAIRS * HALVES), m // HALVES % PAIRS, m % HALVES
                pe.wait_ge(normed, w * TT + 4 * half + 4)
                if m >= 4:
                    pe.wait_ge(qk_ready, m - 3)
                for j in range(4):
                    last = pe.transpose(banks[m % 4][:, j * P:(j + 1) * P],
                                        (pr.k if w else pr.q)[:, 4 * half + j, pair * P:(pair + 1) * P], ident[:])
                last.then_inc(transposed, 1)
            pe.wait_ge(qk_ready, 2 * PAIRS * HALVES)

            def scores(p, r, first):
                pe.wait_ge(diag_ready, p * (2 * R) + (2 * r + 2))
                if not (first and r < 4):
                    pe.wait_ge(negs_ready, p * R + (r - 3))
                start = row_start[r] * GRID_W
                pe.matmul(banks[r % 4][:], q_diag[:, r % 4], k_t[:, p, start:start + WIN_H * GRID_W], start=True,
                          stop=True).then_inc(scores_ready, 1)

            def turn(p, r, first):
                pe.wait_ge(probs_scaled, p * R + (r + 1))
                if not (first and r < 2):
                    pe.wait_ge(probs_t_ready, p * R + (r - 1))
                for j in range(4):
                    last = pe.transpose(banks[4 + r % 2][:, j * P:(j + 1) * P], probs[:, r % 4, j * P:(j + 1) * P],
                                        ident[:])
                last.then_inc(probs_turned, 1)

            def values(p, r, first):
                g = r // 4
                pe.wait_ge(probs_t_ready, p * R + (r + 1))
                if r == 0:
                    pe.wait_ge(v_pair_ready, p * 2 + 2)
                if r % 4 == 0 and not (first and g < 2):
                    pe.wait_ge(out_read, p * (2 * GROUPS) + 2 * (g - 1))
                tile = row_start[r] // 2 + (TT if row_start[r] % 2 else 0)
                for j in range(4):
                    last = pe.matmul(banks[6 + g % 2][:, (r % 4) * P:(r % 4 + 1) * P], v_pair[:, tile + j],
                                     probs_t[:, r % 4, j * P:(j + 1) * P], start=(j == 0), stop=(j == 3))
                if r % 4 == 3:
                    last.then_inc(out_ready, 1)

            def pair(p, first):
                for i in range(R + 3):
                    if i < R:
                        scores(p, i, first)
                    if 2 <= i < R + 2:
                        turn(p, i - 2, first)
                    if i >= 3:
                        values(p, i - 3, first)
            pairs(pe, pair)
    return y_t


def mlstm(nc, mem, pr, conv_w, conv_b, w_q, w_k, gn, ident, banks):
    sem = lambda s: mem.semaphore(f"ml_{s}")
    NC, DIRS = T // P, 2
    UD = MLH * NC
    U = DIRS * UD
    SCALE = MLD ** -0.5
    MAXLOW = -3.0e38
    FWD, BWD = slice(0, UD), slice(UD, U)

    u_t = mem.at("ml_uT", AT_H, [P, MLH, T])
    q_t = mem.at("ml_qT", AT_H + 16, [P, MLH, T])
    k_t = mem.at("ml_kT", AT_H + 32, [P, MLH, T])
    k_tok = mem.at("ml_k", AT_H + 48, [P, NC, MLH, MLD])
    m_all = [mem.at("ml_M_fwd", AT_X, [P, MLH, NC, P]),
             mem.at("ml_M_bwd", AT_H, [P, MLH, NC, P])]
    hs = mem.at("ml_h", AT_REST + 49, [P, NC, MLH, MLD])
    state = mem.at("ml_state", AT_REST + 65, [P, DIRS, MLH, MLD + 1])
    w_qk = mem.at("ml_w_qk", AT_W, [P, 2, MLH, MLD])
    conv = mem.at("ml_conv", AT_W + 4, [P, 2, T])
    taps = mem.at("ml_taps", AT_W + 12, [P, MLH, TAPS])
    conv_bias = mem.at("ml_conv_bias", AT_W + 12.25, [P, MLH])
    names = "li f neg_abs expf lnf lf b z runmax M m floor weights ones m0_rows decay_rows".split()
    row = {n: mem.at(f"ml_{n}", AT_W + 13 + 0.5 * i, [U, P]) for i, n in enumerate(names)}
    col = {n: mem.at(f"ml_{n}", AT_W + 22 + 0.0625 * i, [U, 1])
           for i, n in enumerate("g mloc m0 end neg_end decay".split())}
    line = mem.at("ml_line", AT_W + 23, [1, 4, U])
    one = mem.at("ml_one", AT_W + 24, [1, 1])
    unit_cols = mem.at("ml_unit_cols", AT_SMALL + 1, [P, 5, U])
    z_cols, w_cols, floor_cols, m0_cols, decay_cols = (unit_cols[:, i] for i in range(5))
    mask = mem.at("ml_mask", AT_SMALL + 2.5, [P, DIRS, P])
    ring = lambda n, kib: mem.at(f"ml_{n}", AT_W + kib, [P, DIRS, MLH, P])
    arg, weight, weighted = ring("arg", 0), ring("weight", 4), ring("weighted", 8)
    carry, q_scaled = ring("carry", 12), ring("q_scaled", 16)
    k_chunk, k_weighted = ring("k_chunk", 20), ring("k_weighted", 24)
    den = mem.at("ml_den", AT_SMALL + 4, [P, DIRS, MLH])
    den_max = mem.at("ml_den_max", AT_SMALL + 4.0625, [P, DIRS, MLH])
    den_inv = mem.at("ml_den_inv", AT_SMALL + 4.125, [P, DIRS, MLH])
    o = mem.at("ml_o", AT_X, [P, NC, MLH, MLD])
    squares = mem.at("ml_squares", AT_W, [P, NC, MLH, MLD])
    gn_all = mem.at("ml_gn_all", AT_W + 16, [P, MLH, MLD])
    sumsq = mem.at("ml_sumsq", AT_SMALL + 4.25, [P, NC, MLH])
    meansq = mem.at("ml_meansq", AT_SMALL + 4.375, [P, NC, MLH])
    root = mem.at("ml_root", AT_SMALL + 4.5, [P, NC, MLH])
    rstd = mem.at("ml_rstd", AT_SMALL + 4.625, [P, NC, MLH])
    gates_dram = nc.dram_tensor("gates_scratch", [NGATE * NC, P], F32, kind="Internal").ap()
    m_dram = nc.dram_tensor("m_scratch", [U, P], F32, kind="Internal").ap()

    gates_stored, units_loaded = sem("gates_stored"), sem("units_loaded")
    weights_loaded, taps_loaded = sem("weights_loaded"), sem("taps_loaded")
    chain = sem("chain")
    abs_ready, exp_ready, one_plus_ready, ln_ready = sem("abs"), sem("exp"), sem("one_plus"), sem("ln")
    ends_ready, ends_turned = sem("ends_ready"), sem("ends_turned")
    m0_line_ready, m0_turned = sem("m0_line_ready"), sem("m0_turned")
    m_ready, unit_vectors_ready = sem("m_ready"), sem("unit_vectors_ready")
    exps_ready, rows_ready, cols_turned, cols_ready = sem("exps"), sem("rows"), sem("cols_turned"), sem("cols_ready")
    ones_ready, masked, hs_zeroed = sem("ones_ready"), sem("masked"), sem("hs_zeroed")
    conv_ready, u_ready, qk_done, q_read, k_read = (sem(s) for s in "conv u qk_done q_read k_read".split())
    m_stored, m_loaded = sem("m_stored"), sem("m_loaded")

    with nc.Block() as block:
        @block.sync
        def _(sp):
            sp.dma_start(gates_dram.rearrange("(g c) l -> g (c l)", g=NGATE), pr.gates[:]).then_inc(gates_stored, 16)
            with nc.allow_non_contiguous_dma(reason="taps and biases per channel"):
                for h in range(MLH):
                    sp.dma_start(taps[:, h], conv_w[0, :, h * P:(h + 1) * P].rearrange("j p -> p j"))\
                      .then_inc(taps_loaded, 16)
                sp.dma_start(conv_bias[:], conv_b.rearrange("o (h p) -> p (o h)", p=P)).then_inc(taps_loaded, 16)
            sp.wait_ge(gates_stored, 16)
            for d in range(DIRS):
                for n, name in enumerate(("li", "f")):
                    first = (2 * d + n) * UD
                    sp.dma_start(row[name][d * UD:(d + 1) * UD, :], gates_dram[first:first + UD, :])\
                      .then_inc(units_loaded, 16)
            sp.dma_start(w_qk[:, 0], w_q.rearrange("o h d e -> d (o h) e")).then_inc(weights_loaded, 16)
            sp.dma_start(w_qk[:, 1], w_k.rearrange("o h d e -> d (o h) e")).then_inc(weights_loaded, 16)
            sp.wait_ge(m_ready, 1)
            sp.dma_start(m_dram, row["M"][:]).then_inc(m_stored, 16)
            sp.wait_ge(m_stored, 16)
            for d in range(DIRS):
                if d == 0:
                    sp.wait_ge(u_ready, MLH)
                else:
                    sp.wait_ge(qk_done, 4 * MLH + NC)
                sp.dma_start(m_all[d][:].rearrange("p h c l -> p (h c l)"),
                             m_dram[d * UD:(d + 1) * UD, :].rearrange("u l -> (u l)").partition_broadcast(P))\
                  .then_inc(m_loaded, 16)
            sp.wait_ge(m_loaded, 32)

        @block.gpsimd
        def _(pool):
            pool.memset(row["ones"][:], 1.0).then_inc(ones_ready, 1)
            pool.memset(one[:], 1.0).then_inc(ones_ready, 1)
            pool.memset(line[:], 0.0).then_inc(ones_ready, 1)
            pool.memset(mask[:], 0.0).then_inc(ones_ready, 1)
            pool.wait_ge(ones_ready, 4)
            pool.affine_select(out=mask[:, 0], in_=mask[:, 0], compare_op=ALU.is_ge, fill=-NEG, base=0,
                               pattern=[[1, P]], channel_multiplier=-1).then_inc(masked, 1)
            pool.affine_select(out=mask[:, 1], in_=mask[:, 1], compare_op=ALU.is_ge, fill=-NEG, base=0,
                               pattern=[[-1, P]], channel_multiplier=1).then_inc(masked, 1)
            pool.memset(hs[:], 0.0).then_inc(hs_zeroed, 1)
            pool.memset(state[:], 0.0).then_inc(hs_zeroed, 1)
            pool.wait_ge(masked, 2)
            pool.wait_ge(hs_zeroed, 2)

        @block.vector
        def _(dve):
            steps = [0]

            def step(instruction):
                steps[0] += 1
                instruction.then_inc(chain, 1)
                dve.wait_ge(chain, steps[0])

            dve.wait_ge(taps_loaded, 16 * (MLH + 1))
            for h in range(MLH):
                acc = conv[:, h % 2]
                if h >= 2:
                    dve.wait_ge(u_ready, h - 1)
                step(dve.tensor_scalar(acc, pr.c[:, h, 0:T], taps[:, h, 0:1], conv_bias[:, h:h + 1], ALU.mult, ALU.add))
                for j in range(1, TAPS):
                    tap = dve.scalar_tensor_tensor(out=acc, in0=pr.c[:, h, j:j + T], scalar=taps[:, h, j:j + 1],
                                                   in1=acc, op0=ALU.mult, op1=ALU.add)
                    if j < TAPS - 1:
                        step(tap)
                tap.then_inc(conv_ready, 1)
            dve.wait_ge(units_loaded, 64)
            dve.wait_ge(ones_ready, 3)
            dve.scalar_tensor_tensor(out=row["neg_abs"][:], in0=row["f"][:], scalar=-1.0, in1=row["f"][:],
                                     op0=ALU.mult, op1=ALU.min).then_inc(abs_ready, 1)
            dve.wait_ge(exp_ready, 1)
            dve.tensor_scalar(row["expf"][:], row["expf"][:], 1.0, None, ALU.add).then_inc(one_plus_ready, 1)
            dve.wait_ge(ln_ready, 1)
            step(dve.scalar_tensor_tensor(out=row["lf"][:], in0=row["f"][:], scalar=0.0, in1=row["lnf"][:],
                                          op0=ALU.min, op1=ALU.subtract))
            ones, lf, b, z, runmax = (row[n] for n in ("ones", "lf", "b", "z", "runmax"))
            step(dve.tensor_tensor_scan(b[FWD], ones[FWD], lf[FWD], 0.0, ALU.mult, ALU.add))
            step(dve.tensor_tensor_scan(b[BWD, ::-1], ones[BWD], lf[BWD, ::-1], 0.0, ALU.mult, ALU.add))
            step(dve.tensor_tensor(z[:], row["li"][:], b[:], ALU.subtract))
            step(dve.tensor_tensor_scan(runmax[FWD], ones[FWD], z[FWD], MAXLOW, ALU.mult, ALU.max))
            step(dve.tensor_tensor_scan(runmax[BWD, ::-1], ones[BWD], z[BWD, ::-1], MAXLOW, ALU.mult, ALU.max))
            for part, last in ((FWD, slice(P - 1, P)), (BWD, slice(0, 1))):
                step(dve.tensor_copy(col["g"][part], b[part, last]))
                dve.tensor_tensor(col["mloc"][part], b[part, last], runmax[part, last], ALU.add).then_inc(ends_ready, 1)
            dve.wait_ge(ends_turned, 1)
            step(dve.tensor_copy(line[:, 0:2], banks[4][0:1, 0:2 * U].rearrange("p (a u) -> p a u", a=2)))
            for d in range(DIRS):
                for h in range(MLH):
                    first = d * UD + h * NC
                    g, mloc, m = (line[:, i, first:first + NC] for i in range(3))
                    if d:
                        g, mloc, m = g[:, ::-1], mloc[:, ::-1], m[:, ::-1]
                    step(dve.tensor_tensor_scan(m, g, mloc, 0.0, ALU.add, ALU.max))
            by_head = lambda i, d: line[:, i, d * UD:(d + 1) * UD].rearrange("p (h c) -> p h c", h=MLH)
            step(dve.tensor_copy(by_head(3, 0)[:, :, 1:NC], by_head(2, 0)[:, :, 0:NC - 1]))
            dve.tensor_copy(by_head(3, 1)[:, :, 0:NC - 1], by_head(2, 1)[:, :, 1:NC]).then_inc(m0_line_ready, 1)
            dve.wait_ge(m0_turned, 1)
            step(dve.tensor_copy(col["m0"][:], banks[5][0:U, 0:1]))
            dve.tensor_scalar(row["M"][:], runmax[:], col["m0"][:], None, ALU.max).then_inc(m_ready, 1)
            dve.wait_ge(m_ready, 1)
            step(dve.tensor_tensor(row["m"][:], b[:], row["M"][:], ALU.add))
            for part, last in ((FWD, slice(P - 1, P)), (BWD, slice(0, 1))):
                dve.tensor_scalar(col["neg_end"][part], row["M"][part, last], -1.0, None, ALU.mult)\
                   .then_inc(unit_vectors_ready, 1)
            dve.tensor_scalar(row["m0_rows"][:], ones[:], col["m0"][:], None, ALU.mult).then_inc(rows_ready, 1)
            dve.wait_ge(exps_ready, 3)
            dve.tensor_scalar(row["decay_rows"][:], ones[:], col["decay"][:], None, ALU.mult).then_inc(rows_ready, 1)
            dve.wait_ge(cols_turned, 1)
            dve.tensor_copy(unit_cols[:].rearrange("p a u -> p (a u)"), banks[6][:, 0:5 * U]).then_inc(cols_ready, 1)
            dve.wait_ge(cols_ready, 1)
            for n in range(2 * MLH):
                dve.wait_ge(qk_done, 2 * n + 2)
                dve.tensor_scalar(k_t[:, n // 2, n % 2 * BANK:(n % 2 + 1) * BANK], banks[2 * (n % 2) + 1][:], SCALE,
                                  None, ALU.mult).then_inc(k_read, 1)

        @block.scalar
        def _(a):
            for h in range(MLH):
                a.wait_ge(conv_ready, h + 1)
                a.activation(u_t[:, h], conv[:, h % 2], ACT.Silu).then_inc(u_ready, 1)
            a.wait_ge(abs_ready, 1)
            a.activation(row["expf"][:], row["neg_abs"][:], ACT.Exp).then_inc(exp_ready, 1)
            a.wait_ge(one_plus_ready, 1)
            a.activation(row["lnf"][:], row["expf"][:], ACT.Ln).then_inc(ln_ready, 1)
            a.wait_ge(unit_vectors_ready, 2)
            a.activation(row["floor"][:], row["m"][:], ACT.Exp, scale=-1.0).then_inc(exps_ready, 1)
            a.activation(row["weights"][:], row["z"][:], ACT.Exp, bias=col["neg_end"][:]).then_inc(exps_ready, 1)
            a.activation(col["decay"][:], col["m0"][:], ACT.Exp, bias=col["neg_end"][:]).then_inc(exps_ready, 1)
            for n in range(2 * MLH):
                a.wait_ge(qk_done, 2 * n + 1)
                a.activation(q_t[:, n // 2, n % 2 * BANK:(n % 2 + 1) * BANK], banks[2 * (n % 2)][:], ACT.Copy)\
                 .then_inc(q_read, 1)
            for c in range(NC):
                a.wait_ge(qk_done, 4 * MLH + c + 1)
                a.activation(k_tok[:, c].rearrange("p h e -> p (h e)"), banks[2 * (c % 2)][:], ACT.Copy, scale=SCALE)\
                 .then_inc(q_read, 1)

        @block.tensor
        def _(pe):
            pe.wait_ge(ends_ready, 2)
            pe.matmul(banks[4][0:1, 0:U], col["g"][:], ident[0:U, 0:U], start=True, stop=True)
            pe.matmul(banks[4][0:1, U:2 * U], col["mloc"][:], ident[0:U, 0:U], start=True, stop=True)\
              .then_inc(ends_turned, 1)
            pe.wait_ge(m0_line_ready, 1)
            pe.matmul(banks[5][0:U, 0:1], line[:, 3, :], one[:], start=True, stop=True).then_inc(m0_turned, 1)
            pe.wait_ge(rows_ready, 2)
            for i, name in enumerate(("z", "weights", "floor")):
                pe.transpose(banks[6][:, i * U:(i + 1) * U], row[name][:], ident[0:U, 0:U])
            for i, name in ((3, "m0_rows"), (4, "decay_rows")):
                last = pe.matmul(banks[6][:, i * U:(i + 1) * U], row[name][:], ident[0:U, 0:U], start=True, stop=True)
            last.then_inc(cols_turned, 1)
            pe.wait_ge(weights_loaded, 32)
            for n in range(2 * MLH):
                h, half = divmod(n, 2)
                pe.wait_ge(u_ready, h + 1)
                if n >= 2:
                    pe.wait_ge(q_read, n - 1)
                    pe.wait_ge(k_read, n - 1)
                for w in range(2):
                    pe.matmul(banks[2 * half + w][:], w_qk[:, w, h], u_t[:, h, half * BANK:(half + 1) * BANK],
                              start=True, stop=True).then_inc(qk_done, 1)
            for c in range(NC):
                pe.wait_ge(q_read, 2 * MLH + c - 1)
                for h in range(MLH):
                    last = pe.matmul(banks[2 * (c % 2)][:, h * P:(h + 1) * P], u_t[:, h, c * P:(c + 1) * P], w_qk[:, 1, h],
                                     start=True, stop=True)
                last.then_inc(qk_done, 1)

    k_copied, k_scaled, q_carried = sem("k_copied"), sem("k_scaled"), sem("q_carried")
    arg_ready, weight_ready, carry_ready = sem("arg_ready"), sem("weight_ready"), sem("carry_ready")
    scores_done, weighted_ready, sums_done, update_done = (
        sem(s) for s in "scores_done weighted_ready sums_done update_done".split())
    updated, den_step, h_added = sem("updated"), sem("den_step"), sem("h_added")


    def steps(eng, step):
        step(0, True, False)
        with eng.Fori(1, NC - 1) as i:
            step(i, False, False)
        step(NC - 1, False, True)

    chunk = lambda i, d: i * -1 + (NC - 1) if d else i
    following = lambda i, d: (i + d, 1 - d)
    units_of = lambda cols, c, d: cols[:, d * UD:(d + 1) * UD].rearrange("p (h c) -> p h c", h=MLH)[:, :, c]
    head_bank = lambda d, h: banks[2 + 2 * d + h // 2][:, (h % 2) * (MLD + 1):(h % 2 + 1) * (MLD + 1)]
    update_bank = lambda h: banks[6 + h // 2][:, (h % 2) * (MLD + 1):(h % 2 + 1) * (MLD + 1)]

    with nc.Block() as block:
        @block.gpsimd
        def _(pool):
            def step(i, first, last_step):
                for d in range(DIRS):
                    n, c = i * 2 + d, chunk(i, d)
                    if not first:
                        pool.wait_ge(update_done, n - 1)
                    pool.tensor_tensor(k_weighted[:, d], k_tok[:, c],
                                       units_of(w_cols, c, d).unsqueeze(2).to_broadcast([P, MLH, P]), ALU.mult)\
                        .then_inc(k_scaled, 1)
                    pool.wait_ge(carry_ready, n + 1)
                    if not first:
                        pool.wait_ge(sums_done, n - 1)
                    pool.tensor_tensor(q_scaled[:, d], q_t[:, :, bass.ds(c * P, P)], carry[:, d], ALU.mult)\
                        .then_inc(q_carried, 1)
            steps(pool, step)

        @block.scalar
        def _(a):
            def step(i, first, last_step):
                for d in range(DIRS):
                    n, c = i * 2 + d, chunk(i, d)
                    if not first:
                        a.wait_ge(scores_done, n - 1)
                    a.activation(k_chunk[:, d], k_t[:, :, bass.ds(c * P, P)], ACT.Copy).then_inc(k_copied, 1)
                    a.wait_ge(arg_ready, n + 1)
                    if not first:
                        a.wait_ge(weighted_ready, n - 1)
                    for h in range(MLH):
                        unit = d * UD + h * NC + c
                        last = a.activation(weight[:, d, h], arg[:, d, h], ACT.Exp, scale=-1.0,
                                            bias=z_cols[:, bass.ds(unit, 1)])
                    last.then_inc(weight_ready, 1)
                    if not first:
                        a.wait_ge(q_carried, n - 1)
                    for h in range(MLH):
                        unit = d * UD + h * NC + c
                        last = a.activation(carry[:, d, h], m_all[d][:, h, c], ACT.Exp, scale=-1.0,
                                            bias=m0_cols[:, bass.ds(unit, 1)])
                    last.then_inc(carry_ready, 1)
            steps(a, step)

        @block.vector
        def _(dve):
            def mask_m(i, d, first):
                if not first:
                    dve.wait_ge(weight_ready, i * 2 + (d - 1))
                dve.tensor_tensor(arg[:, d], m_all[d][:, :, chunk(i, d)], mask[:, d].unsqueeze(1).to_broadcast([P, MLH, P]),
                                  ALU.add).then_inc(arg_ready, 1)

            def weigh(i, d, first):
                n = i * 2 + d
                dve.wait_ge(weight_ready, n + 1)
                if not first:
                    dve.wait_ge(sums_done, n - 1)
                dve.wait_ge(scores_done, n + 1)
                dve.tensor_tensor(weighted[:, d], weight[:, d], banks[d][:].rearrange("p (h l) -> p h l", h=MLH),
                                  ALU.mult).then_inc(weighted_ready, 1)

            def absorb(i, d):
                n, c = i * 2 + d, chunk(i, d)
                dve.wait_ge(sums_done, n + 1)
                dve.wait_ge(update_done, n + 1)
                for h in range(MLH):
                    unit = d * UD + h * NC + c
                    last = dve.scalar_tensor_tensor(out=state[:, d, h], in0=state[:, d, h],
                                                    scalar=decay_cols[:, bass.ds(unit, 1)], in1=update_bank(h),
                                                    op0=ALU.mult, op1=ALU.add)
                last.then_inc(updated, 1)
                floors = units_of(floor_cols, c, d)
                dens = [banks[2 + 2 * d + half][:, 0:2 * (MLD + 1)].rearrange("p (h e) -> p h e", h=2)[:, :, MLD]
                        for half in range(2)]
                for half in range(2):
                    pair = slice(2 * half, 2 * half + 2)
                    last = dve.scalar_tensor_tensor(out=den[:, d, pair], in0=dens[half], scalar=-1.0,
                                                    in1=floors[:, pair], op0=ALU.mult, op1=ALU.max)
                last.then_inc(den_step, 1)
                dve.wait_ge(den_step, n * 3 + 1)
                for half in range(2):
                    pair = slice(2 * half, 2 * half + 2)
                    last = dve.tensor_tensor(den_max[:, d, pair], dens[half], den[:, d, pair], ALU.max)
                last.then_inc(den_step, 1)
                dve.wait_ge(den_step, n * 3 + 2)
                dve.reciprocal(den_inv[:, d], den_max[:, d]).then_inc(den_step, 1)
                dve.wait_ge(den_step, n * 3 + 3)
                for h in range(MLH):
                    last = dve.scalar_tensor_tensor(out=hs[:, c, h], in0=head_bank(d, h)[:, 0:MLD],
                                                    scalar=den_inv[:, d, h:h + 1], in1=hs[:, c, h],
                                                    op0=ALU.mult, op1=ALU.add)
                last.then_inc(h_added, 1)

            for d in range(DIRS):
                mask_m(0, d, True)
            weigh(0, 0, True)

            def step(i, first, last_step):
                for d in range(DIRS):
                    if not last_step:
                        mask_m(i + 1, d, False)
                    if not (last_step and d):
                        weigh(*following(i, d), first and d == 0)
                    absorb(i, d)
            steps(dve, step)

        @block.tensor
        def _(pe):
            def scores(i, d, first):
                n, c = i * 2 + d, chunk(i, d)
                pe.wait_ge(k_copied, n + 1)
                if not first:
                    pe.wait_ge(weighted_ready, n - 1)
                for h in range(MLH):
                    last = pe.matmul(banks[d][:, h * P:(h + 1) * P], k_chunk[:, d, h], q_t[:, h, bass.ds(c * P, P)],
                                     start=True, stop=True)
                last.then_inc(scores_done, 1)

            def sums(i, d, first):
                n, c = i * 2 + d, chunk(i, d)
                pe.wait_ge(weighted_ready, n + 1)
                pe.wait_ge(q_carried, n + 1)
                if not first:
                    pe.wait_ge(updated, n - 1)
                    pe.wait_ge(h_added, n - 1)
                for h in range(MLH):
                    pe.matmul(head_bank(d, h), weighted[:, d, h], pr.v[:, c, h], start=True, stop=False)
                    last = pe.matmul(head_bank(d, h), q_scaled[:, d, h], state[:, d, h], start=False, stop=True)
                last.then_inc(sums_done, 1)
                pe.wait_ge(k_scaled, n + 1)
                if not (first and d == 0):
                    pe.wait_ge(updated, n)
                for h in range(MLH):
                    last = pe.matmul(update_bank(h), k_weighted[:, d, h], pr.v[:, c, h], start=True, stop=True)
                last.then_inc(update_done, 1)

            scores(0, 0, True)

            def step(i, first, last_step):
                for d in range(DIRS):
                    if not (last_step and d):
                        scores(*following(i, d), first and d == 0)
                    sums(i, d, first)
            steps(pe, step)

    o_loaded, gn_loaded = sem("o_loaded"), sem("gn_loaded")
    squared, mean_ready, root_ready, y_step, sigmoid_ready = (
        sem(s) for s in "squared mean_ready root_ready y_step sigmoid_ready".split())

    with nc.Block() as block:
        @block.sync
        def _(sp):
            sp.dma_start(o[:].rearrange("p c h e -> p c (h e)"), pr.o_dram.rearrange("(c p) w -> p c w", p=P))\
              .then_inc(o_loaded, 16)
            sp.dma_start(gn_all[:].rearrange("p h e -> p (h e)"), gn.rearrange("o h e -> (o h e)").partition_broadcast(P))\
              .then_inc(gn_loaded, 16)

        @block.scalar
        def _(a):
            for c in range(NC):
                a.activation(squares[:, c], hs[:, c], ACT.Square).then_inc(squared, 1)
            a.wait_ge(mean_ready, 1)
            a.activation(root[:], meansq[:], ACT.Sqrt).then_inc(root_ready, 1)
            a.wait_ge(o_loaded, 16)
            for c in range(NC):
                a.activation(o[:, c], o[:, c], ACT.Sigmoid).then_inc(sigmoid_ready, 1)

        @block.vector
        def _(dve):
            for c in range(NC):
                dve.wait_ge(squared, c + 1)
                dve.tensor_reduce(sumsq[:, c], squares[:, c], AX.X, ALU.add).then_inc(y_step, 1)
            dve.wait_ge(y_step, NC)
            dve.tensor_scalar(meansq[:], sumsq[:], 1.0 / MLD, EPS, ALU.mult, ALU.add).then_inc(mean_ready, 1)
            dve.wait_ge(root_ready, 1)
            dve.reciprocal(rstd[:], root[:]).then_inc(y_step, 1)
            dve.wait_ge(y_step, NC + 1)
            dve.wait_ge(gn_loaded, 16)
            for c in range(NC):
                dve.tensor_tensor(hs[:, c], hs[:, c], rstd[:, c].unsqueeze(2).to_broadcast([P, MLH, MLD]), ALU.mult)\
                   .then_inc(y_step, 1)
                dve.wait_ge(y_step, NC + 2 + 3 * c)
                dve.tensor_tensor(hs[:, c], hs[:, c], gn_all[:], ALU.mult).then_inc(y_step, 1)
                dve.wait_ge(y_step, NC + 3 + 3 * c)
                dve.wait_ge(sigmoid_ready, c + 1)
                dve.tensor_tensor(hs[:, c], hs[:, c], o[:, c], ALU.mult).then_inc(y_step, 1)
            dve.wait_ge(y_step, NC + 1 + 3 * NC)
    return hs


def mix_out(nc, mem, x, x_scratch, y_ml, y_na, w_out, ident, banks, follower, prefetch):
    sem = lambda s: mem.semaphore(f"out_{s}")
    y_hi = mem.at("out_y_hi", AT_H, [P, KD, T], F32R)
    y_lo = mem.at("out_y_lo", AT_H + 32, [P, KD, T], F32R)
    w_hi = mem.at("out_w_hi", AT_W, [P, KD, BANK], F32R)
    w_lo = mem.at("out_w_lo", AT_W + 16, [P, KD, BANK], F32R)
    raw = mem.at("out_raw", AT_REST, [P, HALVES, KD, BANK])
    w_v = w_out.rearrange("o (k p) (s c) -> p (o k) s c", p=P, s=HALVES)

    x_loaded = [sem(f"x_loaded{t}") for t in range(TT)]
    raw_loaded = [sem(f"raw_loaded{s}") for s in range(HALVES)]
    hi_ready, w_split = sem("hi_ready"), sem("w_split")
    piece_used = sem("piece_used")
    transposed = sem("transposed")
    y_hi_ready, y_split = sem("y_hi_ready"), sem("y_split")
    tile_done, added = sem("tile_done"), sem("added")
    STEPS = [(half, kd) for half in range(HALVES) for kd in range(KD)]
    turned_before = lambda half, kd: half * MLH + min(kd, MLH)

    with nc.Block() as block:
        @block.sync
        def _(sp):
            for kd in range(KD):
                sp.dma_start(raw[:, 0, kd], w_v[:, kd, 0]).then_inc(raw_loaded[0], 16)
            for t in range(TT):
                sp.dma_start(x[:, t, :], x_scratch[t * P:(t + 1) * P, :]).then_inc(x_loaded[t], 16)
            for kd in range(KD):
                sp.dma_start(raw[:, 1, kd], w_v[:, kd, 1]).then_inc(raw_loaded[1], 16)
            sp.wait_ge(y_split, HALVES * KD)
            follower.load(sp)
            prefetch(sp)
            follower.sync_tail(sp)

        def y_source(half, kd):
            if kd < MLH:
                return banks[4 + turned_before(half, kd) % 4][:]
            return y_na[:, kd - MLH, half * BANK:(half + 1) * BANK]

        @block.scalar
        def _(a):
            for half, kd in STEPS:
                if kd < MLH:
                    a.wait_ge(transposed, turned_before(half, kd) + 1)
                a.activation(y_hi[:, kd, half * BANK:(half + 1) * BANK], y_source(half, kd), ACT.Copy)\
                 .then_inc(y_hi_ready, 1)
            for s in range(HALVES):
                a.wait_ge(raw_loaded[s], 16 * KD)
                for kd in range(KD):
                    if s and kd < KD - 1:
                        a.wait_ge(piece_used, kd + 1)
                    elif s:
                        a.wait_ge(tile_done, TT)
                    a.activation(w_hi[:, kd], raw[:, s, kd], ACT.Copy).then_inc(hi_ready, 1)
            a.wait_ge(w_split, KD * HALVES)
            follower.scalar_tail(a, lambda eng, t: eng.wait_ge(added, TT + t + 1))

        @block.vector
        def _(dve):
            for n, (half, kd) in enumerate(STEPS):
                dve.wait_ge(y_hi_ready, n + 1)
                cols = slice(half * BANK, (half + 1) * BANK)
                dve.tensor_tensor(y_lo[:, kd, cols], y_source(half, kd), y_hi[:, kd, cols].bitcast(F32),
                                  ALU.subtract).then_inc(y_split, 1)
            for s in range(HALVES):
                for kd in range(KD):
                    dve.wait_ge(hi_ready, KD * s + kd + 1)
                    dve.tensor_tensor(w_lo[:, kd], raw[:, s, kd], w_hi[:, kd].bitcast(F32), ALU.subtract)\
                       .then_inc(w_split, 1)
                for t in range(TT):
                    part = x[:, t, s * BANK:(s + 1) * BANK]
                    if s == 0:
                        dve.wait_ge(x_loaded[t], 16)
                    dve.wait_ge(tile_done, TT * s + t + 1)
                    dve.tensor_tensor(part, banks[t][:], part, ALU.add).then_inc(added, 1)
                    if s and t >= 4:
                        follower.vector_after_tile(dve, t)
            follower.vector_tail(dve)

        @block.tensor
        def _(pe):
            for half in range(HALVES):
                for h in range(MLH):
                    n = half * MLH + h
                    if n >= 4:
                        pe.wait_ge(y_split, n - 3)
                    for j in range(4):
                        last = pe.transpose(banks[4 + n % 4][:, j * P:(j + 1) * P], y_ml[:, 4 * half + j, h], ident[:])
                    last.then_inc(transposed, 1)
            for s in range(HALVES):
                for t in range(TT):
                    if s:
                        pe.wait_ge(added, t + 1)
                    elif t % 4 == 0:
                        pe.wait_ge(y_split, KD * (t // 4 + 1))
                    for kd in range(KD):
                        if t == 0:
                            pe.wait_ge(w_split, KD * s + kd + 1)
                        rows = slice(t * P, (t + 1) * P)
                        last = split_product(pe, banks[t][:], y_hi[:, kd, rows], y_lo[:, kd, rows],
                                             w_hi[:, kd], w_lo[:, kd], kd == 0, kd == KD - 1)
                        if s == 0 and t == TT - 1 and kd < KD - 1:
                            last.then_inc(piece_used, 1)
                    last.then_inc(tile_done, 1)
            follower.tensor_tail(pe)


class FinalNorm:

    GROUPS = ((0, 4), (4, 6), (6, 8))

    def __init__(self, nc, mem, x, gain, out):
        self.x, self.gain, self.out = x, gain, out
        self.g = mem.at("final_g", AT_H, [P, D])
        self.result = mem.at("final_result", AT_H + 8, [P, TT, D])
        self.sumsq, self.meansq, self.root, self.rstd = (
            mem.at(f"final_{n}", AT_SMALL + 0.5 + 0.0625 * i, [P, TT]) for i, n in enumerate("sumsq meansq root rstd".split()))
        (self.gain_loaded, self.squared, self.mean_ready, self.root_ready, self.rstd_ready, self.result_ready,
         self.stored) = (mem.semaphore(f"final_{s}") for s in
                         "gain_loaded squared mean_ready root_ready rstd_ready result_ready stored".split())

    def load(self, sp):
        sp.dma_start(self.g[:], self.gain.rearrange("o d -> (o d)").partition_broadcast(P)).then_inc(self.gain_loaded, 16)

    def sync_tail(self, sp):
        for t in range(TT):
            sp.wait_ge(self.result_ready, t + 1)
            sp.dma_start(self.out[t * P:(t + 1) * P, :], self.result[:, t]).then_inc(self.stored, 16)
        sp.wait_ge(self.stored, 16 * TT)

    def scalar_tail(self, act, x_here):
        for n, (first, end) in enumerate(self.GROUPS):
            for t in range(first, end):
                x_here(act, t)
                act.activation(self.result[:, t], self.x[:, t], ACT.Square, accum_out=self.sumsq[:, t:t + 1])\
                   .then_inc(self.squared, 1)
            act.wait_ge(self.mean_ready, n + 1)
            act.activation(self.root[:, first:end], self.meansq[:, first:end], ACT.Sqrt).then_inc(self.root_ready, 1)

    def statistics(self, dve, n):
        first, end = self.GROUPS[n]
        dve.wait_ge(self.squared, end)
        dve.tensor_scalar(self.meansq[:, first:end], self.sumsq[:, first:end], 1.0 / D, EPS, ALU.mult, ALU.add)\
           .then_inc(self.mean_ready, 1)
        dve.wait_ge(self.root_ready, n + 1)
        dve.reciprocal(self.rstd[:, first:end], self.root[:, first:end]).then_inc(self.rstd_ready, 1)
        dve.wait_ge(self.rstd_ready, n + 1)

    def results(self, dve, *tiles):
        for t in tiles:
            dve.scalar_tensor_tensor(out=self.result[:, t], in0=self.x[:, t], scalar=self.rstd[:, t:t + 1],
                                     in1=self.g[:], op0=ALU.mult, op1=ALU.mult).then_inc(self.result_ready, 1)

    def vector_after_tile(self, dve, t):
        if t == 4:
            self.statistics(dve, 0)
            dve.wait_ge(self.gain_loaded, 16)
            self.results(dve, 0)
        elif t == 5:
            self.results(dve, 1)
        elif t == 6:
            self.statistics(dve, 1)
            self.results(dve, 2)

    def vector_tail(self, dve):
        self.results(dve, 3, 4, 5)
        self.statistics(dve, 2)
        self.results(dve, 6, 7)

    def tensor_tail(self, pe):
        pass


def hybrid_mlstm_natten_macaron_encoder_kernel(
        nc, x, norm_ffn1, w1_gate, w1_up, w1_down, norm_mix, w_in, b_gates, conv_w, conv_b, w_q_ml, w_k_ml, gn_ml,
        gq_na, gk_na, rpb, w_out, norm_ffn2, w2_gate, w2_up, w2_down, norm_final, out):
    mem = Memory(nc)
    banks = [nc.alloc_psum_tensor(f"bank{k}", [P, BANK], F32) for k in range(8)]
    x_scratch = nc.dram_tensor("x_scratch", [T, D], F32, kind="Internal").ap()
    resident = mem.at("x_resident", AT_X, [P, TT, D])
    ident = make_identity(nc, mem)
    ffn1 = FeedForward(nc, mem, "ffn1", resident, norm_ffn1, w1_gate, w1_up, w1_down, ident, banks)
    x_loaded = start(nc, resident, x.rearrange("o t d -> (o t) d"), ffn1)
    projection = Projection(nc, mem, resident, norm_mix, w_in, ident, banks)
    x_stored = ffn1.run(lambda eng, t: eng.wait_ge(x_loaded[t], 16), x_scratch, projection.norm, projection.prefetch)
    projected = project(nc, mem, projection, x_stored, b_gates, banks)
    y_ml = mlstm(nc, mem, projected, conv_w, conv_b, w_q_ml, w_k_ml, gn_ml, ident, banks)
    y_na = attend(nc, mem, projected, gq_na, gk_na, rpb, ident, banks)
    mem.clear_semaphores()
    ffn2 = FeedForward(nc, mem, "ffn2", resident, norm_ffn2, w2_gate, w2_up, w2_down, ident, banks)
    mix_out(nc, mem, resident, x_scratch, y_ml, y_na, w_out, ident, banks, ffn2.norm, ffn2.prefetch)
    ffn2.run(lambda eng, t: None, None, FinalNorm(nc, mem, resident, norm_final, out.rearrange("o t d -> (o t) d")),
             lambda sp: None)


_INS = ["x", "norm_ffn1", "w1_gate", "w1_up", "w1_down", "norm_mix", "w_in", "b_gates", "conv_w", "conv_b", "w_q_ml",
        "w_k_ml", "gn_ml", "gq_na", "gk_na", "rpb", "w_out", "norm_ffn2", "w2_gate", "w2_up", "w2_down", "norm_final"]
_OUTS = [((1, T, D), "float32")]


def kernel(**inputs):
    import numpy as _np
    import concourse.bacc as _bacc
    from concourse import mybir as _mybir
    from concourse.bass_utils import run_bass_kernel_spmd as _run

    nc = _bacc.Bacc("TRN2", target_bir_lowering=False, num_devices=1)
    arrays, args = {}, []
    for name in _INS:
        a = _np.ascontiguousarray(inputs[name])
        arrays[f"in_{name}_dram"] = a
        args.append(nc.dram_tensor(f"in_{name}_dram", a.shape, _mybir.dt.from_np(a.dtype), kind="ExternalInput").ap())
    for i, (shape, dtype) in enumerate(_OUTS):
        dt = _mybir.dt.from_np(_np.dtype(dtype))
        args.append(nc.dram_tensor(f"out_{i}_dram", shape, dt, kind="ExternalOutput").ap())
    hybrid_mlstm_natten_macaron_encoder_kernel(nc, *args)
    r = _run(nc, [arrays], core_ids=[0])
    return r.results[0]["out_0_dram"]
```

```python
from contextlib import ExitStack

import concourse.bass as bass
from concourse import mybir

F32 = mybir.dt.float32
F32R = mybir.dt.float32r
ALU = mybir.AluOpType
ACT = mybir.ActivationFunctionType
AX = mybir.AxisListType

P = 128
KB = 1024
BANK = 512
EPS = 1e-6

T = 1024
D = 1024
DFF = 2816
TT = T // P
KD = D // P
HALVES = T // BANK
NF = DFF // P
NCH = NF // 2

GRID_W = 64
GRID_H = T // GRID_W
MLH, MLD = 4, 128
MLW = MLH * MLD
TAPS = 5
NAH, NAD = 8, 64
NAW = NAH * NAD
PAIRS = NAH // 2
WIN_H, WIN_W = 8, 16
NDR, NDC = 2 * WIN_H - 1, 2 * WIN_W - 1
NGATE = 4 * MLH
DIN = 3 * MLW + NGATE + 3 * NAW
NC, DIRS = T // P, 2
UD = MLH * NC
U = DIRS * UD
FWD, BWD = slice(0, UD), slice(UD, U)
LOWEST = -3.0e38
WARM_UP = 32
EARLY = 4
NEG = -1.0e30


class Memory:

    def __init__(self, nc):
        self.nc = nc
        self.semaphores = []
        self.base = -(-nc.sbuf_base // 64) * 64

    def semaphore(self, name):
        self.semaphores.append(self.nc.alloc_semaphore(name))
        return self.semaphores[-1]

    def clear_semaphores(self):
        self.nc.clear_and_free_semaphores(self.semaphores)
        self.nc.all_engine_barrier()
        self.semaphores = []

    def at(self, name, kib, shape, dtype=F32):
        return self.nc.alloc_sbuf_tensor_at(name, shape, dtype, offset=self.base + int(kib * KB))


AT_SMALL = 0
AT_X = 7
AT_H = 39
AT_W = 103
AT_REST = 135


def make_identity(nc, mem):
    ident = mem.at("ident", AT_SMALL, [P, P])
    identity_zeroed = mem.semaphore("identity_zeroed")
    identity_made = mem.semaphore("identity_made")
    with nc.Block() as block:
        @block.gpsimd
        def _(pool):
            pool.memset(ident[:], 0.0).then_inc(identity_zeroed, 1)
            pool.wait_ge(identity_zeroed, 1)
            pool.affine_select(out=ident[:], in_=ident[:], compare_op=ALU.not_equal, fill=1.0, base=0,
                               pattern=[[-1, P]], channel_multiplier=1).then_inc(identity_made, 1)
            pool.wait_ge(identity_made, 1)
    return ident


def load_table(act, mem, ident, function, name):
    unused = mem.at(f"unused_{name}", AT_SMALL + 6.875, [P, 1])
    act.activation(unused[:], ident[:, 0:1], function)


class Norm:

    def __init__(self, nc, mem, tag, x, gain, ident, banks):
        sem = lambda s: mem.semaphore(f"{tag}_{s}")
        self.nc, self.x, self.gain, self.ident = nc, x, gain, ident
        self.banks = [banks[0:4], banks[4:8]]
        self.h_hi = mem.at(f"{tag}_h_hi", AT_H, [P, KD, T], F32R)
        self.h_lo = mem.at(f"{tag}_h_lo", AT_H + 32, [P, KD, T], F32R)
        scaled = [mem.at(f"{tag}_scaled{i}", AT_REST + kib, [P, 2, D]) for i, kib in enumerate((8, 24, 0, 16))]
        self.scaled = [scaled[t // 2][:, t % 2] for t in range(TT)]
        self.g = mem.at(f"{tag}_g", AT_SMALL + 0.5, [P, KD])
        self.sumsq = mem.at(f"{tag}_sumsq", AT_SMALL + 0.625, [P, TT])
        self.meansq = mem.at(f"{tag}_meansq", AT_SMALL + 0.6875, [P, TT])
        self.root = mem.at(f"{tag}_root", AT_SMALL + 0.75, [P, TT])
        self.rstd = mem.at(f"{tag}_rstd", AT_SMALL + 0.8125, [P, TT])
        self.gain_loaded = sem("gain_loaded")
        self.squared = sem("squared")
        self.mean_ready = sem("mean_ready")
        self.root_ready = sem("root_ready")
        self.rstd_ready = sem("rstd_ready")
        self.scaled_ready = sem("scaled_ready")
        self.transposed = sem("transposed")
        self.hi_ready = sem("hi_ready")
        self.lo_ready = sem("lo_ready")

    def load(self, sp):
        with self.nc.allow_non_contiguous_dma(reason="a gain per partition"):
            sp.dma_start(self.g[:], self.gain.rearrange("o (k p) -> p (o k)", p=P)).then_inc(self.gain_loaded, 16)

    def squares(self, act, half, x_here):
        for t in range(4 * half, 4 * half + 4):
            x_here(act, t)
            act.activation(self.scaled[t], self.x[:, t, :], ACT.Square,
                           accum_out=self.sumsq[:, t:t + 1]).then_inc(self.squared, 1)
        tiles = slice(4 * half, 4 * half + 4)
        act.wait_ge(self.mean_ready, half + 1)
        act.activation(self.root[:, tiles], self.meansq[:, tiles], ACT.Sqrt).then_inc(self.root_ready, 1)

    def hi_parts(self, act, half):
        act.wait_ge(self.gain_loaded, 16)
        for kd in range(KD):
            act.wait_ge(self.transposed, half * KD + kd + 1)
            act.activation(self.h_hi[:, kd, half * BANK:(half + 1) * BANK], self.banks[half][kd % 4][:], ACT.Copy,
                           scale=self.g[:, kd:kd + 1]).then_inc(self.hi_ready, 1)

    def mean(self, dve, half):
        tiles = slice(4 * half, 4 * half + 4)
        dve.wait_ge(self.squared, 4 * half + 4)
        dve.tensor_scalar(self.meansq[:, tiles], self.sumsq[:, tiles], 1.0 / D, EPS, ALU.mult,
                          ALU.add).then_inc(self.mean_ready, 1)
        dve.wait_ge(self.root_ready, half + 1)
        dve.reciprocal(self.rstd[:, tiles], self.root[:, tiles]).then_inc(self.rstd_ready, 1)
        dve.wait_ge(self.rstd_ready, half + 1)

    def scale(self, dve, t):
        dve.tensor_scalar(self.scaled[t], self.x[:, t, :], self.rstd[:, t:t + 1], None,
                          ALU.mult).then_inc(self.scaled_ready, 1)

    def lo_parts(self, dve, half):
        dve.wait_ge(self.gain_loaded, 16)
        for kd in range(KD):
            dve.wait_ge(self.hi_ready, half * KD + kd + 1)
            cols = slice(half * BANK, (half + 1) * BANK)
            dve.scalar_tensor_tensor(out=self.h_lo[:, kd, cols], in0=self.banks[half][kd % 4][:],
                                     scalar=self.g[:, kd:kd + 1], in1=self.h_hi[:, kd, cols].bitcast(F32),
                                     op0=ALU.mult, op1=ALU.subtract).then_inc(self.lo_ready, 1)

    def transposes(self, pe, half, part):
        pe.wait_ge(self.scaled_ready, 4 * half + 4)
        for kd in range(4 * part, 4 * part + 4):
            if kd >= 4:
                pe.wait_ge(self.lo_ready, half * KD + kd - 3)
            for j in range(4):
                last = pe.transpose(self.banks[half][kd % 4][:, j * P:(j + 1) * P],
                                    self.scaled[4 * half + j][:, kd * P:(kd + 1) * P], self.ident[:])
            last.then_inc(self.transposed, 1)


    def scalar_tail(self, act, x_here, between=lambda act: None):
        self.squares(act, 0, x_here)
        between(act)
        self.hi_parts(act, 0)

    def vector_after_tile(self, dve, t):
        if t == 4:
            self.mean(dve, 0)
        for tile in {4: (0, 1), 5: (2, 3)}.get(t, ()):
            self.scale(dve, tile)

    def vector_before_last(self, dve):
        self.lo_parts(dve, 0)

    def vector_tail(self, dve):
        pass

    def tensor_tail(self, pe, part):
        self.transposes(pe, 0, part)

    def sync_tail(self, sp):
        pass

    def pool_tail(self, pool):
        pass


def start(nc, x, x_dram, ffn, ident, banks):
    warm = ffn.mem.semaphore("warm")
    x_loaded = [ffn.mem.semaphore(f"x_loaded{t}") for t in range(TT)]
    norm = ffn.norm
    with nc.Block() as block:
        @block.sync
        def _(sp):
            for t in range(TT):
                if t == 4:
                    norm.load(sp)
                    ffn.prefetch(sp)
                sp.dma_start(x[:, t, :], x_dram[t * P:(t + 1) * P, :]).then_inc(x_loaded[t], 16)

        @block.scalar
        def _(act):
            load_table(act, ffn.mem, ident, ACT.Sqrt, "sqrt")
            norm.scalar_tail(act, lambda eng, t: eng.wait_ge(x_loaded[t], 16),
                             ffn.scalar_head)

        @block.vector
        def _(dve):
            norm.mean(dve, 0)
            for t in range(4):
                norm.scale(dve, t)
            ffn.vector_head(dve)
            norm.vector_before_last(dve)

        @block.tensor
        def _(pe):
            for n in range(WARM_UP):
                last = pe.matmul(banks[7][:, 0:P], ident[:], ident[:], start=True, stop=True)
            last.then_inc(warm, 1)
            norm.tensor_tail(pe, 0)
            norm.tensor_tail(pe, 1)
            pe.wait_ge(warm, 1)
    return x_loaded


def split_product(pe, out, w_hi, w_lo, r_hi, r_lo, first, last):
    pe.matmul(out, w_hi, r_hi, start=first, stop=False)
    pe.matmul(out, w_hi, r_lo, start=False, stop=False)
    return pe.matmul(out, w_lo, r_hi, start=False, stop=last)


class FeedForward:

    def __init__(self, nc, mem, tag, x, gain, w_gate, w_up, w_down, ident, banks):
        self.nc, self.mem, self.tag, self.x, self.banks = nc, mem, tag, x, banks
        self.norm = Norm(nc, mem, tag, x, gain, ident, banks)
        self.raw_gate = mem.at(f"{tag}_raw_gate", AT_REST + 32, [P, KD, 2 * P])
        self.raw_up = mem.at(f"{tag}_raw_up", AT_REST + 40, [P, KD, 2 * P])
        self.raw_down = mem.at(f"{tag}_raw_down", AT_REST + 48, [P, 2, D])
        self.gate_v = w_gate.rearrange("o (k p) f -> p (o k) f", p=P)
        self.up_v = w_up.rearrange("o (k p) f -> p (o k) f", p=P)
        self.down_v = w_down.rearrange("o (f p) d -> p (o f) d", p=P)
        self.gate_loaded, self.up_loaded, self.down_loaded = (
            mem.semaphore(f"{tag}_{s}_loaded") for s in ("gate", "up", "down"))
        self.w_hi = mem.at(f"{tag}_w_hi", AT_W, [P, 2, 2, KD, P], F32R)
        self.w_lo = mem.at(f"{tag}_w_lo", AT_W + 16, [P, 2, 2, KD, P], F32R)
        self.gate_up_hi = mem.semaphore(f"{tag}_gate_up_hi")
        self.gate_up_split = mem.semaphore(f"{tag}_gate_up_split")

    def load_gate_up(self, sp, c):
        cols = bass.ds(c * (2 * P), 2 * P)
        sp.dma_start(self.raw_gate[:], self.gate_v[:, :, cols]).then_inc(self.gate_loaded, 16)
        sp.dma_start(self.raw_up[:], self.up_v[:, :, cols]).then_inc(self.up_loaded, 16)

    def load_down(self, sp, c):
        sp.dma_start(self.raw_down[:], self.down_v[:, bass.ds(c * 2, 2), :]).then_inc(self.down_loaded, 16)

    def prefetch(self, sp):
        self.load_gate_up(sp, 0)
        self.load_down(sp, 0)

    def high_gate_up(self, a, j, k, which=(0, 1)):
        for m in which:
            raw, loaded = ((self.raw_gate, self.gate_loaded), (self.raw_up, self.up_loaded))[m]
            a.wait_ge(loaded, (j - k) * 8 + 16)
            a.activation(self.w_hi[:, k, m], raw[:, :, k * P:(k + 1) * P], ACT.Copy).then_inc(self.gate_up_hi, 1)

    def low_gate_up(self, dve, j, k, which=(0, 1)):
        for m in which:
            raw = (self.raw_gate, self.raw_up)[m]
            dve.wait_ge(self.gate_up_hi, j * 2 + (m + 1))
            low = dve.tensor_tensor(self.w_lo[:, k, m], raw[:, :, k * P:(k + 1) * P], self.w_hi[:, k, m].bitcast(F32),
                                    ALU.subtract)
        if 1 in which:
            low.then_inc(self.gate_up_split, 1)


    def scalar_head(self, a):
        self.high_gate_up(a, 0, 0, (0,))

    def vector_head(self, dve):
        self.low_gate_up(dve, 0, 0, (0,))

    def run(self, x_here, x_scratch, next_phase):
        feed_forward(self, x_here, x_scratch, next_phase)
        return self.stored


def feed_forward(ffn, x_here, x_scratch, next_phase):
    follower = next_phase.norm
    nc, mem, tag, x, banks, norm = ffn.nc, ffn.mem, ffn.tag, ffn.x, ffn.banks, ffn.norm
    raw_gate, raw_up, raw_down = ffn.raw_gate, ffn.raw_up, ffn.raw_down
    down_loaded, w_hi, w_lo, gate_up_split = ffn.down_loaded, ffn.w_hi, ffn.w_lo, ffn.gate_up_split
    sem = lambda s: mem.semaphore(f"{tag}_{s}")

    act_hi = mem.at(f"{tag}_act_hi", AT_REST, [P, 4, T], F32R)
    act_lo = mem.at(f"{tag}_act_lo", AT_REST + 16, [P, 4, T], F32R)
    down_hi = mem.at(f"{tag}_down_hi", AT_REST + 56, [P, 2, D], F32R)
    down_lo = mem.at(f"{tag}_down_lo", AT_REST + 64, [P, 2, D], F32R)
    last_down_hi = mem.at(f"{tag}_last_down_hi", AT_REST + 32, [P, 2, D], F32R)
    last_down_lo = mem.at(f"{tag}_last_down_lo", AT_REST + 40, [P, 2, D], F32R)
    silu = mem.at(f"{tag}_silu", AT_SMALL + 1, [P, BANK])
    act = mem.at(f"{tag}_act", AT_SMALL + 3, [P, BANK])

    down_hi_ready = sem("down_hi_ready")
    down_split = sem("down_split")
    gate_up_done = sem("gate_up_done")
    silu_ready = sem("silu_ready")
    act_ready = sem("act_ready")
    act_hi_ready = sem("act_hi_ready")
    act_split = sem("act_split")
    down_done = sem("down_done")
    added = sem("added")
    stored = ffn.stored = sem("stored")

    OUT = TT * HALVES

    def chunks(eng, step):
        step(1, 1, True)
        with eng.Fori(0, (NCH - 3) // 2) as i:
            for parity in range(2):
                step(2 * i + (2 + parity), parity, False)
        step(NCH - 1, (NCH - 1) % 2, False)

    LAST = OUT * (NCH - 1)
    x_added = lambda eng, t: eng.wait_ge(added, LAST + HALVES * (t + 1))

    with nc.Block() as block:
        @block.sync
        def _(sp):
            def step(c, parity, first):
                sp.wait_ge(gate_up_split, 2 * c)
                ffn.load_gate_up(sp, c)
                sp.wait_ge(down_split, c)
                ffn.load_down(sp, c)
            chunks(sp, step)
            sp.wait_ge(down_split, NCH)
            sp.wait_ge(down_done, LAST)
            follower.load(sp)
            next_phase.prefetch(sp)
            if x_scratch is not None:
                for t in range(TT):
                    x_added(sp, t)
                    sp.dma_start(x_scratch[t * P:(t + 1) * P, :], x[:, t, :]).then_inc(stored, 16)
            follower.sync_tail(sp)

        @block.gpsimd
        def _(pool):
            follower.pool_tail(pool)

        @block.scalar
        def _(a):
            def split_gate_up(j, k, chunk_done):
                a.wait_ge(gate_up_done, chunk_done)
                ffn.high_gate_up(a, j, k)

            def activate(j, slot):
                for half in range(HALVES):
                    n = j * 2 + half
                    a.wait_ge(gate_up_done, n + 1)
                    if not (isinstance(n, int) and n < 1):
                        a.wait_ge(act_ready, n)
                    a.activation(silu[:], banks[half][:], ACT.Silu).then_inc(silu_ready, 1)
                    a.wait_ge(act_ready, n + 1)
                    a.activation(act_hi[:, slot, half * BANK:(half + 1) * BANK], act[:], ACT.Copy)\
                     .then_inc(act_hi_ready, 1)

            def split_down(c, first, hi):
                if not first:
                    a.wait_ge(down_done, c * OUT)
                a.wait_ge(down_loaded, c * 16 + 16)
                a.activation(hi[:], raw_down[:], ACT.Copy).then_inc(down_hi_ready, 1)

            ffn.high_gate_up(a, 0, 0, (1,))
            norm.squares(a, 1, x_here)
            ffn.high_gate_up(a, 1, 1)
            norm.hi_parts(a, 1)
            activate(0, 0)

            def step(c, parity, first):
                split_gate_up(c * 2, 0, c * 4 - 2)
                activate(c * 2 - 1, 2 * (1 - parity) + 1)
                split_down(c - 1, first, down_hi)
                split_gate_up(c * 2 + 1, 1, c * 4)
                activate(c * 2, 2 * parity)
            chunks(a, step)
            a.wait_ge(gate_up_split, NF)
            split_down(NCH - 1, True, last_down_hi)
            activate(NF - 1, (NF - 1) % 4)
            follower.scalar_tail(a, x_added, next_phase.scalar_head)

        @block.vector
        def _(dve):
            def activate(j, slot):
                for half in range(HALVES):
                    n = j * 2 + half
                    cols = slice(half * BANK, (half + 1) * BANK)
                    dve.wait_ge(silu_ready, n + 1)
                    if not (isinstance(n, int) and n < 1):
                        dve.wait_ge(act_split, n)
                    dve.tensor_tensor(act[:], silu[:], banks[2 + half][:], ALU.mult).then_inc(act_ready, 1)
                    dve.wait_ge(act_hi_ready, n + 1)
                    dve.tensor_tensor(act_lo[:, slot, cols], act[:], act_hi[:, slot, cols].bitcast(F32),
                                      ALU.subtract).then_inc(act_split, 1)

            def add(c, follower=None):
                for k in range(OUT):
                    t, half = divmod(k, HALVES)
                    part = x[:, t, half * BANK:(half + 1) * BANK]
                    if follower and k == OUT - 2:
                        follower.vector_before_last(dve)
                    dve.wait_ge(down_done, c * OUT + (k + 1))
                    dve.scalar_tensor_tensor(out=part, in0=banks[4 + k % 4][:], scalar=0.5, in1=part,
                                             op0=ALU.mult, op1=ALU.add).then_inc(added, 1)
                    if follower and half and t >= 4:
                        follower.vector_after_tile(dve, t)
                        if t == TT - 2:
                            next_phase.vector_head(dve)

            def split_down(c, hi, lo):
                dve.wait_ge(down_hi_ready, c + 1)
                dve.tensor_tensor(lo[:], raw_down[:], hi[:].bitcast(F32), ALU.subtract).then_inc(down_split, 1)

            ffn.low_gate_up(dve, 0, 0, (1,))
            norm.mean(dve, 1)
            for t in range(4, TT):
                norm.scale(dve, t)
            ffn.low_gate_up(dve, 1, 1)
            norm.lo_parts(dve, 1)
            activate(0, 0)

            def step(c, parity, first):
                ffn.low_gate_up(dve, c * 2, 0)
                activate(c * 2 - 1, 2 * (1 - parity) + 1)
                if not first:
                    add(c - 2)
                split_down(c - 1, down_hi, down_lo)
                ffn.low_gate_up(dve, c * 2 + 1, 1)
                activate(c * 2, 2 * parity)
            chunks(dve, step)
            split_down(NCH - 1, last_down_hi, last_down_lo)
            activate(NF - 1, (NF - 1) % 4)
            add(NCH - 2)
            add(NCH - 1, follower)
            follower.vector_tail(dve)

        @block.tensor
        def _(pe):
            def gate_up(j, k, first):
                if not first:
                    pe.wait_ge(gate_up_split, j + 1)
                for half in range(HALVES):
                    cols = slice(half * BANK, (half + 1) * BANK)
                    if first and half:
                        pe.wait_ge(norm.lo_ready, HALVES * KD)
                    if not first:
                        pe.wait_ge(act_ready, j * 2 + (half - 1))
                    for m in range(2):
                        if first and m:
                            pe.wait_ge(gate_up_split, 1)
                        for kd in range(KD):
                            if first and half == 0 and m == 1 and kd in (3, 6):
                                norm.transposes(pe, 1, kd // 4)
                            last = split_product(pe, banks[2 * m + half][:], w_hi[:, k, m, kd], w_lo[:, k, m, kd],
                                                 norm.h_hi[:, kd, cols], norm.h_lo[:, kd, cols],
                                                 kd == 0, kd == KD - 1)
                    last.then_inc(gate_up_done, 1)

            def down(c, parity, first, hi, lo, follower=None):
                pe.wait_ge(act_split, c * 4 + 4)
                pe.wait_ge(down_split, c + 1)
                for k in range(OUT):
                    t, half = divmod(k, HALVES)
                    if follower and k >= OUT - 2:
                        follower.tensor_tail(pe, k - (OUT - 2))
                    if not (first and k < 4):
                        pe.wait_ge(added, c * OUT + (k - 3))
                    for f in range(2):
                        rows = act_hi[:, 2 * parity + f, t * P:(t + 1) * P], act_lo[:, 2 * parity + f, t * P:(t + 1) * P]
                        cols = slice(half * BANK, (half + 1) * BANK)
                        last = split_product(pe, banks[4 + k % 4][:], *rows, hi[:, f, cols], lo[:, f, cols],
                                             f == 0, f == 1)
                    last.then_inc(down_done, 1)

            pe.wait_ge(norm.lo_ready, KD)
            gate_up(0, 0, True)
            gate_up(1, 1, False)

            def step(c, parity, first):
                gate_up(c * 2, 0, False)
                gate_up(c * 2 + 1, 1, False)
                down(c - 1, 1 - parity, first, down_hi, down_lo)
            chunks(pe, step)
            down(NCH - 1, (NCH - 1) % 2, False, last_down_hi, last_down_lo, follower)


class Projected:

    def __init__(self, nc, mem, ident):
        self.wait_carrier, self.carried = mem.at("na_wait_carrier", AT_SMALL + 6.8125, [P, 1]), ident[:, 0:1]
        self.c = mem.at("conv", AT_X - 0.0625, [P, MLH, T + TAPS - 1])
        self.gates = mem.at("gates", AT_X + 17, [NGATE, T])
        self.q_t = mem.at("na_qT", AT_REST, [P, PAIRS, T])
        self.k_t = mem.at("na_kT", AT_REST + 16, [P, PAIRS, T])
        self.q_hi = mem.at("na_q_hi", AT_X + 12, [P, 4, P], F32R)
        self.q_lo = mem.at("na_q_lo", AT_X + 14, [P, 4, P], F32R)
        self.k_hi = mem.at("na_k_hi", AT_H + 32, [P, PAIRS, T], F32R)
        self.k_lo = mem.at("na_k_lo", AT_REST + 16, [P, PAIRS, T], F32R)
        self.v = mem.at("v_ml", AT_REST + 32, [P, TT, MLH, MLD + 1])
        self.units = UnitVectors(mem)
        self.w_qk = mem.at("ml_w_qk", AT_REST + 68, [P, 2, MLH, MLD])
        self.w_qk_loaded = mem.semaphore("w_qk_loaded")
        dram = lambda name, shape: nc.dram_tensor(name, shape, F32, kind="Internal").ap()
        self.o_dram = dram("o_scratch", [T, MLW])
        self.v_dram = dram("v_scratch", [T, NAW])
        self.gates_dram = dram("gates_scratch", [NGATE * NC, P])
        self.m_dram = dram("m_scratch", [U, P])
        self.pad_dram = dram("rpb_scratch", [NAH * NDR, 2 * GRID_W - 1])


    def high_keys(self, a, p, done):
        a.activation(self.k_hi[:, p], self.k_t[:, p], ACT.Copy).then_inc(done, 1)

    def low_keys(self, dve, p, done):
        dve.tensor_tensor(self.k_lo[:, p], self.k_t[:, p], self.k_hi[:, p].bitcast(F32), ALU.subtract).then_inc(done, 1)

    def copy_queries(self, pool, p, r, high, highs, done):
        blocks = []
        for h in range(2):
            rows = slice(h * NAD, (h + 1) * NAD)
            blocks.append((self.q_t[rows, p, r * GRID_W:(r + 1) * GRID_W],
                           *(part[rows, r % 4, h * GRID_W:(h + 1) * GRID_W] for part in (self.q_hi, self.q_lo))))
        for q, hi, lo in blocks:
            pool.tensor_copy(hi, q).then_inc(high, 1)
        pool.wait_ge(high, highs + 2)
        pool.tensor_tensor(self.wait_carrier[0:NAD], self.carried[0:NAD], self.carried[0:NAD], ALU.subtract)
        for q, hi, lo in blocks:
            pool.tensor_tensor(lo, q, hi.bitcast(F32), ALU.subtract).then_inc(done, 1)


class UnitVectors:

    def __init__(self, mem):
        names = "li f z M ones m0_rows decay_rows neg_abs expf lnf lf b runmax m floor weights".split()
        places = [AT_X + 29 + 0.5 * i for i in range(6)] + [AT_REST + 48.25 + 0.5 * i for i in range(10)]
        self.row = {n: mem.at(f"ml_{n}", at, [U, P]) for n, at in zip(names, places)}
        self.col = {n: mem.at(f"ml_{n}", AT_REST + 53.5 + 0.0625 * i, [U, 1])
                    for i, n in enumerate("g mloc m0 end neg_end decay".split())}
        self.line = mem.at("ml_line", AT_REST + 54, [1, 4, U])
        self.one = mem.at("ml_one", AT_REST + 55, [1, 1])
        self.cols = mem.at("ml_unit_cols", AT_SMALL + 1, [P, 5, U])
        sem = lambda s: mem.semaphore(f"ml_{s}")
        self.chain = sem("chain")
        self.chain_steps = 0
        (self.loaded, self.ones_ready, self.abs_ready, self.exp_ready, self.one_plus_ready, self.ln_ready,
         self.ends_ready, self.ends_turned, self.m0_line_ready, self.m0_turned, self.m_ready, self.vectors_ready,
         self.exps_ready, self.rows_ready, self.cols_turned, self.cols_ready) = (sem(s) for s in (
             "units_loaded ones abs exp one_plus ln ends_ready ends_turned m0_line_ready m0_turned m_ready "
             "unit_vectors_ready exps rows cols_turned cols_ready").split())

    def step(self, dve, instruction):
        self.chain_steps += 1
        instruction.then_inc(self.chain, 1)
        dve.wait_ge(self.chain, self.chain_steps)


    def vector_to_ends(self, dve):
        row, col, step = self.row, self.col, self.step
        dve.wait_ge(self.loaded, 64)
        dve.wait_ge(self.ones_ready, 3)
        dve.scalar_tensor_tensor(out=row["neg_abs"][:], in0=row["f"][:], scalar=-1.0, in1=row["f"][:],
                                 op0=ALU.mult, op1=ALU.min).then_inc(self.abs_ready, 1)
        dve.wait_ge(self.exp_ready, 1)
        dve.tensor_scalar(row["expf"][:], row["expf"][:], 1.0, None, ALU.add).then_inc(self.one_plus_ready, 1)
        dve.wait_ge(self.ln_ready, 1)
        step(dve, dve.scalar_tensor_tensor(out=row["lf"][:], in0=row["f"][:], scalar=0.0, in1=row["lnf"][:],
                                           op0=ALU.min, op1=ALU.subtract))
        ones, lf, b, z, runmax = (row[n] for n in ("ones", "lf", "b", "z", "runmax"))
        step(dve, dve.tensor_tensor_scan(b[FWD], ones[FWD], lf[FWD], 0.0, ALU.mult, ALU.add))
        step(dve, dve.tensor_tensor_scan(b[BWD, ::-1], ones[BWD], lf[BWD, ::-1], 0.0, ALU.mult, ALU.add))
        step(dve, dve.tensor_tensor(z[:], row["li"][:], b[:], ALU.subtract))
        step(dve, dve.tensor_tensor_scan(runmax[FWD], ones[FWD], z[FWD], LOWEST, ALU.mult, ALU.max))
        step(dve, dve.tensor_tensor_scan(runmax[BWD, ::-1], ones[BWD], z[BWD, ::-1], LOWEST, ALU.mult, ALU.max))
        for part, last in ((FWD, slice(P - 1, P)), (BWD, slice(0, 1))):
            step(dve, dve.tensor_copy(col["g"][part], b[part, last]))
            dve.tensor_tensor(col["mloc"][part], b[part, last], runmax[part, last], ALU.add).then_inc(self.ends_ready, 1)

    def vector_to_m0(self, dve, bank):
        line, step = self.line, self.step
        dve.wait_ge(self.ends_turned, 1)
        step(dve, dve.tensor_copy(line[:, 0:2], bank[0:1, 0:2 * U].rearrange("p (a u) -> p a u", a=2)))
        for d in range(2):
            for h in range(MLH):
                first = d * UD + h * NC
                g, mloc, m = (line[:, i, first:first + NC] for i in range(3))
                if d:
                    g, mloc, m = g[:, ::-1], mloc[:, ::-1], m[:, ::-1]
                step(dve, dve.tensor_tensor_scan(m, g, mloc, 0.0, ALU.add, ALU.max))
        by_head = lambda i, d: line[:, i, d * UD:(d + 1) * UD].rearrange("p (h c) -> p h c", h=MLH)
        step(dve, dve.tensor_copy(by_head(3, 0)[:, :, 1:NC], by_head(2, 0)[:, :, 0:NC - 1]))
        dve.tensor_copy(by_head(3, 1)[:, :, 0:NC - 1], by_head(2, 1)[:, :, 1:NC]).then_inc(self.m0_line_ready, 1)

    def vector_to_m(self, dve, bank):
        row, col, step = self.row, self.col, self.step
        dve.wait_ge(self.m0_turned, 1)
        step(dve, dve.tensor_copy(col["m0"][:], bank[0:U, 0:1]))
        dve.tensor_scalar(row["M"][:], row["runmax"][:], col["m0"][:], None, ALU.max).then_inc(self.m_ready, 1)
        dve.wait_ge(self.m_ready, 1)
        step(dve, dve.tensor_tensor(row["m"][:], row["b"][:], row["M"][:], ALU.add))
        for part, last in ((FWD, slice(P - 1, P)), (BWD, slice(0, 1))):
            dve.tensor_scalar(col["neg_end"][part], row["M"][part, last], -1.0, None, ALU.mult)\
               .then_inc(self.vectors_ready, 1)
        dve.tensor_scalar(row["m0_rows"][:], row["ones"][:], col["m0"][:], None, ALU.mult).then_inc(self.rows_ready, 1)

    def vector_decay(self, dve):
        dve.wait_ge(self.exps_ready, 3)
        dve.tensor_scalar(self.row["decay_rows"][:], self.row["ones"][:], self.col["decay"][:], None, ALU.mult)\
           .then_inc(self.rows_ready, 1)

    def vector_cols(self, dve, bank):
        dve.wait_ge(self.cols_turned, 1)
        dve.tensor_copy(self.cols[:].rearrange("p a u -> p (a u)"), bank[:, 0:5 * U]).then_inc(self.cols_ready, 1)


    def scalar_log(self, a):
        a.wait_ge(self.abs_ready, 1)
        a.activation(self.row["expf"][:], self.row["neg_abs"][:], ACT.Exp).then_inc(self.exp_ready, 1)
        a.wait_ge(self.one_plus_ready, 1)
        a.activation(self.row["lnf"][:], self.row["expf"][:], ACT.Ln).then_inc(self.ln_ready, 1)

    def scalar_exps(self, a):
        row, neg_end = self.row, self.col["neg_end"]
        a.wait_ge(self.vectors_ready, 2)
        a.activation(row["floor"][:], row["m"][:], ACT.Exp, scale=-1.0).then_inc(self.exps_ready, 1)
        a.activation(row["weights"][:], row["z"][:], ACT.Exp, bias=neg_end[:]).then_inc(self.exps_ready, 1)
        a.activation(self.col["decay"][:], self.col["m0"][:], ACT.Exp, bias=neg_end[:]).then_inc(self.exps_ready, 1)


    def tensor_ends(self, pe, bank, ident):
        pe.wait_ge(self.ends_ready, 2)
        pe.matmul(bank[0:1, 0:U], self.col["g"][:], ident[0:U, 0:U], start=True, stop=True)
        pe.matmul(bank[0:1, U:2 * U], self.col["mloc"][:], ident[0:U, 0:U], start=True, stop=True)\
          .then_inc(self.ends_turned, 1)

    def tensor_m0(self, pe, bank):
        pe.wait_ge(self.m0_line_ready, 1)
        pe.matmul(bank[0:U, 0:1], self.line[:, 3, :], self.one[:], start=True, stop=True).then_inc(self.m0_turned, 1)

    def tensor_cols(self, pe, bank, ident):
        pe.wait_ge(self.rows_ready, 2)
        for i, name in enumerate(("z", "weights", "floor")):
            pe.transpose(bank[:, i * U:(i + 1) * U], self.row[name][:], ident[0:U, 0:U])
        for i, name in ((3, "m0_rows"), (4, "decay_rows")):
            last = pe.matmul(bank[:, i * U:(i + 1) * U], self.row[name][:], ident[0:U, 0:U], start=True, stop=True)
        last.then_inc(self.cols_turned, 1)


class Projection:

    def __init__(self, nc, mem, x, gain, w_in, ident, banks):
        self.norm = Norm(nc, mem, "mix", x, gain, ident, banks)
        self.raw = mem.at("proj_raw", AT_REST + 56, [P, KD, BANK])
        self.w_v = w_in.rearrange("o (k p) c -> p (o k) c", p=P)
        self.raw_gates = mem.at("proj_raw_gates", AT_X + 25, [P, KD, P])
        self.gates_loaded = mem.semaphore("proj_gates_loaded")
        self.raw_loaded = [mem.semaphore(f"proj_raw_loaded{k}") for k in range(KD)]
        self.w_hi = mem.at("proj_w_hi", AT_W, [P, KD, BANK], F32R)
        self.w_lo = mem.at("proj_w_lo", AT_W + 16, [P, KD, BANK], F32R)
        self.hi_ready = mem.semaphore("proj_hi_ready")
        self.w_split = mem.semaphore("proj_w_split")

    def load(self, sp, kd, col):
        sp.dma_start(self.raw[:, kd], self.w_v[:, kd, col:col + BANK]).then_inc(self.raw_loaded[kd], 16)

    def prefetch(self, sp):
        for kd in range(KD):
            self.load(sp, kd, 0)

    def raw_of(self, s):
        return self.raw_gates if s == 1 else self.raw

    def high_part(self, a, s, kd, width):
        if s == 1:
            a.wait_ge(self.gates_loaded, 16)
        else:
            a.wait_ge(self.raw_loaded[kd], 16 * max(s, 1))
        a.activation(self.w_hi[:, kd, 0:width], self.raw_of(s)[:, kd, 0:width], ACT.Copy).then_inc(self.hi_ready, 1)

    def low_part(self, dve, s, kd, width):
        dve.wait_ge(self.hi_ready, KD * s + kd + 1)
        dve.tensor_tensor(self.w_lo[:, kd, 0:width], self.raw_of(s)[:, kd, 0:width], self.w_hi[:, kd, 0:width].bitcast(F32),
                          ALU.subtract).then_inc(self.w_split, 1)


    def scalar_head(self, a):
        for kd in range(KD):
            self.high_part(a, 0, kd, BANK)

    def vector_head(self, dve):
        for kd in range(KD // 2):
            self.low_part(dve, 0, kd, BANK)

    def vector_rest(self, dve):
        for kd in range(KD // 2, KD):
            self.low_part(dve, 0, kd, BANK)


def project(nc, mem, projection, x_stored, b_gates, conv_w, conv_b, w_q, w_k, gq, gk, rpb, ident, banks):
    sem = lambda s: mem.semaphore(f"proj_{s}")
    norm = projection.norm
    out = Projected(nc, mem, ident)
    units = out.units
    w_hi, w_lo, w_split = projection.w_hi, projection.w_lo, projection.w_split
    bias = mem.at("gate_bias", AT_SMALL + 0.9375, [NGATE, 1])
    stage = [mem.at("stage_a", AT_X + 21, [P, 4, BANK]), mem.at("stage_b", AT_REST + 32, [P, 4, BANK])]
    conv = mem.at("conv_sum", AT_REST + 40, [P, 2, T])
    taps = mem.at("conv_taps", AT_REST + 55.125, [P, MLH, TAPS])
    conv_bias = mem.at("conv_bias", AT_REST + 55.25, [P, MLH])
    gains = mem.at("na_gains", AT_SMALL + 4.75, [P, 2])
    gain_q = mem.at("na_gain_q", AT_SMALL + 4.8125, [P, 1])
    squares = mem.at("na_squares", AT_SMALL + 4.875, [P, NAW])
    sumsq, meansq, root, rstd = (mem.at(f"na_{n}", AT_SMALL + 2.5 + 0.125 * i, [P, 4, NAH])
                                 for i, n in enumerate("sumsq meansq root rstd".split()))
    pad = mem.at("na_pad", AT_SMALL + 3.5, [NAH * NDR, 2 * GRID_W - 1])

    gate_col = 3 * MLW
    C_IN, GATES, Q_NA, K_NA, V_NA, O_ML, V_ML = range(7)
    slabs = [(0, BANK), (gate_col, P)] + [(gate_col + NGATE + NAW * n, BANK) for n in range(3)]
    slabs += [(2 * MLW, BANK), (MLW, BANK)]

    bias_loaded, taps_loaded, gains_loaded = sem("bias_loaded"), sem("taps_loaded"), sem("gains_loaded")
    piece_used = sem("piece_used")
    tile_done = sem("tile_done")
    read_out = [sem("even_read"), sem("odd_read")]
    odd_sigmoid = sem("odd_sigmoid")
    padded = sem("padded")
    stage_stored = [sem(f"stage_stored{k}") for k in range(4)]
    conv_ready, u_ready = sem("conv_ready"), sem("u_ready")
    gates_stored, m_stored = sem("gates_stored"), sem("m_stored")
    pad_zeroed, pad_loaded, pad_stored = sem("pad_zeroed"), sem("pad_loaded"), sem("pad_stored")
    gain_scaled = sem("gain_scaled")
    squared, summed, normed = sem("na_squared"), sem("na_summed"), sem("na_normed")
    mean_ready, root_ready, rstd_ready = sem("na_mean"), sem("na_root"), sem("na_rstd")
    turned, qk_ready = sem("na_turned"), sem("na_qk_ready")
    MT = 8

    first_tile = lambda s: 0 if s == C_IN else 8 if s == GATES else 10 + MT * (s - 2)
    reads_through = lambda s, t: (t // 2 if s == C_IN else 4 if s == GATES else 5 + 4 * (s - 2) + t // 2) + 1

    def wait_read(eng, s, t):
        eng.wait_ge(read_out[t % 2], reads_through(s, t))

    def destination(s, t):
        if s == C_IN:
            half, m = divmod(t, MLH)
            return out.c[:, m, 2 + half * BANK:2 + (half + 1) * BANK]
        if s == V_ML:
            return out.v[:, t, :, 0:MLD]
        if s in (Q_NA, K_NA):
            return stage[t // 4][:, t % 4]
        return stage[0][:, t % 4]

    def source(s, t):
        b = banks[t if s == C_IN else t % 4][:]
        return b.rearrange("p (h d) -> p h d", h=MLH) if s == V_ML else b

    def wait_destination(eng, s, t):
        if s == K_NA:
            eng.wait_ge(turned, 4 * (t // 4 + 1))
        elif s == V_NA and t < 4:
            eng.wait_ge(turned, 12)
        elif s in (V_NA, O_ML):
            eng.wait_ge(stage_stored[t % 4], 16 * (t // 4 if s == V_NA else 2 + t // 4))
        elif s == V_ML and t < 2:
            eng.wait_ge(turned, 16)
            eng.wait_ge(u_ready, MLH)

    with nc.Block() as block:
        @block.sync
        def _(sp):
            with nc.allow_non_contiguous_dma(reason="values per partition"):
                sp.dma_start(bias[:], b_gates.rearrange("o g -> g o")).then_inc(bias_loaded, 16)
                for h in range(MLH):
                    sp.dma_start(taps[:, h], conv_w[0, :, h * P:(h + 1) * P].rearrange("j p -> p j"))\
                      .then_inc(taps_loaded, 16)
                sp.dma_start(conv_bias[:], conv_b.rearrange("o (h p) -> p (o h)", p=P)).then_inc(taps_loaded, 16)
                for h in range(2):
                    for n, g in enumerate((gq, gk)):
                        sp.dma_start(gains[h * NAD:(h + 1) * NAD, n:n + 1], g.rearrange("o d -> d o"))\
                          .then_inc(gains_loaded, 16)
            for s in range(Q_NA, len(slabs)):
                split_before = KD * (0 if s == Q_NA else s - 1)
                for kd in range(KD):
                    sp.wait_ge(w_split, split_before + kd + 1)
                    projection.load(sp, kd, slabs[s][0])
                if s == Q_NA:
                    sp.wait_ge(x_stored, 16 * TT)
                    sp.wait_ge(norm.scaled_ready, TT)
                    sp.dma_start(projection.raw_gates[:], projection.w_v[:, :, gate_col:gate_col + P])\
                      .then_inc(projection.gates_loaded, 16)
            sp.wait_ge(w_split, KD * len(slabs))
            for n, w in enumerate((w_q, w_k)):
                sp.dma_start(out.w_qk[:, n], w.rearrange("o h d e -> d (o h) e")).then_inc(out.w_qk_loaded, 16)

        @block.gpsimd
        def _(pool):
            pool.memset(pad[:], 0.0).then_inc(pad_zeroed, 1)
            pool.wait_ge(pad_zeroed, 1)
            pool.dma_start(pad[:, GRID_W - WIN_W:GRID_W - WIN_W + NDC], rpb.rearrange("o h r c -> (o h r) c"))\
                .then_inc(pad_loaded, 16)
            pool.wait_ge(pad_loaded, 16)
            pool.dma_start(out.pad_dram, pad[:]).then_inc(pad_stored, 16)
            pool.wait_ge(x_stored, 16 * TT)
            pool.wait_ge(norm.lo_ready, HALVES * KD)
            pool.memset(out.c[:, :, 0:2], 0.0).then_inc(padded, 1)
            pool.memset(out.c[:, :, T + 2:T + 4], 0.0).then_inc(padded, 1)
            pool.memset(units.row["ones"][:], 1.0).then_inc(units.ones_ready, 1)
            pool.memset(units.one[:], 1.0).then_inc(units.ones_ready, 1)
            pool.memset(units.line[:], 0.0).then_inc(units.ones_ready, 1)
            wait_read(pool, GATES, 0)
            wait_read(pool, GATES, 1)
            pool.dma_start(out.gates_dram.rearrange("(g c) l -> g (c l)", g=NGATE), out.gates[:]).then_inc(gates_stored, 16)
            pool.wait_ge(gates_stored, 16)
            for d in range(2):
                for n, name in enumerate(("li", "f")):
                    first = (2 * d + n) * UD
                    pool.dma_start(units.row[name][d * UD:(d + 1) * UD, :], out.gates_dram[first:first + UD, :])\
                        .then_inc(units.loaded, 16)
            for s, dram in ((V_NA, out.v_dram), (O_ML, out.o_dram)):
                for t in range(TT):
                    if s == O_ML and t % 2:
                        pool.wait_ge(odd_sigmoid, t // 2 + 1)
                    else:
                        wait_read(pool, s, t)
                    pool.dma_start(dram[t * P:(t + 1) * P, :], stage[0][:, t % 4, :]).then_inc(stage_stored[t % 4], 16)
            pool.wait_ge(u_ready, MLH)
            pool.wait_ge(turned, 16)
            pool.memset(out.v[:, :, :, MLD:MLD + 1], 1.0).then_inc(padded, 1)
            pool.wait_ge(units.m_ready, 1)
            pool.dma_start(out.m_dram, units.row["M"][:]).then_inc(m_stored, 16)
            for k in range(4):
                pool.wait_ge(stage_stored[k], 16 * 4)
            pool.wait_ge(padded, 3)
            pool.wait_ge(pad_stored, 16)
            pool.wait_ge(m_stored, 16)

        @block.scalar
        def _(a):
            def split(s):
                for kd in range(KD):
                    if kd < KD - 1:
                        a.wait_ge(piece_used, (KD - 1) * (s - 1) + kd + 1)
                    else:
                        a.wait_ge(tile_done, first_tile(s))
                    projection.high_part(a, s, kd, slabs[s][1])

            def read(s, t, func=ACT.Copy):
                a.wait_ge(tile_done, first_tile(s) + t + 1)
                wait_destination(a, s, t)
                a.activation(destination(s, t), source(s, t), func).then_inc(read_out[t % 2], 1)

            def squares_of(batch):
                w, half = divmod(batch, 2)
                for j in range(4):
                    n = 4 * batch + j
                    if n:
                        a.wait_ge(summed, n)
                    wait_read(a, Q_NA + w, 4 * half + j)
                    a.activation(squares[:], stage[half][:, j], ACT.Square).then_inc(squared, 1)
                a.wait_ge(mean_ready, batch + 1)
                a.activation(root[:], meansq[:], ACT.Sqrt).then_inc(root_ready, 1)

            def read_turned(batch):
                w, half = divmod(batch, 2)
                a.wait_ge(gain_scaled, 1)
                for pair in range(PAIRS):
                    a.wait_ge(turned, 4 * batch + pair + 1)
                    to, turn = (out.q_t, out.k_t)[w][:, pair, half * BANK:(half + 1) * BANK], banks[4 + pair][:]
                    if w == 0:
                        to = to.rearrange("d (r q) -> d r q", q=GRID_W)
                        turn = turn.rearrange("d (r q) -> d r q", q=GRID_W)[:, :, ::-1]
                    a.activation(to, turn, ACT.Copy, scale=(gains[:, 1:2] if w else gain_q[:])).then_inc(qk_ready, 1)

            def silu(h):
                a.wait_ge(conv_ready, h + 1)
                a.activation(out.c[:, h, 2:T + 2], conv[:, h % 2], ACT.Silu).then_inc(u_ready, 1)

            norm.squares(a, 1, lambda eng, t: None)
            a.wait_ge(x_stored, 16 * TT)
            read(C_IN, 0)
            read(C_IN, 2)
            norm.hi_parts(a, 1)
            read(C_IN, 4)
            split(GATES)
            read(C_IN, 6)
            split(Q_NA)
            a.wait_ge(tile_done, first_tile(GATES) + 1)
            a.wait_ge(bias_loaded, 16)
            a.activation(out.gates[:, 0:BANK], banks[4][0:NGATE, :], ACT.Identity, bias=bias[:]).then_inc(read_out[0], 1)
            a.wait_ge(gains_loaded, 64)
            read(Q_NA, 0)
            read(Q_NA, 2)
            silu(0)
            squares_of(0)
            read(Q_NA, 4)
            read(Q_NA, 6)
            read_turned(0)
            split(K_NA)
            silu(1)
            squares_of(1)
            read(K_NA, 0)
            read(K_NA, 2)
            read_turned(1)
            silu(2)
            squares_of(2)
            read(K_NA, 4)
            read(K_NA, 6)
            read_turned(2)
            split(V_NA)
            squares_of(3)
            read(V_NA, 0)
            read(V_NA, 2)
            read_turned(3)
            silu(3)
            units.scalar_log(a)
            read(V_NA, 4)
            read(V_NA, 6)
            split(O_ML)
            for t in range(MT):
                if t % 2 == 0:
                    if t == MT - 2:
                        split(V_ML)
                    read(O_ML, t, ACT.Sigmoid)
                else:
                    wait_read(a, O_ML, t)
                    a.activation(stage[0][:, t % 4], stage[0][:, t % 4], ACT.Sigmoid).then_inc(odd_sigmoid, 1)
                if t == 1:
                    units.scalar_exps(a)
            for t in range(0, MT, 2):
                read(V_ML, t)

        @block.vector
        def _(dve):
            def split(s):
                for kd in range(KD):
                    projection.low_part(dve, s, kd, slabs[s][1])

            def read(s, t):
                dve.wait_ge(tile_done, first_tile(s) + t + 1)
                wait_destination(dve, s, t)
                dve.tensor_copy(destination(s, t), source(s, t)).then_inc(read_out[t % 2], 1)

            def convolve(h):
                acc = conv[:, h % 2]
                if h >= 2:
                    dve.wait_ge(u_ready, h - 1)
                units.step(dve, dve.tensor_scalar(acc, out.c[:, h, 0:T], taps[:, h, 0:1], conv_bias[:, h:h + 1],
                                                  ALU.mult, ALU.add))
                for j in range(1, TAPS):
                    tap = dve.scalar_tensor_tensor(out=acc, in0=out.c[:, h, j:j + T], scalar=taps[:, h, j:j + 1],
                                                   in1=acc, op0=ALU.mult, op1=ALU.add)
                    if j < TAPS - 1:
                        units.step(dve, tap)
                tap.then_inc(conv_ready, 1)

            def norm_of(batch):
                half = batch % 2
                for j in range(4):
                    dve.wait_ge(squared, 4 * batch + j + 1)
                    dve.tensor_reduce(sumsq[:, j], squares[:].rearrange("p (h d) -> p h d", d=NAD), AX.X, ALU.add)\
                       .then_inc(summed, 1)
                dve.wait_ge(summed, 4 * batch + 4)
                dve.tensor_scalar(meansq[:], sumsq[:], 1.0 / NAD, EPS, ALU.mult, ALU.add).then_inc(mean_ready, 1)
                dve.wait_ge(root_ready, batch + 1)
                dve.reciprocal(rstd[:], root[:]).then_inc(rstd_ready, 1)
                dve.wait_ge(rstd_ready, batch + 1)
                for j in range(4):
                    tile = stage[half][:, j].rearrange("p (h d) -> p h d", d=NAD)
                    dve.tensor_tensor(tile, tile, rstd[:, j].unsqueeze(2).to_broadcast([P, NAH, NAD]), ALU.mult)\
                       .then_inc(normed, 1)

            projection.vector_rest(dve)
            norm.mean(dve, 1)
            for t in range(4, TT):
                norm.scale(dve, t)
            dve.wait_ge(x_stored, 16 * TT)
            read(C_IN, 1)
            norm.lo_parts(dve, 1)
            read(C_IN, 3)
            read(C_IN, 5)
            split(GATES)
            read(C_IN, 7)
            split(Q_NA)
            dve.wait_ge(tile_done, first_tile(GATES) + 2)
            dve.wait_ge(bias_loaded, 16)
            dve.tensor_scalar(out.gates[:, BANK:T], banks[5][0:NGATE, :], bias[:], None, ALU.add).then_inc(read_out[1], 1)
            dve.wait_ge(gains_loaded, 64)
            dve.tensor_scalar(gain_q[:], gains[:, 0:1], NAD ** -0.5, None, ALU.mult).then_inc(gain_scaled, 1)
            read(Q_NA, 1)
            dve.wait_ge(taps_loaded, 16 * (MLH + 1))
            dve.wait_ge(padded, 2)
            wait_read(dve, C_IN, 6)
            wait_read(dve, C_IN, 7)
            convolve(0)
            read(Q_NA, 3)
            norm_of(0)
            read(Q_NA, 5)
            convolve(1)
            split(K_NA)
            read(Q_NA, 7)
            norm_of(1)
            read(K_NA, 1)
            convolve(2)
            read(K_NA, 3)
            norm_of(2)
            read(K_NA, 5)
            split(V_NA)
            read(K_NA, 7)
            norm_of(3)
            read(V_NA, 1)
            convolve(3)
            read(V_NA, 3)
            units.vector_to_ends(dve)
            read(V_NA, 5)
            units.vector_to_m0(dve, banks[4])
            split(O_ML)
            read(V_NA, 7)
            units.vector_to_m(dve, banks[5])
            read(O_ML, 1)
            units.vector_decay(dve)
            read(O_ML, 3)
            read(O_ML, 5)
            split(V_ML)
            read(O_ML, 7)
            for t in range(1, MT, 2):
                read(V_ML, t)
            units.vector_cols(dve, banks[6])

        @block.tensor
        def _(pe):
            cols = [slice(half * BANK, (half + 1) * BANK) for half in range(HALVES)]
            pe.wait_ge(norm.lo_ready, KD)
            for t in range(MT):
                half, m = divmod(t, MLH)
                if t == MLH:
                    pe.wait_ge(norm.lo_ready, HALVES * KD)
                for kd in range(KD):
                    if t == 0:
                        pe.wait_ge(w_split, kd + 1)
                    if t == MLH - 1 and kd in (3, 6):
                        norm.transposes(pe, 1, kd // 4)
                    last = split_product(pe, banks[t][:], w_hi[:, kd, m * P:(m + 1) * P], w_lo[:, kd, m * P:(m + 1) * P],
                                         norm.h_hi[:, kd, cols[half]], norm.h_lo[:, kd, cols[half]],
                                         kd == 0, kd == KD - 1)
                    if t == MT - 1 and kd < KD - 1:
                        last.then_inc(piece_used, 1)
                last.then_inc(tile_done, 1)
            for half in range(HALVES):
                wait_read(pe, C_IN, 4 + half)
                for kd in range(KD):
                    if half == 0:
                        pe.wait_ge(w_split, KD + kd + 1)
                    last = split_product(pe, banks[4 + half][:], w_hi[:, kd, 0:P], w_lo[:, kd, 0:P],
                                         norm.h_hi[:, kd, cols[half]], norm.h_lo[:, kd, cols[half]],
                                         kd == 0, kd == KD - 1)
                    if half and kd < KD - 1:
                        last.then_inc(piece_used, 1)
                last.then_inc(tile_done, 1)

            def token_slab(n, after):
                for t in range(TT):
                    pe.wait_ge(read_out[t % 2], n * 4 + (t // 2 + 4))
                    for kd in range(KD):
                        if t == 0:
                            pe.wait_ge(w_split, n * KD + (2 * KD + kd + 1))
                        rows = slice(t * P, (t + 1) * P)
                        last = split_product(pe, banks[t % 4][:], norm.h_hi[:, kd, rows], norm.h_lo[:, kd, rows],
                                             w_hi[:, kd, :], w_lo[:, kd, :], kd == 0, kd == KD - 1)
                        if t == TT - 1 and kd < KD - 1:
                            last.then_inc(piece_used, 1)
                    last.then_inc(tile_done, 1)
                    if t in after:
                        after[t]()

            def turn(batch):
                half = batch % 2
                pe.wait_ge(normed, 4 * batch + 4)
                if batch == 0:
                    wait_read(pe, C_IN, 6)
                    wait_read(pe, C_IN, 7)
                    wait_read(pe, GATES, 0)
                    wait_read(pe, GATES, 1)
                if batch:
                    pe.wait_ge(qk_ready, 4 * batch)
                for pair in range(PAIRS):
                    for j in range(4):
                        last = pe.transpose(banks[4 + pair][:, j * P:(j + 1) * P],
                                            stage[half][:, j, pair * P:(pair + 1) * P], ident[:])
                    last.then_inc(turned, 1)

            def ends():
                pe.wait_ge(qk_ready, 16)
                units.tensor_ends(pe, banks[4], ident)

            token_slab(0, {6: lambda: turn(0)})
            token_slab(1, {2: lambda: turn(1), 6: lambda: turn(2)})
            token_slab(2, {2: lambda: turn(3), 5: ends, 7: lambda: units.tensor_m0(pe, banks[5])})
            with pe.Fori(3, 5) as n:
                token_slab(n, {})
            units.tensor_cols(pe, banks[6], ident)
    return out


def attend(nc, mem, pr, bias, window, head_norm, ident, banks, prefetch):
    sem = lambda s: mem.semaphore(f"na_{s}")
    k_hi, k_lo = pr.k_hi, pr.k_lo
    y_hi = mem.at("na_y_hi", AT_H + 16, [P, PAIRS, T], F32R)
    y_lo = mem.at("na_y_lo", AT_H + 48, [P, PAIRS, T], F32R)
    v_pair = mem.at("na_v_pair", AT_X, [P, 2 * TT - 1, P])
    negs = mem.at("na_negs", AT_W + 24, [P, 4, BANK])
    probs = mem.at("na_probs", AT_X + 16, [P, 4, BANK])
    probs_t = mem.at("na_probsT", AT_X + 24, [P, 4, BANK])
    bias_pair = mem.at("na_bias_pair", AT_W + 16, [P, NDR, GRID_W])
    neg_max = mem.at("na_neg_max", AT_SMALL + 3.5, [P, 4])
    row_sum = mem.at("na_row_sum", AT_SMALL + 3.5625, [P, 4])
    inv_sum = mem.at("na_inv_sum", AT_SMALL + 3.625, [P, 4])
    v_even = pr.v_dram.rearrange("(t p) c -> p t c", p=P)
    v_odd = pr.v_dram[GRID_W:T - GRID_W, :].rearrange("(t p) c -> p t c", p=P)

    bias_ready = sem("bias_ready")
    k_high, k_split = sem("k_high"), sem("k_split")
    diag_high, diag_ready = sem("diag_high"), sem("diag_ready")
    v_first = sem("v_first")
    v_rest = sem("v_rest")
    scores_ready = sem("scores_ready")
    negs_ready = sem("negs_ready")
    probs_ready = sem("probs_ready")
    inv_ready = sem("inv_ready")
    probs_scaled = sem("probs_scaled")
    probs_turned = sem("probs_turned")
    probs_t_ready = sem("probs_t_ready")
    out_ready = sem("out_ready")
    out_high = sem("out_high")
    out_read = sem("out_read")

    row_start = [min(max(r - WIN_H // 2, 0), GRID_H - WIN_H) for r in range(GRID_H)]
    R = GRID_H
    GROUPS = R // 4

    def group_of(p, g, h):
        rows, cols = slice(h * NAD, (h + 1) * NAD), slice(g * 4 * GRID_W, (g + 1) * 4 * GRID_W)
        grid = lambda ap: ap.rearrange("d (r q) -> d r q", r=4)
        return (grid(banks[6 + g % 2][rows, :])[:, :, h * GRID_W:(h + 1) * GRID_W][:, :, ::-1],
                grid(y_hi[rows, p, cols]), grid(y_lo[rows, p, cols]))

    def pairs(eng, pair):
        pair(0, True)
        with eng.Fori(1, PAIRS) as p:
            pair(p, False)

    def rows(eng, *stages):
        def pair(p, first, last):
            for i in range(R):
                for ahead, work in stages:
                    if i + ahead < R:
                        work(p, i + ahead, first, last)
                    elif not last:
                        work(p + 1, i + ahead - R, False, False)
        for i in range(-max(ahead for ahead, work in stages), 0):
            for ahead, work in stages:
                if i + ahead >= 0:
                    work(0, i + ahead, True, False)
        pair(0, True, False)
        with eng.Fori(1, PAIRS - 1) as p:
            pair(p, False, False)
        pair(PAIRS - 1, False, True)

    with nc.Block() as block:
        @block.sync
        def _(sp):
            def pair(p, first):
                cols = bass.ds(p * P, P)
                if not first:
                    sp.wait_ge(out_ready, p * GROUPS - 1)
                sp.dma_start(v_pair[:, 0:TT // 2], v_even[:, 0:TT // 2, cols]).then_inc(v_first, 16)
                sp.dma_start(v_pair[:, TT:], v_odd[:, :, cols]).then_inc(v_first, 16)
                if not first:
                    sp.wait_ge(out_ready, p * GROUPS)
                sp.dma_start(v_pair[:, TT // 2:TT], v_even[:, TT // 2:, cols]).then_inc(v_rest, 16)
                if first:
                    head_norm.load(sp)
                    prefetch(sp)
            pairs(sp, pair)

        @block.gpsimd
        def _(pool):
            def pair(p, first):
                for r in range(EARLY if first else 0, R):
                    pool.wait_ge(scores_ready, p * R + (r - 3))
                    pr.copy_queries(pool, p, r, diag_high, p * (2 * R) + 2 * (r - EARLY), diag_ready)
                    if r == (13 if first else 2):
                        pool.wait_ge(diag_ready, p * (2 * R) + (2 * (r - EARLY) + 2))
                        if first:
                            pool.wait_ge(head_norm.gn_loaded, 16)
                            pool.wait_ge(head_norm.o_loaded, 16)
                        head_norm.gain(pool, p)
                        pool.wait_ge(head_norm.gained, p + 1)
            pairs(pool, pair)

        @block.scalar
        def _(a):
            def exponentials(p, r, first, last):
                if first and 0 < r < PAIRS:
                    pr.high_keys(a, r, k_high)
                a.wait_ge(negs_ready, p * R + (r + 1))
                if not (first and r < 4):
                    a.wait_ge(probs_turned, p * R + (r - 3))
                a.activation(probs[:, r % 4], negs[:, r % 4], ACT.Exp, scale=-1.0, bias=neg_max[:, r % 4:r % 4 + 1],
                             accum_out=row_sum[:, r % 4:r % 4 + 1]).then_inc(probs_ready, 1)

            def read_turned(p, r, first, last):
                a.wait_ge(probs_turned, p * R + (r + 1))
                a.activation(probs_t[:, r % 4], banks[4 + r % 2][:], ACT.Copy).then_inc(probs_t_ready, 1)

            def high_parts(p, r, first, last):
                if r % 4 == 3:
                    a.wait_ge(out_ready, p * GROUPS + (r // 4 + 1))
                    for h in range(2):
                        source, hi, lo = group_of(p, r // 4, h)
                        a.activation(hi, source, ACT.Copy).then_inc(out_high, 1)
                if first:
                    head_norm.scalar_statistics(a, r)
            rows(a, (4, exponentials), (2, read_turned), (0, high_parts))

        @block.vector
        def _(dve):
            def bias_of_pair(p, first):
                if not first:
                    dve.wait_ge(negs_ready, p * R)
                in_window = lambda rows: window[:].unsqueeze(1).to_broadcast([P, rows, GRID_W])
                dve.tensor_tensor(bias_pair[:, WIN_H - 1:], bias[:, p, WIN_H - 1:], in_window(WIN_H), ALU.add)\
                   .then_inc(bias_ready, 1)
                dve.wait_ge(bias_ready, p * 2 + 1)
                dve.wait_ge(scores_ready, p * R + 1)
                dve.tensor_tensor(bias_pair[:, 0:WIN_H - 1], bias[:, p, 0:WIN_H - 1], in_window(WIN_H - 1), ALU.add)\
                   .then_inc(bias_ready, 1)

            def negate_and_max(p, r):
                dr = row_start[r] - r + WIN_H - 1
                dve.tensor_tensor_reduce(negs[:, r % 4], banks[r % 4][:],
                                         bias_pair[:, dr:dr + WIN_H].rearrange("c r k -> c (r k)"), -1.0, 3.0e38,
                                         ALU.add, ALU.min, neg_max[:, r % 4:r % 4 + 1]).then_inc(negs_ready, 1)

            def start_normalising(n, slot):
                dve.wait_ge(probs_ready, n + 1)
                dve.reciprocal(inv_sum[:, slot:slot + 1], row_sum[:, slot:slot + 1]).then_inc(inv_ready, 1)

            def normalise(n, slot):
                dve.wait_ge(inv_ready, n + 1)
                dve.tensor_scalar(probs[:, slot], probs[:, slot], inv_sum[:, slot:slot + 1], None, ALU.mult)\
                   .then_inc(probs_scaled, 1)

            def maxima(p, r, first, last):
                if r == 0:
                    bias_of_pair(p, first)
                elif r == 1:
                    dve.wait_ge(bias_ready, p * 2 + 2)
                dve.wait_ge(scores_ready, p * R + (r + 1))
                if not (first and r == 0):
                    start_normalising(p * R + (r - 1), (r - 1) % 4)
                negate_and_max(p, r)
                if not (first and r == 0):
                    normalise(p * R + (r - 1), (r - 1) % 4)
                if first and 0 < r < PAIRS:
                    dve.wait_ge(k_high, r)
                    pr.low_keys(dve, r, k_split)
                if last and r == R - 1:
                    start_normalising(p * R + r, r % 4)
                    normalise(p * R + r, r % 4)

            def low_parts(p, r, first, last):
                if r % 4 == 3:
                    for h in range(2):
                        dve.wait_ge(out_high, p * (2 * GROUPS) + (r // 4 * 2 + h + 1))
                        source, hi, lo = group_of(p, r // 4, h)
                        dve.tensor_tensor(lo, source, hi.bitcast(F32), ALU.subtract).then_inc(out_read, 1)
                if first:
                    head_norm.vector_statistics(dve, r)
                elif r >= R - NC:
                    if r == R - NC:
                        dve.wait_ge(head_norm.gained, p)
                    head_norm.product(dve, p - 1, r - (R - NC))
                elif last:
                    if r == 0:
                        dve.wait_ge(head_norm.gained, MLH)
                    head_norm.product(dve, MLH - 1, r)
            rows(dve, (5, maxima), (0, low_parts))

        @block.tensor
        def _(pe):
            def scores(p, r, first, last):
                if not (first and r < EARLY):
                    pe.wait_ge(diag_ready, p * (2 * R) + (2 * (r - EARLY) + 2))
                if not (first and r < 4):
                    pe.wait_ge(negs_ready, p * R + (r - 3))
                start = row_start[r] * GRID_W
                if r == 0 and not first:
                    pe.wait_ge(k_split, p)
                keys = slice(start, start + WIN_H * GRID_W)
                split_product(pe, banks[r % 4][:], pr.q_hi[:, r % 4], pr.q_lo[:, r % 4], k_hi[:, p, keys], k_lo[:, p, keys],
                              True, True).then_inc(scores_ready, 1)

            def turn(p, r, first, last):
                pe.wait_ge(probs_scaled, p * R + (r + 1))
                if not (first and r < 2):
                    pe.wait_ge(probs_t_ready, p * R + (r - 1))
                for j in range(4):
                    done = pe.transpose(banks[4 + r % 2][:, j * P:(j + 1) * P], probs[:, r % 4, j * P:(j + 1) * P],
                                        ident[:])
                done.then_inc(probs_turned, 1)

            def values(p, r, first, last):
                g = r // 4
                pe.wait_ge(probs_t_ready, p * R + (r + 1))
                if r == 0:
                    pe.wait_ge(v_first, p * 32 + 32)
                if r == 6:
                    pe.wait_ge(v_rest, p * 16 + 16)
                if r % 4 == 0 and not (first and g < 2):
                    pe.wait_ge(out_read, p * (2 * GROUPS) + 2 * (g - 1))
                tile = row_start[r] // 2 + (TT if row_start[r] % 2 else 0)
                for j in range(4):
                    done = pe.matmul(banks[6 + g % 2][:, (r % 4) * P:(r % 4 + 1) * P], v_pair[:, tile + j],
                                     probs_t[:, r % 4, j * P:(j + 1) * P], start=(j == 0), stop=(j == 3))
                if r % 4 == 3:
                    done.then_inc(out_ready, 1)

            rows(pe, (3, scores), (1, turn), (0, values))
    return y_hi, y_lo


def mlstm(nc, mem, pr, ident, banks):
    sem = lambda s: mem.semaphore(f"ml_{s}")
    SCALE = MLD ** -0.5
    u_t = pr.c[:, :, 2:T + 2]
    z_cols, w_cols, floor_cols, m0_cols, decay_cols = (pr.units.cols[:, i] for i in range(5))
    m_all = [mem.at("ml_M_fwd", AT_H, [P, MLH, NC, P]),
             mem.at("ml_M_bwd", AT_X + 16, [P, MLH, NC, P])]
    q_t = mem.at("ml_qT", AT_H + 16, [P, MLH, T])
    k_t = mem.at("ml_kT", AT_H + 32, [P, MLH, T])
    k_tok = mem.at("ml_k", AT_H + 48, [P, NC, MLH, MLD])
    hs = mem.at("ml_h", AT_REST + 48.25, [P, NC, MLH, MLD])
    state = mem.at("ml_state", AT_REST + 64.25, [P, DIRS, MLH, MLD + 1])
    mask = mem.at("ml_mask", AT_SMALL + 2.5, [P, DIRS, P])
    ring = lambda n, at: mem.at(f"ml_{n}", at, [P, DIRS, MLH, P])
    weight, weighted, carry = (ring(n, AT_X + 4 * i) for i, n in enumerate("weight weighted carry".split()))
    q_scaled, k_chunk, k_weighted, arg = (ring(n, AT_W + 16 + 4 * i) for i, n in enumerate(
        "q_scaled k_chunk k_weighted arg".split()))
    den = mem.at("ml_den", AT_SMALL + 4, [P, DIRS, MLH])
    den_max = mem.at("ml_den_max", AT_SMALL + 4.0625, [P, DIRS, MLH])
    den_inv = mem.at("ml_den_inv", AT_SMALL + 4.125, [P, DIRS, MLH])
    bias = mem.at("na_bias", AT_W, [P, PAIRS, NDR, GRID_W])
    window = mem.at("na_window", AT_SMALL + 3.75, [P, GRID_W])

    masked, zeroed = sem("masked"), sem("zeroed")
    qk_done, q_read, k_read = sem("qk_done"), sem("q_read"), sem("k_read")
    m_loaded = sem("m_loaded")
    keys_high, keys_low = mem.semaphore("na_keys_high"), mem.semaphore("na_keys_low")
    diag_zeroed, diag_high, diag_early = (mem.semaphore(f"na_diag_{s}_early") for s in ("zeroed", "high", "ready"))
    bias_loaded = mem.semaphore("na_bias_loaded")

    k_copied, k_scaled, q_carried = sem("k_copied"), sem("k_scaled"), sem("q_carried")
    arg_ready, weight_ready, carry_ready = sem("arg_ready"), sem("weight_ready"), sem("carry_ready")
    scores_done, weighted_ready, sums_done, update_done = (
        sem(s) for s in "scores_done weighted_ready sums_done update_done".split())
    updated, den_step, h_added = sem("updated"), sem("den_step"), sem("h_added")


    def steps(eng, step):
        step(0, True, False)
        with eng.Fori(1, NC - 1) as i:
            step(i, False, False)
        step(NC - 1, False, True)

    chunk = lambda i, d: i * -1 + (NC - 1) if d else i
    following = lambda i, d: (i + d, 1 - d)
    units_of = lambda cols, c, d: cols[:, d * UD:(d + 1) * UD].rearrange("p (h c) -> p h c", h=MLH)[:, :, c]
    head_bank = lambda d, h: banks[2 + 2 * d + h // 2][:, (h % 2) * (MLD + 1):(h % 2 + 1) * (MLD + 1)]
    update_bank = lambda h: banks[6 + h // 2][:, (h % 2) * (MLD + 1):(h % 2 + 1) * (MLD + 1)]

    with nc.Block() as block:
        @block.sync
        def _(sp):
            for d in range(DIRS):
                sp.dma_start(m_all[d][:].rearrange("p h c l -> p (h c l)"),
                             pr.m_dram[d * UD:(d + 1) * UD, :].rearrange("u l -> (u l)").partition_broadcast(P))\
                  .then_inc(m_loaded, 16)
            width = 2 * GRID_W - 1
            for pair in range(PAIRS):
                for h in range(2):
                    first = (2 * pair + h) * NDR * width
                    sp.dma_start(bias[h * GRID_W:(h + 1) * GRID_W, pair],
                                 bass.AP(tensor=pr.pad_dram.tensor, offset=first,
                                         ap=[[1, GRID_W], [width, NDR], [1, GRID_W]])).then_inc(bias_loaded, 16)
            sp.wait_ge(m_loaded, 32)

            sp.wait_ge(bias_loaded, 16 * NAH)

        @block.gpsimd
        def _(pool):
            pool.memset(mask[:], 0.0).then_inc(zeroed, 1)
            pool.wait_ge(zeroed, 1)
            pool.affine_select(out=mask[:, 0], in_=mask[:, 0], compare_op=ALU.is_ge, fill=-NEG, base=0,
                               pattern=[[1, P]], channel_multiplier=-1).then_inc(masked, 1)
            pool.affine_select(out=mask[:, 1], in_=mask[:, 1], compare_op=ALU.is_ge, fill=-NEG, base=0,
                               pattern=[[-1, P]], channel_multiplier=1).then_inc(masked, 1)
            pool.memset(hs[:], 0.0).then_inc(zeroed, 1)
            pool.memset(window[:], 0.0).then_inc(zeroed, 1)
            pool.wait_ge(zeroed, 3)
            pool.wait_ge(masked, 2)
            for h in range(2):
                part = window[h * GRID_W:(h + 1) * GRID_W]
                low, high = part[:, 0:GRID_W - WIN_W], part[:, WIN_W:GRID_W]
                pool.affine_select(out=low, in_=low, compare_op=ALU.is_ge, fill=NEG, base=WIN_W // 2 - (GRID_W - 1),
                                   pattern=[[1, GRID_W - WIN_W]], channel_multiplier=1).then_inc(masked, 1)
                pool.wait_ge(masked, 2 * h + 3)
                pool.affine_select(out=high, in_=high, compare_op=ALU.is_ge, fill=NEG,
                                   base=WIN_W // 2 - 1 - WIN_W + GRID_W - 1,
                                   pattern=[[-1, GRID_W - WIN_W]], channel_multiplier=-1).then_inc(masked, 1)
            pool.wait_ge(masked, 6)

            pool.wait_ge(m_loaded, 32)

            def mask_m(i, d, first):
                if not first:
                    pool.wait_ge(weight_ready, i * 2 + (d - 1))
                pool.tensor_tensor(arg[:, d], m_all[d][:, :, chunk(i, d)],
                                   mask[:, d].unsqueeze(1).to_broadcast([P, MLH, P]), ALU.add).then_inc(arg_ready, 1)

            for d in range(DIRS):
                mask_m(0, d, True)
            pool.wait_ge(qk_done, 4 * MLH + NC)
            pool.memset(state[:], 0.0).then_inc(zeroed, 1)
            pool.wait_ge(zeroed, 4)
            pool.wait_ge(q_read, 2 * MLH + NC)

            def step(i, first, last_step):
                for d in range(DIRS):
                    n, c = i * 2 + d, chunk(i, d)
                    if not last_step:
                        if not first:
                            pool.wait_ge(update_done, n - 1)
                        pool.tensor_tensor(k_weighted[:, d], k_tok[:, c],
                                           units_of(w_cols, c, d).unsqueeze(2).to_broadcast([P, MLH, P]), ALU.mult)\
                            .then_inc(k_scaled, 1)
                    if not first:
                        pool.wait_ge(carry_ready, n - 1)
                        pool.wait_ge(sums_done, n - 1)
                        pool.tensor_tensor(q_scaled[:, d], q_t[:, :, bass.ds(c * P, P)], carry[:, d], ALU.mult)\
                            .then_inc(q_carried, 1)
                    if not last_step:
                        mask_m(i + 1, d, False)
            steps(pool, step)
            for part in (pr.q_hi, pr.q_lo):
                pool.memset(part[:].bitcast(F32), 0.0).then_inc(diag_zeroed, 1)
            pool.wait_ge(diag_zeroed, 2)
            for r in range(EARLY):
                pr.copy_queries(pool, 0, r, diag_high, 2 * r, diag_early)
            pool.wait_ge(diag_early, 2 * EARLY)

        @block.scalar
        def _(a):
            load_table(a, mem, ident, ACT.Exp, "exp")
            for n in range(2 * MLH):
                a.wait_ge(qk_done, 2 * n + 1)
                a.activation(q_t[:, n // 2, n % 2 * BANK:(n % 2 + 1) * BANK], banks[2 * (n % 2)][:], ACT.Copy)\
                 .then_inc(q_read, 1)
            for c in range(NC):
                a.wait_ge(qk_done, 4 * MLH + c + 1)
                a.activation(k_tok[:, c].rearrange("p h e -> p (h e)"), banks[2 * (c % 2)][:], ACT.Copy, scale=SCALE)\
                 .then_inc(q_read, 1)

            a.wait_ge(k_read, 2 * MLH)
            a.wait_ge(m_loaded, 32)
            a.wait_ge(qk_done, 4 * MLH + NC)
            def step(i, first, last_step):
                for d in range(DIRS):
                    n, c = i * 2 + d, chunk(i, d)
                    if not first:
                        a.wait_ge(scores_done, n - 1)
                    a.activation(k_chunk[:, d], k_t[:, :, bass.ds(c * P, P)], ACT.Copy).then_inc(k_copied, 1)
                    a.wait_ge(arg_ready, n + 1)
                    if not first:
                        a.wait_ge(weighted_ready, n - 1)
                    for h in range(MLH):
                        unit = d * UD + h * NC + c
                        last = a.activation(weight[:, d, h], arg[:, d, h], ACT.Exp, scale=-1.0,
                                            bias=z_cols[:, bass.ds(unit, 1)])
                    last.then_inc(weight_ready, 1)
                    if not first:
                        a.wait_ge(sums_done, n - 1)
                        for h in range(MLH):
                            unit = d * UD + h * NC + c
                            last = a.activation(carry[:, d, h], m_all[d][:, h, c], ACT.Exp, scale=-1.0,
                                                bias=m0_cols[:, bass.ds(unit, 1)])
                        last.then_inc(carry_ready, 1)
            steps(a, step)
            a.wait_ge(k_copied, DIRS * NC)
            pr.high_keys(a, 0, keys_high)

        @block.vector
        def _(dve):
            for n in range(2 * MLH):
                dve.wait_ge(qk_done, 2 * n + 2)
                dve.tensor_scalar(k_t[:, n // 2, n % 2 * BANK:(n % 2 + 1) * BANK], banks[2 * (n % 2) + 1][:], SCALE,
                                  None, ALU.mult).then_inc(k_read, 1)

            dve.wait_ge(zeroed, 4)
            def weigh(i, d, first):
                n = i * 2 + d
                dve.wait_ge(weight_ready, n + 1)
                if not first:
                    dve.wait_ge(sums_done, n - 1)
                dve.wait_ge(scores_done, n + 1)
                dve.tensor_tensor(weighted[:, d], weight[:, d], banks[d][:].rearrange("p (h l) -> p h l", h=MLH),
                                  ALU.mult).then_inc(weighted_ready, 1)

            def absorb(i, d, last_step):
                n, c = i * 2 + d, chunk(i, d)
                dve.wait_ge(sums_done, n + 1)
                if not last_step:
                    dve.wait_ge(update_done, n + 1)
                    for h in range(MLH):
                        unit = d * UD + h * NC + c
                        last = dve.scalar_tensor_tensor(out=state[:, d, h], in0=state[:, d, h],
                                                        scalar=decay_cols[:, bass.ds(unit, 1)], in1=update_bank(h),
                                                        op0=ALU.mult, op1=ALU.add)
                    last.then_inc(updated, 1)
                floors = units_of(floor_cols, c, d)
                dens = [banks[2 + 2 * d + half][:, 0:2 * (MLD + 1)].rearrange("p (h e) -> p h e", h=2)[:, :, MLD]
                        for half in range(2)]
                for half in range(2):
                    pair = slice(2 * half, 2 * half + 2)
                    last = dve.scalar_tensor_tensor(out=den[:, d, pair], in0=dens[half], scalar=-1.0,
                                                    in1=floors[:, pair], op0=ALU.mult, op1=ALU.max)
                last.then_inc(den_step, 1)
                dve.wait_ge(den_step, n * 3 + 1)
                for half in range(2):
                    pair = slice(2 * half, 2 * half + 2)
                    last = dve.tensor_tensor(den_max[:, d, pair], dens[half], den[:, d, pair], ALU.max)
                last.then_inc(den_step, 1)
                dve.wait_ge(den_step, n * 3 + 2)
                dve.reciprocal(den_inv[:, d], den_max[:, d]).then_inc(den_step, 1)
                dve.wait_ge(den_step, n * 3 + 3)
                for h in range(MLH):
                    last = dve.scalar_tensor_tensor(out=hs[:, c, h], in0=head_bank(d, h)[:, 0:MLD],
                                                    scalar=den_inv[:, d, h:h + 1], in1=hs[:, c, h],
                                                    op0=ALU.mult, op1=ALU.add)
                last.then_inc(h_added, 1)

            weigh(0, 0, True)

            def step(i, first, last_step):
                for d in range(DIRS):
                    if not (last_step and d):
                        weigh(*following(i, d), first and d == 0)
                    if last_step and d == 0:
                        dve.wait_ge(keys_high, 1)
                        pr.low_keys(dve, 0, keys_low)
                    absorb(i, d, last_step)
            steps(dve, step)

        @block.tensor
        def _(pe):
            pe.wait_ge(pr.w_qk_loaded, 32)
            for n in range(2 * MLH):
                h, half = divmod(n, 2)
                if n >= 2:
                    pe.wait_ge(q_read, n - 1)
                    pe.wait_ge(k_read, n - 1)
                for w in range(2):
                    pe.matmul(banks[2 * half + w][:], pr.w_qk[:, w, h], u_t[:, h, half * BANK:(half + 1) * BANK],
                              start=True, stop=True).then_inc(qk_done, 1)
            for c in range(NC):
                pe.wait_ge(q_read, 2 * MLH + c - 1)
                for h in range(MLH):
                    last = pe.matmul(banks[2 * (c % 2)][:, h * P:(h + 1) * P], u_t[:, h, c * P:(c + 1) * P],
                                     pr.w_qk[:, 1, h], start=True, stop=True)
                last.then_inc(qk_done, 1)

            pe.wait_ge(q_read, 2 * MLH + NC)
            def scores(i, d, first):
                n, c = i * 2 + d, chunk(i, d)
                pe.wait_ge(k_copied, n + 1)
                if not first:
                    pe.wait_ge(weighted_ready, n - 1)
                for h in range(MLH):
                    last = pe.matmul(banks[d][:, h * P:(h + 1) * P], k_chunk[:, d, h], q_t[:, h, bass.ds(c * P, P)],
                                     start=True, stop=True)
                last.then_inc(scores_done, 1)

            def sums(i, d, first, last_step):
                n, c = i * 2 + d, chunk(i, d)
                pe.wait_ge(weighted_ready, n + 1)
                if not first:
                    pe.wait_ge(q_carried, n - 1)
                    pe.wait_ge(updated, n - 1)
                    pe.wait_ge(h_added, n - 1)
                for h in range(MLH):
                    last = pe.matmul(head_bank(d, h), weighted[:, d, h], pr.v[:, c, h], start=True, stop=first)
                    if not first:
                        last = pe.matmul(head_bank(d, h), q_scaled[:, d, h], state[:, d, h], start=False, stop=True)
                last.then_inc(sums_done, 1)
                if last_step:
                    return
                pe.wait_ge(k_scaled, n + 1)
                if not (first and d == 0):
                    pe.wait_ge(updated, n)
                for h in range(MLH):
                    last = pe.matmul(update_bank(h), k_weighted[:, d, h], pr.v[:, c, h], start=True, stop=True)
                last.then_inc(update_done, 1)

            scores(0, 0, True)

            def step(i, first, last_step):
                for d in range(DIRS):
                    if not (last_step and d):
                        scores(*following(i, d), first and d == 0)
                    sums(i, d, first, last_step)
            steps(pe, step)
    return hs, bias, window


class HeadNorm:

    def __init__(self, nc, mem, hs, o_dram, gn):
        self.hs, self.o_dram, self.gn = hs, o_dram, gn
        self.o = mem.at("ml_o", AT_H, [P, NC, MLH, MLD])
        self.squares = mem.at("ml_squares", AT_X + 8, [P, 2, MLH, MLD])
        self.gn_all = mem.at("ml_gn_all", AT_W + 22, [P, MLH, MLD])
        self.sumsq, self.meansq, self.root, self.rstd = (
            mem.at(f"ml_{n}", AT_SMALL + 4.25 + 0.125 * i, [P, NC, MLH]) for i, n in enumerate(
                "sumsq meansq root rstd".split()))
        sem = lambda s: mem.semaphore(f"ml_{s}")
        self.o_loaded, self.gn_loaded = sem("o_loaded"), sem("gn_loaded")
        self.squared, self.summed, self.mean_ready, self.root_ready, self.rstd_ready, self.gained, self.y_ready = (
            sem(s) for s in "squared summed mean_ready root_ready rstd_ready gained y_ready".split())

    def load(self, sp):
        sp.dma_start(self.gn_all[:].rearrange("p h e -> p (h e)"), self.gn.rearrange("o h e -> (o h e)").partition_broadcast(P))\
          .then_inc(self.gn_loaded, 16)
        sp.dma_start(self.o[:].rearrange("p c h e -> p c (h e)"), self.o_dram.rearrange("(c p) w -> p c w", p=P))\
          .then_inc(self.o_loaded, 16)

    def scalar_statistics(self, a, r):
        if r < NC:
            if r >= 2:
                a.wait_ge(self.summed, r - 1)
            a.activation(self.squares[:, r % 2], self.hs[:, r], ACT.Square).then_inc(self.squared, 1)
        elif r == NC + 2:
            a.wait_ge(self.mean_ready, 1)
            a.activation(self.root[:], self.meansq[:], ACT.Sqrt).then_inc(self.root_ready, 1)

    def vector_statistics(self, dve, r):
        if r < NC:
            dve.wait_ge(self.squared, r + 1)
            dve.tensor_reduce(self.sumsq[:, r], self.squares[:, r % 2], AX.X, ALU.add).then_inc(self.summed, 1)
        elif r == NC:
            dve.wait_ge(self.summed, NC)
            dve.tensor_scalar(self.meansq[:], self.sumsq[:], 1.0 / MLD, EPS, ALU.mult, ALU.add).then_inc(self.mean_ready, 1)
        elif r == NC + 4:
            dve.wait_ge(self.root_ready, 1)
            dve.reciprocal(self.rstd[:], self.root[:]).then_inc(self.rstd_ready, 1)
        elif r == NC + 5:
            dve.wait_ge(self.rstd_ready, 1)

    def gain(self, pool, h):
        o = self.o[:, :, h]
        pool.tensor_tensor(o, o, self.gn_all[:, h].unsqueeze(1).to_broadcast([P, NC, MLD]), ALU.mult).then_inc(self.gained, 1)

    def product(self, dve, h, c):
        y = self.hs[:, c, h]
        dve.scalar_tensor_tensor(out=y, in0=y, scalar=self.rstd[:, c, bass.ds(h, 1)], in1=self.o[:, c, h],
                                 op0=ALU.mult, op1=ALU.mult).then_inc(self.y_ready, 1)


class MixOut:

    def __init__(self, nc, mem, w_out):
        self.raw = [mem.at(f"out_raw{s}", AT_REST + at, [P, KD, BANK]) for s, at in enumerate((32, 0))]
        self.w_v = w_out.rearrange("o (k p) (s c) -> p (o k) s c", p=P, s=HALVES)
        self.raw_loaded = [mem.semaphore(f"out_raw_loaded{s}") for s in range(HALVES)]

    def load(self, sp, s):
        for kd in range(KD):
            sp.dma_start(self.raw[s][:, kd], self.w_v[:, kd, s]).then_inc(self.raw_loaded[s], 16)

    def prefetch(self, sp):
        self.load(sp, 0)


def mix_out(nc, mem, mix, x, x_scratch, y_ml, y_na, ident, banks, ffn):
    sem = lambda s: mem.semaphore(f"out_{s}")
    follower, raw, raw_loaded = ffn.norm, mix.raw, mix.raw_loaded
    y_hi = mem.at("out_y_hi", AT_H, [P, MLH, T], F32R)
    y_lo = mem.at("out_y_lo", AT_H + 32, [P, MLH, T], F32R)
    y_rows = lambda kd, rows: [y[:, kd % MLH, rows] for y in ((y_hi, y_lo) if kd < MLH else y_na)]
    w_hi = mem.at("out_w_hi", AT_W, [P, KD, BANK], F32R)
    w_lo = mem.at("out_w_lo", AT_W + 16, [P, KD, BANK], F32R)

    x_loaded = [sem(f"x_loaded{t}") for t in range(TT)]
    hi_ready, w_split = sem("hi_ready"), sem("w_split")
    piece_used = sem("piece_used")
    transposed = sem("transposed")
    y_hi_ready, y_split = sem("y_hi_ready"), sem("y_split")
    tile_done, added = sem("tile_done"), sem("added")
    ORDER = [*range(MLH, KD), *range(MLH)]

    with nc.Block() as block:
        @block.sync
        def _(sp):
            mix.load(sp, 1)
            for t in range(TT):
                sp.dma_start(x[:, t, :], x_scratch[t * P:(t + 1) * P, :]).then_inc(x_loaded[t], 16)
            sp.wait_ge(transposed, HALVES * MLH)
            sp.wait_ge(w_split, KD)
            follower.load(sp)
            ffn.prefetch(sp)

        bank_of = lambda n: banks[4 + n % 4][:]
        y_cols = lambda n: slice(n // MLH * BANK, (n // MLH + 1) * BANK)

        @block.scalar
        def _(a):
            def split(s, steps):
                for k in steps:
                    if s and k < KD - 1:
                        a.wait_ge(piece_used, k + 1)
                    elif s:
                        a.wait_ge(tile_done, TT)
                    a.wait_ge(raw_loaded[s], 16 * KD)
                    kd = k if s else ORDER[k]
                    a.activation(w_hi[:, kd], raw[s][:, kd], ACT.Copy).then_inc(hi_ready, 1)

            def y_parts(half):
                for n in range(half * MLH, (half + 1) * MLH):
                    a.wait_ge(transposed, n + 1)
                    a.activation(y_hi[:, n % MLH, y_cols(n)], bank_of(n), ACT.Copy).then_inc(y_hi_ready, 1)

            split(0, range(4))
            y_parts(0)
            split(0, range(4, KD))
            y_parts(1)
            split(1, range(KD))
            a.wait_ge(w_split, KD * HALVES)
            follower.scalar_tail(a, lambda eng, t: eng.wait_ge(added, TT + t + 1))
            a.wait_ge(piece_used, KD - 1 + 4)
            ffn.scalar_head(a)

        @block.vector
        def _(dve):
            def split(s, steps):
                for k in steps:
                    dve.wait_ge(hi_ready, KD * s + k + 1)
                    kd = k if s else ORDER[k]
                    dve.tensor_tensor(w_lo[:, kd], raw[s][:, kd], w_hi[:, kd].bitcast(F32), ALU.subtract)\
                       .then_inc(w_split, 1)

            def y_parts(half):
                for n in range(half * MLH, (half + 1) * MLH):
                    dve.wait_ge(y_hi_ready, n + 1)
                    dve.tensor_tensor(y_lo[:, n % MLH, y_cols(n)], bank_of(n), y_hi[:, n % MLH, y_cols(n)].bitcast(F32),
                                      ALU.subtract).then_inc(y_split, 1)

            split(0, range(4))
            y_parts(0)
            split(0, range(4, KD))
            y_parts(1)
            for s in range(HALVES):
                for t in range(TT):
                    if s == 0 and t == TT - 1:
                        split(1, range(KD))
                    part = x[:, t, s * BANK:(s + 1) * BANK]
                    if s == 0:
                        dve.wait_ge(x_loaded[t], 16)
                    if s and t == TT - 1:
                        follower.vector_before_last(dve)
                    dve.wait_ge(tile_done, TT * s + t + 1)
                    dve.tensor_tensor(part, banks[t][:], part, ALU.add).then_inc(added, 1)
                    if s and t >= 4:
                        follower.vector_after_tile(dve, t)
            ffn.vector_head(dve)

        @block.tensor
        def _(pe):
            def transposes(half):
                for h in range(MLH):
                    n = half * MLH + h
                    if n >= 4:
                        pe.wait_ge(y_split, n - 3)
                    for j in range(4):
                        last = pe.transpose(bank_of(n)[:, j * P:(j + 1) * P], y_ml[:, 4 * half + j, h], ident[:])
                    last.then_inc(transposed, 1)

            transposes(0)
            for s in range(HALVES):
                halves = [(0, range(4)), (1, range(4)), (0, range(4, KD)), (1, range(4, KD))]
                for t, steps in [*(halves if s == 0 else [(0, range(KD)), (1, range(KD))]),
                                 *((t, range(KD)) for t in range(2, TT))]:
                    if s:
                        pe.wait_ge(added, t + 1)
                    elif t == 2:
                        transposes(1)
                    elif t == 4:
                        pe.wait_ge(y_split, HALVES * MLH)
                    for k in steps:
                        if s and t == TT - 1 and k in (0, 4):
                            if k == 0:
                                pe.wait_ge(added, TT + 4)
                            follower.tensor_tail(pe, k // 4)
                        kd = ORDER[k] if s == 0 and t < 2 else k
                        if t == 0:
                            pe.wait_ge(w_split, KD * s + k + 1)
                            if s == 0 and kd < MLH:
                                pe.wait_ge(y_split, kd + 1)
                        rows = slice(t * P, (t + 1) * P)
                        last = split_product(pe, banks[t][:], *y_rows(kd, rows),
                                             w_hi[:, kd], w_lo[:, kd], k == 0, k == KD - 1)
                        if t == TT - 1 and k < KD - 1:
                            last.then_inc(piece_used, 1)
                    if k == KD - 1:
                        last.then_inc(tile_done, 1)


class FinalNorm:

    GROUPS = ((0, 4), (4, 7), (7, 8))

    def __init__(self, nc, mem, x, gain, out):
        self.x, self.gain, self.out = x, gain, out
        self.norm = self
        self.g = mem.at("final_g", AT_H, [P, D])
        self.result = mem.at("final_result", AT_H + 8, [P, TT, D])
        self.sumsq, self.meansq, self.root, self.rstd = (
            mem.at(f"final_{n}", AT_SMALL + 0.5 + 0.0625 * i, [P, TT]) for i, n in enumerate("sumsq meansq root rstd".split()))
        self.scaled = mem.at("final_scaled", AT_H + 40, [P, 4, D])
        (self.scaled_ready, self.early_ready) = (mem.semaphore(f"final_{s}") for s in ("scaled_ready", "early_ready"))
        (self.gain_loaded, self.squared, self.mean_ready, self.root_ready, self.rstd_ready, self.result_ready,
         self.stored) = (mem.semaphore(f"final_{s}") for s in
                         "gain_loaded squared mean_ready root_ready rstd_ready result_ready stored".split())

    def load(self, sp):
        sp.dma_start(self.g[:], self.gain.rearrange("o d -> (o d)").partition_broadcast(P)).then_inc(self.gain_loaded, 16)

    def sync_tail(self, sp):
        for t in range(TT):
            if t < 4:
                sp.wait_ge(self.early_ready, t + 1)
            else:
                sp.wait_ge(self.result_ready, t - 3)
            sp.dma_start(self.out[t * P:(t + 1) * P, :], self.result[:, t]).then_inc(self.stored, 16)
        sp.wait_ge(self.stored, 16 * TT)

    def scalar_tail(self, act, x_here, between):
        for n, (first, end) in enumerate(self.GROUPS):
            for t in range(first, end):
                x_here(act, t)
                act.activation(self.result[:, t], self.x[:, t], ACT.Square, accum_out=self.sumsq[:, t:t + 1])\
                   .then_inc(self.squared, 1)
            act.wait_ge(self.mean_ready, n + 1)
            act.activation(self.root[:, first:end], self.meansq[:, first:end], ACT.Sqrt).then_inc(self.root_ready, 1)
            if n == 0:
                act.wait_ge(self.rstd_ready, 1)
                for t in range(4):
                    act.activation(self.scaled[:, t], self.x[:, t], ACT.Copy, scale=self.rstd[:, t:t + 1])\
                       .then_inc(self.scaled_ready, 1)

    def pool_tail(self, pool):
        pool.wait_ge(self.gain_loaded, 16)
        for t in range(4):
            pool.wait_ge(self.scaled_ready, t + 1)
            pool.tensor_tensor(self.result[:, t], self.scaled[:, t], self.g[:], ALU.mult).then_inc(self.early_ready, 1)

    def statistics(self, dve, n):
        first, end = self.GROUPS[n]
        dve.wait_ge(self.squared, end)
        dve.tensor_scalar(self.meansq[:, first:end], self.sumsq[:, first:end], 1.0 / D, EPS, ALU.mult, ALU.add)\
           .then_inc(self.mean_ready, 1)
        dve.wait_ge(self.root_ready, n + 1)
        dve.reciprocal(self.rstd[:, first:end], self.root[:, first:end]).then_inc(self.rstd_ready, 1)
        dve.wait_ge(self.rstd_ready, n + 1)

    def results(self, dve, *tiles):
        for t in tiles:
            dve.scalar_tensor_tensor(out=self.result[:, t], in0=self.x[:, t], scalar=self.rstd[:, t:t + 1],
                                     in1=self.g[:], op0=ALU.mult, op1=ALU.mult).then_inc(self.result_ready, 1)

    def vector_after_tile(self, dve, t):
        if t == 4:
            self.statistics(dve, 0)
            dve.wait_ge(self.gain_loaded, 16)

    def vector_tail(self, dve):
        self.statistics(dve, 1)
        self.results(dve, 4, 5)
        self.statistics(dve, 2)
        self.results(dve, 6, 7)

    def vector_before_last(self, dve):
        pass

    def tensor_tail(self, pe, part):
        pass

    def prefetch(self, sp):
        pass

    def scalar_head(self, act):
        pass

    def vector_head(self, dve):
        pass


def hybrid_mlstm_natten_macaron_encoder_kernel(
        nc, x, norm_ffn1, w1_gate, w1_up, w1_down, norm_mix, w_in, b_gates, conv_w, conv_b, w_q_ml, w_k_ml, gn_ml,
        gq_na, gk_na, rpb, w_out, norm_ffn2, w2_gate, w2_up, w2_down, norm_final, out):
    mem = Memory(nc)
    banks = [nc.alloc_psum_tensor(f"bank{k}", [P, BANK], F32) for k in range(8)]
    x_scratch = nc.dram_tensor("x_scratch", [T, D], F32, kind="Internal").ap()
    resident = mem.at("x_resident", AT_X, [P, TT, D])
    ident = make_identity(nc, mem)
    ffn1 = FeedForward(nc, mem, "ffn1", resident, norm_ffn1, w1_gate, w1_up, w1_down, ident, banks)
    x_loaded = start(nc, resident, x.rearrange("o t d -> (o t) d"), ffn1, ident, banks)
    projection = Projection(nc, mem, resident, norm_mix, w_in, ident, banks)
    x_stored = ffn1.run(lambda eng, t: eng.wait_ge(x_loaded[t], 16), x_scratch, projection)
    projected = project(nc, mem, projection, x_stored, b_gates, conv_w, conv_b, w_q_ml, w_k_ml, gq_na, gk_na, rpb,
                        ident, banks)
    y_ml, *na_bias = mlstm(nc, mem, projected, ident, banks)
    mem.clear_semaphores()
    mix = MixOut(nc, mem, w_out)
    y_na = attend(nc, mem, projected, *na_bias, HeadNorm(nc, mem, y_ml, projected.o_dram, gn_ml), ident,
                  banks, mix.prefetch)
    ffn2 = FeedForward(nc, mem, "ffn2", resident, norm_ffn2, w2_gate, w2_up, w2_down, ident, banks)
    mix_out(nc, mem, mix, resident, x_scratch, y_ml, y_na, ident, banks, ffn2)
    ffn2.run(lambda eng, t: None, None, FinalNorm(nc, mem, resident, norm_final, out.rearrange("o t d -> (o t) d")))


_INS = ["x", "norm_ffn1", "w1_gate", "w1_up", "w1_down", "norm_mix", "w_in", "b_gates", "conv_w", "conv_b", "w_q_ml",
        "w_k_ml", "gn_ml", "gq_na", "gk_na", "rpb", "w_out", "norm_ffn2", "w2_gate", "w2_up", "w2_down", "norm_final"]
_OUTS = [((1, T, D), "float32")]


def kernel(**inputs):
    import numpy as _np
    import concourse.bacc as _bacc
    from concourse import mybir as _mybir
    from concourse.bass_utils import run_bass_kernel_spmd as _run

    nc = _bacc.Bacc("TRN2", target_bir_lowering=False, num_devices=1)
    arrays, args = {}, []
    for name in _INS:
        a = _np.ascontiguousarray(inputs[name])
        arrays[f"in_{name}_dram"] = a
        args.append(nc.dram_tensor(f"in_{name}_dram", a.shape, _mybir.dt.from_np(a.dtype), kind="ExternalInput").ap())
    for i, (shape, dtype) in enumerate(_OUTS):
        dt = _mybir.dt.from_np(_np.dtype(dtype))
        args.append(nc.dram_tensor(f"out_{i}_dram", shape, dt, kind="ExternalOutput").ap())
    hybrid_mlstm_natten_macaron_encoder_kernel(nc, *args)
    r = _run(nc, [arrays], core_ids=[0])
    return r.results[0]["out_0_dram"]
```
